# Optimizing a Trainium2 kernel written in Bass

```python
import jax, jax.numpy as jnp
from jax import lax
import numpy as np

D_MODEL = 1024
BATCH = 1
SEQ = 2048
DEPTH = 1

CHUNK = 64
RMS_EPS = 1e-6
GLA_HEADS = 4
GLA_DK = 64
GLA_DV = 128
GLA_LOWRANK = 16
GLA_GATE_NORM = 16.0
SWA_Q_HEADS = 8
SWA_KV_HEADS = 2
SWA_HEAD_DIM = 64
WINDOW = 128
WIN_CHUNKS = WINDOW // CHUNK
ROPE_THETA = 500000.0
ROPE_DIM = SWA_HEAD_DIM // 4
D_FF = 2816
CONV_WIDTH = 3

GLA_QK = GLA_HEADS * GLA_DK
GLA_V = GLA_HEADS * GLA_DV
SWA_Q = SWA_Q_HEADS * SWA_HEAD_DIM
SWA_KV = SWA_KV_HEADS * SWA_HEAD_DIM
D_MIX = GLA_V + SWA_Q
IN_SPLITS = (GLA_QK, GLA_QK, GLA_V, GLA_V, GLA_LOWRANK, SWA_Q, SWA_KV, SWA_KV)
D_IN = GLA_QK + GLA_QK + GLA_V + GLA_V + GLA_LOWRANK + SWA_Q + SWA_KV + SWA_KV

kernel_name = 'hybrid_gla_swa_sink_convffn'

def rms_norm(x, w):
    xf = x.astype(jnp.float32)
    var = jnp.mean(xf * xf, axis=-1, keepdims=True)
    return (xf * lax.rsqrt(var + RMS_EPS)).astype(x.dtype) * w

def gla_mixer(q, k, v, r, gk_low, gk_w2, gk_b, norm_w):
    B, S, _ = q.shape
    nC = S // CHUNK
    f32 = jnp.float32
    gk = jax.nn.log_sigmoid((gk_low @ gk_w2 + gk_b).astype(f32)) / GLA_GATE_NORM

    def to_chunks(t, dh):
        return t.astype(f32).reshape(B, nC, CHUNK, GLA_HEADS, dh).transpose(1, 0, 3, 2, 4)

    qc = to_chunks(q, GLA_DK) * (GLA_DK ** -0.5)
    kc = to_chunks(k, GLA_DK)
    vc = to_chunks(v, GLA_DV)
    gc = to_chunks(gk, GLA_DK)
    causal = jnp.tril(jnp.ones((CHUNK, CHUNK), dtype=bool))

    def step(state, inp):
        qi, ki, vi, gi = inp
        b = jnp.cumsum(gi, axis=2)
        o_inter = jnp.einsum('bhcd,bhde->bhce', qi * jnp.exp(b), state)
        diff = b[:, :, :, None, :] - b[:, :, None, :, :]
        decay = jnp.exp(jnp.where(causal[:, :, None], diff, -jnp.inf))
        scores = jnp.einsum('bhid,bhjd,bhijd->bhij', qi, ki, decay)
        o_intra = jnp.einsum('bhij,bhje->bhie', scores, vi)
        b_last = b[:, :, -1:, :]
        k_dec = ki * jnp.exp(b_last - b)
        new_state = jnp.exp(b_last[:, :, 0, :])[..., None] * state + jnp.einsum('bhcd,bhce->bhde', k_dec, vi)
        return new_state, o_inter + o_intra

    state0 = jnp.zeros((B, GLA_HEADS, GLA_DK, GLA_DV), f32)
    _, o = lax.scan(step, state0, (qc, kc, vc, gc))
    o = o.transpose(1, 0, 3, 2, 4).reshape(B, S, GLA_HEADS, GLA_DV)
    o = rms_norm(o, norm_w.astype(f32)).reshape(B, S, GLA_V)
    return (o * jax.nn.silu(r.astype(f32))).astype(v.dtype)

def rope_partial(x, positions):
    half = ROPE_DIM // 2
    inv_freq = ROPE_THETA ** (-jnp.arange(half, dtype=jnp.float32) / half)
    ang = positions.astype(jnp.float32)[..., None] * inv_freq
    cos = jnp.cos(ang)[:, :, None, :]
    sin = jnp.sin(ang)[:, :, None, :]
    x1 = x[..., :half].astype(jnp.float32)
    x2 = x[..., half:ROPE_DIM].astype(jnp.float32)
    rot = jnp.concatenate([x1 * cos - x2 * sin, x2 * cos + x1 * sin], axis=-1)
    return jnp.concatenate([rot.astype(x.dtype), x[..., ROPE_DIM:]], axis=-1)

def swa_sink_mixer(q, k, v, positions, sinks):
    B, S, _ = q.shape
    nC = S // CHUNK
    G = SWA_Q_HEADS // SWA_KV_HEADS
    HD = SWA_HEAD_DIM
    q = rope_partial(q.reshape(B, S, SWA_Q_HEADS, HD), positions)
    k = rope_partial(k.reshape(B, S, SWA_KV_HEADS, HD), positions)
    v = v.reshape(B, S, SWA_KV_HEADS, HD)
    qb = q.reshape(B, nC, CHUNK, SWA_KV_HEADS, G, HD)
    pad = (WIN_CHUNKS - 1) * CHUNK

    def band(t):
        tp = jnp.pad(t, ((0, 0), (pad, 0), (0, 0), (0, 0)))
        tp = tp.reshape(B, nC + WIN_CHUNKS - 1, CHUNK, SWA_KV_HEADS, HD)
        return jnp.concatenate([tp[:, i:i + nC] for i in range(WIN_CHUNKS)], axis=2)

    kb, vb = band(k), band(v)
    chunk_src = jnp.arange(nC)[:, None] + jnp.arange(WIN_CHUNKS)[None, :] - (WIN_CHUNKS - 1)
    valid = jnp.repeat(chunk_src >= 0, CHUNK, axis=1)
    scores = jnp.einsum('bnqkgd,bnskd->bkgnqs', qb, kb).astype(jnp.float32) * (HD ** -0.5)
    scores = jnp.where(valid[:, None, :], scores, -jnp.inf)
    sink = sinks.astype(jnp.float32).reshape(SWA_KV_HEADS, G)[None, :, :, None, None, None]
    sink = jnp.broadcast_to(sink, scores.shape[:-1] + (1,))
    probs = jax.nn.softmax(jnp.concatenate([scores, sink], axis=-1), axis=-1)[..., :-1]
    out = jnp.einsum('bkgnqs,bnskd->bnqkgd', probs.astype(vb.dtype), vb)
    return out.reshape(B, S, SWA_Q)

def conv_ffn(x, w_up, conv_w, conv_b, w_down):
    S = x.shape[1]
    h = x @ w_up
    hp = jnp.pad(h, ((0, 0), (CONV_WIDTH - 1, 0), (0, 0)))
    hc = conv_b
    for i in range(CONV_WIDTH):
        hc = hc + hp[:, i:i + S] * conv_w[i]
    gate, up = jnp.split(hc, 2, axis=-1)
    return (jax.nn.silu(gate) * up) @ w_down

def setup_inputs(seed: int = 0) -> dict:
    key = jax.random.key(seed)
    ks = jax.random.split(key, 16)
    f32 = jnp.float32

    def nrm(k, shape, scale):
        return jax.random.normal(k, shape, f32) * scale

    x = nrm(ks[0], (BATCH, SEQ, D_MODEL), 1.0)
    offset = jax.random.randint(ks[1], (BATCH, 1), 0, 64, dtype=jnp.int32) * CHUNK
    positions = offset + jnp.arange(SEQ, dtype=jnp.int32)[None, :]
    norm1_w = 1.0 + nrm(ks[2], (DEPTH, D_MODEL), 0.02)
    w_in = nrm(ks[3], (DEPTH, D_MODEL, D_IN), D_MODEL ** -0.5)
    gla_gk_w2 = nrm(ks[4], (DEPTH, GLA_LOWRANK, GLA_QK), GLA_LOWRANK ** -0.5)
    gla_gk_b = nrm(ks[5], (DEPTH, GLA_QK), 0.1)
    gla_norm_w = 1.0 + nrm(ks[6], (DEPTH, GLA_DV), 0.02)
    swa_sinks = nrm(ks[7], (DEPTH, SWA_Q_HEADS), 0.5)
    w_out = nrm(ks[8], (DEPTH, D_MIX, D_MODEL), D_MIX ** -0.5)
    norm2_w = 1.0 + nrm(ks[9], (DEPTH, D_MODEL), 0.02)
    w_up = nrm(ks[10], (DEPTH, D_MODEL, 2 * D_FF), D_MODEL ** -0.5)
    conv_w = nrm(ks[11], (DEPTH, CONV_WIDTH, 2 * D_FF), CONV_WIDTH ** -0.5)
    conv_b = nrm(ks[12], (DEPTH, 2 * D_FF), 0.02)
    w_down = nrm(ks[13], (DEPTH, D_FF, D_MODEL), D_FF ** -0.5)
    final_norm_w = 1.0 + nrm(ks[14], (D_MODEL,), 0.02)
    return {'x': x, 'positions': positions, 'norm1_w': norm1_w, 'w_in': w_in,
            'gla_gk_w2': gla_gk_w2, 'gla_gk_b': gla_gk_b, 'gla_norm_w': gla_norm_w,
            'swa_sinks': swa_sinks, 'w_out': w_out, 'norm2_w': norm2_w, 'w_up': w_up,
            'conv_w': conv_w, 'conv_b': conv_b, 'w_down': w_down, 'final_norm_w': final_norm_w}

def reference(x, positions, norm1_w, w_in, gla_gk_w2, gla_gk_b, gla_norm_w, swa_sinks,
              w_out, norm2_w, w_up, conv_w, conv_b, w_down, final_norm_w):
    offsets = np.cumsum(IN_SPLITS)[:-1].tolist()
    for l in range(DEPTH):
        h = rms_norm(x, norm1_w[l])
        z = h @ w_in[l]
        g_q, g_k, g_v, g_r, g_low, s_q, s_k, s_v = jnp.split(z, offsets, axis=-1)
        o_gla = gla_mixer(g_q, g_k, g_v, g_r, g_low, gla_gk_w2[l], gla_gk_b[l], gla_norm_w[l])
        o_swa = swa_sink_mixer(s_q, s_k, s_v, positions, swa_sinks[l])
        x = x + jnp.concatenate([o_gla, o_swa], axis=-1) @ w_out[l]
        x = x + conv_ffn(rms_norm(x, norm2_w[l]), w_up[l], conv_w[l], conv_b[l], w_down[l])
    return rms_norm(x, final_norm_w)


_drawn_inputs = setup_inputs


def setup_inputs(seed=0):
    import zlib

    import numpy as np

    out = dict(_drawn_inputs(seed))
    spreads = {}
    factors = {'norm1_w': 3.018,
     'gla_gk_b': 2.745,
     'gla_norm_w': 6.176,
     'swa_sinks': 64.0,
     'norm2_w': 3.99,
     'conv_b': 4.123,
     'final_norm_w': 8.245}
    for name, (base, spread) in spreads.items():
        noise = np.random.default_rng([zlib.crc32(name.encode()), seed]).standard_normal(out[name].shape)
        drawn = base * np.exp(spread * noise) if base else spread * noise
        out[name] = __import__('jax').numpy.asarray(drawn.astype(out[name].dtype))
    for name, factor in factors.items():
        out[name] = (out[name] * factor).astype(out[name].dtype)
    return out
```

```python
from contextlib import ExitStack

import numpy as np

import concourse.bass as bass
from concourse import mybir

P = 128
D = 1024
KD = D // P
S = 2048
NT = S // P
GH, DK, DV, RANK = 4, 64, 128, 16
QK, GV = GH * DK, GH * DV
SH, KVH, HD = 8, 2, 64
GRP = SH // KVH
SQ, SKV = SH * HD, KVH * HD
DMIX = GV + SQ
D_IN = 2 * QK + 2 * GV + RANK + SQ + 2 * SKV
O_QK, O_V, O_R, O_LOW = 0, 2 * QK, 2 * QK + GV, 2 * QK + 2 * GV
O_SQ = O_LOW + RANK
O_SK = O_SQ + SQ
CHUNK = 64
ROPE = HD // 4
RH = ROPE // 2
THETA = 500000.0
EPS = 1e-6
GATE_NORM = 16.0
FF = 2816
NC_FF = FF // P
HALVES = 2
TPH = NT // HALVES
TOK = S // HALVES
SPANS = [64, 32, 16, 8, 4, 2, 1]
NL = len(SPANS)
FIRST_SPANS = 4
SPAN_PARTS = [(0, FIRST_SPANS), (FIRST_SPANS, NL)]
NEG = -1.0e30
TWO_PI = 6.283185307179586
TP_A = 6.28125
TP_B = float(np.float32(int((TWO_PI - TP_A) * 2 ** 21) / 2.0 ** 21))
TP_C = TWO_PI - TP_A - TP_B
ROUNDER = 12582912.0
PI_IN = 3.1415925

F32 = mybir.dt.float32
F32R = mybir.dt.float32r
I32 = mybir.dt.int32
U8 = mybir.dt.uint8
ALU = mybir.AluOpType
ACT = mybir.ActivationFunctionType
AX_X = mybir.AxisListType.X

GROUPS = ["qk", "sq", "small", "v", "r"]
PIECES = {"qk": [(O_QK, 2 * QK)], "sq": [(O_SQ, SQ)], "small": [(O_LOW, RANK), (O_SK, 2 * SKV)],
          "v": [(O_V, GV)], "r": [(O_R, GV)]}
WIDTH = {g: sum(w for _, w in PIECES[g]) for g in GROUPS}
FIRST = {g: sum(WIDTH[f] for f in GROUPS[:i]) for i, g in enumerate(GROUPS)}


PRIME = 2


def after(n):
    return n + (1 + PRIME)


def mixer_phase(nc, t_in, mix_scratch):
    all_sems = []
    with ExitStack() as ctx:
        def sb(name, shape, dt=F32):
            return ctx.enter_context(nc.sbuf_tensor(name, shape, dt))

        def ps(name, cols):
            return ctx.enter_context(nc.psum_tensor(name, [P, cols], F32))

        def sem(name):
            all_sems.append(nc.alloc_semaphore(name=name))
            return all_sems[-1]

        w_hi = sb("w_in_hi", [P, KD, D_IN], F32R)
        w_lo = sb("w_in_lo", [P, KD, D_IN], F32R)
        x = sb("x_tile", [P, D])
        h_hi = sb("h_hi", [P, KD, P], F32R)
        h_lo = sb("h_lo", [P, KD, P], F32R)
        z_qk = sb("z_qk", [P, 2 * QK])
        z_v = sb("z_v", [P, GV])
        z_r = sb("z_r", [P, GV])
        z_low = sb("z_low", [P, RANK])
        z_sqk = sb("z_sqk", [P, GRP + 1, KVH, HD])
        z_sv = sb("z_sv", [P, SKV])
        ident = sb("ident", [P, P])
        masks = sb("level_masks", [P, NL - 1, P], U8)
        swa_mask = sb("swa_mask", [P, P])
        norm1 = sb("norm1_col", [P, KD])
        w2 = sb("gk_w2", [RANK, QK])
        gkb = sb("gk_b_col", [P, 2])
        sinks = sb("sinks_row", [P, SH])
        nsinks = sb("minus_sinks", [P, SH])
        invf = sb("inv_freq", [P, RH])
        pos_i = sb("pos_i", [P, NT], I32)
        pos_f = sb("pos_f", [P, NT])
        cosT = sb("cosT", [P, NT, RH])
        sinT = sb("sinT", [P, NT, RH])
        nhalf = sb("minus_half", [P, GH])
        stats = sb("bn_stats", [P, 2, 6])
        mv = sb("mean_var", [P, 2])
        ms = sb("mean_square", [P, 1])
        rstd = sb("rstd", [P, 1])
        qkT = sb("qkT", [P, 4, P])
        kwin = sb("k_window", [P, CHUNK + P])
        v_cur = sb("v_cur", [P, SKV])
        v_mid = sb("v_mid", [P, SKV])
        lowT = sb("lowT", [RANK, P])
        gate_a = sb("gate_pre", [P, 2 * P])
        gate_l = sb("gate_log", [P, 2 * P])
        gate_m = sb("gate_min", [P, 2 * P])
        B = sb("gate_cumsum", [P, 2 * P])
        Eb = sb("exp_b", [P, 2 * P])
        kd, kdN, qb = gate_m, gate_a, gate_l
        ks = sb("k_level", [P, NL, 2 * P])
        qs = sb("q_level", [P, NL, 2 * P])
        sqT = qs[:, NL - 2:NL, :].rearrange("p l (b n) -> p (l b) n", b=2)
        pT = sb("intra_scores", [P, 2, 2, P])
        state = sb("state", [P, 2, DV])
        prob = sb("prob", [P, SH, P])
        negm = sb("minus_max", [P, SH])
        den = sb("denominator", [P, SH])
        esink = sb("exp_sink", [P, SH])
        rden = sb("recip_denominator", [P, SH])
        probT = sb("probT", [P, SH, P])
        gate = sb("out_gate", [P, GV])
        ossq = sb("o_ssq", [P, GH])
        orstd = sb("o_rstd", [P, GH])
        mix = prob[:].rearrange("p h k -> p (h k)")
        mixT = probT
        rope_heads = (GRP + 1) * KVH
        rope_room = probT[:].rearrange("p h n -> p (h n)")
        ropeA = rope_room[:, 0:rope_heads * ROPE].rearrange("p (h r) -> p h r", h=rope_heads)
        ropeB = rope_room[:, 512:512 + rope_heads * ROPE].rearrange("p (h r) -> p h r", h=rope_heads)

        squares = ks[:, 0:2, :].rearrange("p l (b n) -> p (l b) n", b=2)
        ang = rope_room[:, 0:NT * RH].rearrange("p (t r) -> p t r", t=NT)

        pj = [ps("proj0", 512), ps("proj1", 512)]
        tr = ps("turn", 1024)
        sc = ps("score", 1024)
        ob = ps("outb", 1024)
        gk_ps = sc[:, 1024 - 2 * P:1024]
        gla_out = [ob[:, 0:2 * DV], sc[:, 512:512 + 2 * DV]]

        owned = {
            "pe": """xT zT sT_k sT_low gk swa_s swa_pT swa_o kdT gla_o gla_up mixT_done""",
            "act": """x_norm hT_hi e_qk e_sq e_small_low e_small_k e_sv e_v e_r r_exp vmid_lo v_copy vmid_hi
                ev_kshift ev_k ev_low ev_qkT ev_pT ev_kd ev_mixT g_abs g_exp g_log g_eb g_kexp lv_exp0 lv_exp1
                swa_exp swa_sinke o_ssq""",
            "pool": """x_rstd o_rstd""",
            "dve": """x_stats x_ms x_sum x_eps hT_lo rope_mul rope_a rope_b ev_sqT g_pre g_min g_sum g_scan g_kdiff
                g_kd g_qb lv_diff0 lv_diff1 lv_k0 lv_k1 lv_qk0 lv_qk1 swa_masked swa_max swa_neg swa_sinkd swa_den swa_rden swa_mix
                st_scaled st_new o_eps o_scaled o_mix r_one r_rec r_gate""",
        }
        s = {n: sem("a_" + n) for names in owned.values() for n in names.split()}
        s_g = {g: sem("a_proj_" + g) for g in GROUPS}
        s_lv = [sem(f"a_lvl{i}") for i in range(NL + 1)]
        s_mg = [sem(f"a_merge{i}") for i in range(NL + 1)]
        stepped = {who: [s[n] for n in names.split()] for who, names in owned.items()}
        stepped["pe"] += [*s_g.values(), *s_lv]
        stepped["dve"] += s_mg
        for n in ("norm1_load", "w_split_hi", "w_split_lo", "dve_setup", "const_ready", "pool_setup", "rope_tab", "rope_act"):
            s[n] = sem("a_" + n)
        NSTAGE = 6
        s_w = [sem(f"a_w_load{i}") for i in range(NSTAGE)]
        s_const = sem("a_const_load")
        s_x = sem("a_x_load")
        s_out = sem("a_mix_store")

        block = ctx.enter_context(nc.Block())

        def prime(eng, who):
            for one in stepped[who]:
                eng.sem_inc(one, PRIME)
        stage_room = [ks[:].rearrange("p l n -> p (l n)"), qs[:].rearrange("p l n -> p (l n)")]
        stage = [stage_room[i // 3][:, (i % 3) * 512:(i % 3 + 1) * 512] for i in range(NSTAGE)]
        pieces = [(g, k) for g in GROUPS for k in range(KD)]

        def loads_of(g):
            return len(PIECES[g])

        def loaded(n):
            return 16 * sum(loads_of(pieces[m][0]) for m in range(n % NSTAGE, n + 1, NSTAGE))

        def last_of_group_evac(g):
            return {"qk": "e_qk", "sq": "e_sq", "small": "e_sv", "v": "e_v", "r": "r_exp"}[g]

        def plain(eng):
            eng.wait_ge(s["const_ready"], 1)

        @block.sync
        def _(sp):
            sp.sem_inc(s_out, 16 * PRIME)
            sp.sem_inc(s_x, 16 * PRIME)
            sp.dma_start(norm1[:], t_in["norm1_w"][0].rearrange("(k p) -> p k", p=P),
                         allow_slow_non_contiguous=True).then_inc(s["norm1_load"], 16)
            sp.dma_start(x[:], t_in["x"][0, 0:P, :]).then_inc(s_x, 16)
            for n, (g, k) in enumerate(pieces):
                if n >= NSTAGE:
                    sp.wait_ge(s["w_split_lo"], n - NSTAGE + 1)
                at = 0
                for c0, w in PIECES[g]:
                    sp.dma_start(stage[n % NSTAGE][:, at:at + w], t_in["w_in"][0, k * P:(k + 1) * P, c0:c0 + w]
                                 ).then_inc(s_w[n % NSTAGE], 16)
                    at += w

            def load_x(n):
                sp.wait_ge(s["xT"], after(n - 1))
                sp.dma_start(x[:], t_in["x"][0, bass.ds(n * P, P), :]).then_inc(s_x, 16)

            def store_mix(t):
                sp.wait_ge(s["ev_mixT"], after(t))
                sp.dma_start(mix_scratch[bass.ds(t, 1)].rearrange("o p k n -> (o p) k n"), mixT[:]).then_inc(s_out, 16)

            load_x(1)
            with sp.Fori(0, NT - 2) as t:
                load_x(t + 2)
                store_mix(t)
            store_mix(NT - 2)
            store_mix(NT - 1)
            sp.wait_ge(s_out, 16 * after(NT - 1))

        @block.tensor
        def _(pe):
            prime(pe, "pe")

            def turn_x(n):
                pe.wait_ge(s["x_norm"], after(n))
                pe.wait_ge(s["swa_mix"], after(n - 2))
                pe.wait_ge(s["o_scaled"], after(n - 2))
                pe.wait_ge(s["hT_lo"], after(n - 1))
                for k in range(KD):
                    last = pe.transpose(ob[:, k * P:(k + 1) * P], x[:, k * P:(k + 1) * P], ident[:])
                last.then_inc(s["xT"], 1)

            def project(n, g):
                i = GROUPS.index(g)
                if i == 0:
                    pe.wait_ge(s["hT_lo"], after(n))
                free = GROUPS[i - 2] if i >= 2 else GROUPS[4 - i]
                pe.wait_ge(s[last_of_group_evac(free)], after(n if i >= 2 else n - 1))
                out = pj[i % 2][:, 0:WIDTH[g]]
                cols = slice(FIRST[g], FIRST[g] + WIDTH[g])
                for k in range(KD):
                    pe.matmul(out, h_hi[:, k, :], w_hi[:, k, cols], start=(k == 0), stop=False)
                    pe.matmul(out, h_hi[:, k, :], w_lo[:, k, cols], start=False, stop=False)
                    last = pe.matmul(out, h_lo[:, k, :], w_hi[:, k, cols], start=False, stop=(k == KD - 1))
                last.then_inc(s_g[g], 1)

            def level(t, l):
                bank = ob if l % 2 == 0 else sc
                if l == 0:
                    pe.wait_ge(s["lv_qk0"], after(t))
                elif l == 1:
                    pe.wait_ge(s["swa_masked"], after(t))
                else:
                    pe.wait_ge(s_mg[l - 2], after(t))
                if l == FIRST_SPANS:
                    pe.wait_ge(s["lv_qk1"], after(t))
                for pair in range(2):
                    for par in range(2):
                        rows = slice(par * DK, (par + 1) * DK)
                        if l < NL:
                            lhs, rhs = ks[rows, l, pair * P:(pair + 1) * P], qs[rows, l, pair * P:(pair + 1) * P]
                        else:
                            lhs, rhs = qkT[rows, 2 + pair, :], qkT[rows, pair, :]
                        at = par * 512 + pair * P
                        last = pe.matmul(bank[:, at:at + P], lhs, rhs, start=True, stop=True)
                last.then_inc(s_lv[l], 1)

            def attend(t, more):
                pe.wait_ge(s["e_qk"], after(t))
                pe.wait_ge(s["rope_b"], after(t))
                pe.wait_ge(s["rope_a"], after(t))
                pe.wait_ge(s["e_small_low"], after(t))
                pe.wait_ge(s["ev_mixT"], after(t - 1))
                for b in range(4):
                    pe.transpose(tr[:, b * P:(b + 1) * P], z_qk[:, b * P:(b + 1) * P], ident[:])
                for b in range(GRP):
                    last = pe.transpose(tr[:, 512 + b * P:512 + (b + 1) * P], z_sqk[:, b, :, :], ident[:])
                last.then_inc(s["zT"], 1)
                pe.wait_ge(s["st_new"], after(t - 1))
                pe.wait_ge(s["o_scaled"], after(t - 1))
                pe.transpose(sc[:, 0:P], z_sqk[:, GRP, :, :], ident[:]).then_inc(s["sT_k"], 1)
                pe.transpose(sc[0:RANK, 512:512 + P], z_low[:], ident[:]).then_inc(s["sT_low"], 1)
                pe.wait_ge(s["ev_low"], after(t))
                for pair in range(2):
                    last = pe.matmul(gk_ps[:, pair * P:(pair + 1) * P], w2[:, pair * P:(pair + 1) * P], lowT[:],
                                     start=True, stop=True)
                last.then_inc(s["gk"], 1)
                if more:
                    project(t + 1, "qk")
                plain(pe)
                pe.wait_ge(s["ev_k"], after(t))
                pe.wait_ge(s["ev_sqT"], after(t))
                pe.wait_ge(s["g_pre"], after(t))
                for b in range(GRP):
                    for g in range(KVH):
                        rows = slice(g * HD, (g + 1) * HD)
                        for c in range(2):
                            last = pe.matmul(
                                sc[c * CHUNK:(c + 1) * CHUNK, g * 512 + b * P:g * 512 + (b + 1) * P],
                                sqT[rows, b, c * CHUNK:(c + 1) * CHUNK], kwin[rows, c * CHUNK:c * CHUNK + P],
                                start=True, stop=True)
                last.then_inc(s["swa_s"], 1)
                if more:
                    project(t + 1, "sq")
                    project(t + 1, "small")
                pe.wait_ge(s["swa_exp"], after(t))
                pe.wait_ge(s["ev_qkT"], after(t))
                for h in range(SH):
                    last = pe.transpose(tr[:, h * P:(h + 1) * P], prob[:, h, :], ident[:])
                last.then_inc(s["swa_pT"], 1)
                for l in range(NL + 1):
                    level(t, l)
                pe.wait_ge(s["g_kd"], after(t))
                pe.wait_ge(s["ev_pT"], after(t))
                for pair in range(2):
                    last = pe.transpose(tr[:, pair * P:(pair + 1) * P], kd[:, pair * P:(pair + 1) * P], ident[:])
                last.then_inc(s["kdT"], 1)
                pe.wait_ge(s["vmid_hi"], after(t))
                pe.wait_ge(s_mg[NL - 1], after(t))
                for h in range(SH):
                    g = h // GRP
                    for c, vals in ((0, v_mid), (1, v_cur)):
                        last = pe.matmul(ob[c * CHUNK:(c + 1) * CHUNK, 512 + h * HD:512 + (h + 1) * HD],
                                         probT[:, h, c * CHUNK:(c + 1) * CHUNK], vals[:, g * HD:(g + 1) * HD],
                                         start=True, stop=True)
                last.then_inc(s["swa_o"], 1)
                if more:
                    project(t + 1, "v")
                pe.wait_ge(s["g_qb"], after(t))
                pe.wait_ge(s_mg[NL], after(t))
                pe.wait_ge(s["st_new"], after(t - 1))
                pe.wait_ge(s["e_v"], after(t))
                for h in range(GH):
                    pair, par = h // 2, h % 2
                    rows = slice(par * DK, (par + 1) * DK)
                    pe.matmul(gla_out[par][:, pair * DV:(pair + 1) * DV], qb[rows, pair * P:(pair + 1) * P],
                              state[rows, pair, :], start=True, stop=False)
                    last = pe.matmul(gla_out[par][:, pair * DV:(pair + 1) * DV], pT[:, par, pair, :],
                                     z_v[:, h * DV:(h + 1) * DV], start=False, stop=True)
                last.then_inc(s["gla_o"], 1)
                pe.wait_ge(s["ev_kd"], after(t))
                for h in range(GH):
                    pair, par = h // 2, h % 2
                    last = pe.matmul(sc[par * DK:(par + 1) * DK, pair * DV:(pair + 1) * DV],
                                     kdN[:, h * DK:(h + 1) * DK], z_v[:, h * DV:(h + 1) * DV], start=True, stop=True)
                last.then_inc(s["gla_up"], 1)
                if more:
                    project(t + 1, "r")
                pe.wait_ge(s["o_mix"], after(t))
                pe.wait_ge(s["swa_mix"], after(t))
                pe.wait_ge(s["ev_kd"], after(t))
                for b in range(KD):
                    last = pe.transpose(tr[:, b * P:(b + 1) * P], mix[:, b * P:(b + 1) * P], ident[:])
                last.then_inc(s["mixT_done"], 1)

            pe.wait_ge(s["const_ready"], 1)
            turn_x(0)
            for i, g in enumerate(GROUPS):
                pe.wait_ge(s["w_split_lo"], (i + 1) * KD)
                project(0, g)
            turn_x(1)
            with pe.Fori(0, NT - 2) as t:
                attend(t, True)
                turn_x(t + 2)
            attend(NT - 2, True)
            attend(NT - 1, False)

        @block.scalar
        def _(act):
            prime(act, "act")

            def norm_x(n):
                act.wait_ge(s["x_rstd"], after(n))
                act.activation(x[:], x[:], ACT.Copy, scale=rstd[:, 0:1]).then_inc(s["x_norm"], 1)

            def split_h(n):
                act.wait_ge(s["xT"], after(n))
                act.wait_ge(s_g["r"], after(n - 1))
                act.activation(h_hi[:].rearrange("p k n -> p (k n)"), ob[:], ACT.Copy).then_inc(s["hT_hi"], 1)

            def evac(n, g):
                act.wait_ge(s_g[g], after(n))
                bank = pj[GROUPS.index(g) % 2]
                if g == "qk":
                    act.wait_ge(s["zT"], after(n - 1))
                    act.activation(z_qk[:], bank[:], ACT.Copy).then_inc(s["e_qk"], 1)
                elif g == "sq":
                    act.wait_ge(s["zT"], after(n - 1))
                    act.activation(z_sqk[:, 0:GRP].rearrange("p b g d -> p g b d"),
                                   bank[:].rearrange("p (g b d) -> p g b d", g=KVH, b=GRP), ACT.Copy
                                   ).then_inc(s["e_sq"], 1)
                elif g == "small":
                    act.wait_ge(s["sT_low"], after(n - 1))
                    act.activation(z_low[:], bank[:, 0:RANK], ACT.Copy).then_inc(s["e_small_low"], 1)
                    act.activation(z_sqk[:, GRP].rearrange("p g d -> p (g d)"), bank[:, RANK:RANK + SKV], ACT.Copy
                                   ).then_inc(s["e_small_k"], 1)
                    act.wait_ge(s["v_copy"], after(n - 1))
                    act.activation(z_sv[:], bank[:, RANK + SKV:RANK + 2 * SKV], ACT.Copy).then_inc(s["e_sv"], 1)
                elif g == "v":
                    act.wait_ge(s["gla_up"], after(n - 1))
                    act.activation(z_v[:], bank[:], ACT.Copy).then_inc(s["e_v"], 1)
                else:
                    act.wait_ge(s["o_mix"], after(n - 1))
                    act.activation(z_r[:], bank[:], ACT.Copy).then_inc(s["e_r"], 1)
                    act.activation(gate[:], bank[:], ACT.Exp, scale=-1.0).then_inc(s["r_exp"], 1)

            for dst, src in ((ident[:], t_in["c_ident"]), (rope_room[:, 0:(NL - 1) * P], t_in["c_masks"]),
                             (swa_mask[:], t_in["c_swa_mask"]), (invf[:], t_in["c_inv_freq"]),
                             (w2[:], t_in["gla_gk_w2"][0]),
                             (gkb[:], t_in["gla_gk_b"][0].rearrange("(k p) -> p k", p=P)),
                             (sinks[:], t_in["swa_sinks"][0].partition_broadcast(P)),
                             (pos_i[:], t_in["positions"][0].rearrange("(t p) -> p t", p=P))):
                act.dma_start(dst, src, allow_slow_non_contiguous=True).then_inc(s_const, 16)
            act.wait_ge(s["norm1_load"], 16)
            for n, (g, k) in enumerate(pieces):
                act.wait_ge(s_w[n % NSTAGE], loaded(n))
                act.activation(w_hi[:, k, FIRST[g]:FIRST[g] + WIDTH[g]], stage[n % NSTAGE][:, 0:WIDTH[g]], ACT.Copy,
                               scale=norm1[:, k:k + 1]).then_inc(s["w_split_hi"], 1)
                if n == NSTAGE - 1:
                    norm_x(0)
                    split_h(0)
                if k == KD - 1 and n >= KD:
                    evac(0, GROUPS[n // KD - 1])
            act.wait_ge(s["rope_tab"], 1)
            act.activation(sinT[:], sinT[:], ACT.Sin)
            act.activation(cosT[:], cosT[:], ACT.Sin).then_inc(s["rope_act"], 1)
            evac(0, GROUPS[-1])
            norm_x(1)
            split_h(1)

            def attend(t, more, norm_next):
                act.wait_ge(s["swa_s"], after(t - 1))
                act.activation(kwin[:, 0:CHUNK], kwin[:, P:P + CHUNK], ACT.Copy).then_inc(s["ev_kshift"], 1)
                act.wait_ge(s["sT_low"], after(t))
                act.wait_ge(s["gk"], after(t - 1))
                act.activation(lowT[:], sc[0:RANK, 512:512 + P], ACT.Copy).then_inc(s["ev_low"], 1)
                act.wait_ge(s["ev_kshift"], after(t))
                act.activation(kwin[:, CHUNK:CHUNK + P], sc[:, 0:P], ACT.Copy).then_inc(s["ev_k"], 1)
                act.activation(qkT[:].rearrange("p b n -> p (b n)"), tr[:, 0:512], ACT.Copy).then_inc(s["ev_qkT"], 1)
                act.wait_ge(s["swa_o"], after(t - 1))
                act.activation(v_mid[0:CHUNK, :], v_cur[CHUNK:P, :], ACT.Copy).then_inc(s["vmid_lo"], 1)
                act.wait_ge(s["vmid_lo"], after(t))
                act.wait_ge(s["e_sv"], after(t))
                act.activation(v_cur[:], z_sv[:], ACT.Copy).then_inc(s["v_copy"], 1)
                act.activation(v_mid[CHUNK:P, :], z_sv[0:CHUNK, :], ACT.Copy).then_inc(s["vmid_hi"], 1)
                act.wait_ge(s["g_pre"], after(t))
                act.activation(gate_l[:], gate_a[:], ACT.Abs).then_inc(s["g_abs"], 1)
                act.wait_ge(s["g_abs"], after(t))
                act.activation(gate_l[:], gate_l[:], ACT.Exp, scale=-1.0).then_inc(s["g_exp"], 1)
                act.wait_ge(s["g_exp"], after(t))
                act.activation(gate_l[:], gate_l[:], ACT.Ln, bias=1.0).then_inc(s["g_log"], 1)
                act.wait_ge(s["g_scan"], after(t))
                act.activation(Eb[:], B[:], ACT.Exp, scale=1.0 / GATE_NORM).then_inc(s["g_eb"], 1)
                act.wait_ge(s["g_kdiff"], after(t))
                act.activation(kd[:], kd[:], ACT.Exp, scale=-1.0 / GATE_NORM).then_inc(s["g_kexp"], 1)
                for i, (l0, l1) in enumerate(SPAN_PARTS):
                    act.wait_ge(s[f"lv_diff{i}"], after(t))
                    if i == 1:
                        if more:
                            evac(t + 1, "qk")
                        act.wait_ge(s["swa_s"], after(t))
                    act.activation(qs[:, l0:l1], ks[:, l0:l1], ACT.Exp, scale=-1.0 / GATE_NORM
                                   ).then_inc(s[f"lv_exp{i}"], 1)
                act.wait_ge(s["swa_neg"], after(t))
                for h in range(SH):
                    last = act.activation(prob[:, h, :], prob[:, h, :], ACT.Exp, bias=negm[:, h:h + 1],
                                          scale=HD ** -0.5, accum_out=den[:, h:h + 1])
                last.then_inc(s["swa_exp"], 1)
                act.wait_ge(s["swa_sinkd"], after(t))
                act.activation(esink[:], esink[:], ACT.Exp).then_inc(s["swa_sinke"], 1)
                if more:
                    evac(t + 1, "sq")
                    evac(t + 1, "small")
                act.wait_ge(s["swa_pT"], after(t))
                act.wait_ge(s_out, after(t - 1) * 16)
                act.activation(probT[:].rearrange("p h n -> p (h n)"), tr[:], ACT.Copy).then_inc(s["ev_pT"], 1)
                act.wait_ge(s["kdT"], after(t))
                act.wait_ge(s["gla_up"], after(t - 1))
                act.activation(kdN[:], tr[:, 0:2 * P], ACT.Copy).then_inc(s["ev_kd"], 1)
                if norm_next:
                    norm_x(t + 2)
                act.wait_ge(s["gla_o"], after(t))
                for h in range(GH):
                    last = act.activation(squares[:, h], gla_out[h % 2][:, (h // 2) * DV:(h // 2 + 1) * DV],
                                          ACT.Square, scale=DK ** -0.5, accum_out=ossq[:, h:h + 1])
                last.then_inc(s["o_ssq"], 1)
                if more:
                    evac(t + 1, "v")
                    evac(t + 1, "r")
                act.wait_ge(s["mixT_done"], after(t))
                act.activation(mixT[:].rearrange("p h n -> p (h n)"), tr[:], ACT.Copy).then_inc(s["ev_mixT"], 1)

            with act.Fori(0, NT - 2) as t:
                attend(t, True, True)
                split_h(t + 2)
            attend(NT - 2, True, False)
            attend(NT - 1, False, False)

        @block.gpsimd
        def _(pool):
            prime(pool, "pool")

            pool.memset(nhalf[:], -0.5).then_inc(s["pool_setup"], 1)
            pool.wait_ge(s["pool_setup"], 1)

            def x_rstd(n):
                pool.wait_ge(s["x_eps"], after(n))
                pool.tensor_tensor(rstd[:], ms[:], nhalf[:, 0:1], ALU.pow).then_inc(s["x_rstd"], 1)

            def attend(t):
                pool.wait_ge(s["o_eps"], after(t))
                pool.tensor_tensor(orstd[:], ossq[:], nhalf[:], ALU.pow).then_inc(s["o_rstd"], 1)

            x_rstd(0)
            x_rstd(1)
            with pool.Fori(0, NT - 2) as t:
                x_rstd(t + 2)
                attend(t)
            attend(NT - 2)
            attend(NT - 1)

        @block.vector
        def _(dve):
            prime(dve, "dve")

            steps = [0]

            def then(ins):
                steps[0] += 1
                ins.then_inc(s["dve_setup"], 1)
                dve.wait_ge(s["dve_setup"], steps[0])

            def norm_x(n):
                dve.wait_ge(s_x, after(n) * 16)
                dve.bn_stats(stats[:, 0, :], x[:, 0:512])
                dve.bn_stats(stats[:, 1, :], x[:, 512:1024]).then_inc(s["x_stats"], 1)
                plain(dve)
                dve.wait_ge(s["x_stats"], after(n))
                dve.bn_aggr(mv[:], stats[:].rearrange("p a b -> p (a b)")).then_inc(s["x_ms"], 1)
                dve.wait_ge(s["x_ms"], after(n))
                dve.scalar_tensor_tensor(out=ms[:], in0=mv[:, 0:1], scalar=mv[:, 0:1], in1=mv[:, 1:2],
                                         op0=ALU.mult, op1=ALU.add).then_inc(s["x_sum"], 1)
                dve.wait_ge(s["x_sum"], after(n))
                dve.tensor_scalar(ms[:], ms[:], EPS, None, ALU.add).then_inc(s["x_eps"], 1)

            def split_h(n):
                dve.wait_ge(s["hT_hi"], after(n))
                dve.tensor_tensor(h_lo[:].rearrange("p k n -> p (k n)"), ob[:],
                                  h_hi[:].rearrange("p k n -> p (k n)").bitcast(F32), ALU.subtract
                                  ).then_inc(s["hT_lo"], 1)

            def rope(n):
                heads = z_sqk[:].rearrange("p b g d -> p (b g) d")[:, :, 0:ROPE]
                halves = heads.rearrange("p h (a r) -> p h a r", a=2)
                nh = (GRP + 1) * KVH
                dve.wait_ge(s["e_sq"], after(n))
                dve.wait_ge(s["e_small_k"], after(n))
                ra = ropeA.rearrange("p h (a r) -> p h a r", a=2)
                rb = ropeB.rearrange("p h (a r) -> p h a r", a=2)
                for a in range(2):
                    c = cosT[:, bass.ds(n, 1), :].to_broadcast([P, nh, RH])
                    sn = sinT[:, bass.ds(n, 1), :].to_broadcast([P, nh, RH])
                    dve.tensor_tensor(ra[:, :, a, :], halves[:, :, a, :], c, ALU.mult)
                    last = dve.tensor_tensor(rb[:, :, a, :], halves[:, :, a, :], sn, ALU.mult)
                last.then_inc(s["rope_mul"], 1)
                dve.wait_ge(s["rope_mul"], after(n))
                dve.tensor_tensor(halves[:, :, 0, :], ra[:, :, 0, :], rb[:, :, 1, :], ALU.subtract
                                  ).then_inc(s["rope_a"], 1)
                dve.tensor_tensor(halves[:, :, 1, :], ra[:, :, 1, :], rb[:, :, 0, :], ALU.add
                                  ).then_inc(s["rope_b"], 1)

            def gate_r(n):
                dve.wait_ge(s["r_exp"], after(n))
                dve.tensor_scalar(gate[:], gate[:], 1.0, None, ALU.add).then_inc(s["r_one"], 1)
                dve.wait_ge(s["r_one"], after(n))
                dve.reciprocal(gate[:], gate[:]).then_inc(s["r_rec"], 1)
                dve.wait_ge(s["r_rec"], after(n))
                dve.tensor_tensor(gate[:], gate[:], z_r[:], ALU.mult).then_inc(s["r_gate"], 1)

            dve.memset(state[:], 0.0)
            dve.memset(pT[:], 0.0)
            dve.memset(kwin[:], 0.0)
            dve.memset(v_cur[:], 0.0)
            dve.wait_ge(s_const, 16 * 8)
            then(dve.tensor_scalar(nsinks[:], sinks[:], -1.0, None, ALU.mult))
            then(dve.tensor_copy(masks[:].rearrange("p l n -> p (l n)"), rope_room[:, 0:(NL - 1) * P]))
            dve.memset(v_mid[:], 0.0).then_inc(s["const_ready"], 1)
            norm_x(0)
            then(dve.tensor_copy(pos_f[:], pos_i[:]))
            then(dve.tensor_tensor(ang, pos_f[:].unsqueeze(2).to_broadcast([P, NT, RH]),
                                   invf[:].unsqueeze(1).to_broadcast([P, NT, RH]), ALU.mult))
            then(dve.tensor_scalar(cosT[:], ang, 1.0 / TWO_PI, ROUNDER, ALU.mult, ALU.add))
            then(dve.tensor_scalar(cosT[:], cosT[:], -ROUNDER, None, ALU.add))
            for part in (TP_A, TP_B, TP_C):
                then(dve.scalar_tensor_tensor(out=ang, in0=cosT[:], scalar=-part, in1=ang,
                                              op0=ALU.mult, op1=ALU.add))
            then(dve.tensor_scalar(sinT[:], ang, PI_IN, -PI_IN, ALU.min, ALU.max))
            then(dve.tensor_scalar(ang, ang, TWO_PI / 4, None, ALU.add))
            then(dve.tensor_scalar(cosT[:], ang, TWO_PI / 2, -TWO_PI, ALU.is_gt, ALU.mult))
            then(dve.tensor_tensor(cosT[:], cosT[:], ang, ALU.add))
            dve.tensor_scalar(cosT[:], cosT[:], PI_IN, -PI_IN, ALU.min, ALU.max).then_inc(s["rope_tab"], 1)
            for n, (g, k) in enumerate(pieces):
                dve.wait_ge(s["w_split_hi"], n + 1)
                cols = slice(FIRST[g], FIRST[g] + WIDTH[g])
                dve.scalar_tensor_tensor(out=w_lo[:, k, cols], in0=stage[n % NSTAGE][:, 0:WIDTH[g]],
                                         scalar=norm1[:, k:k + 1], in1=w_hi[:, k, cols].bitcast(F32),
                                         op0=ALU.mult, op1=ALU.subtract).then_inc(s["w_split_lo"], 1)
                if n == NSTAGE - 1:
                    split_h(0)
            norm_x(1)
            dve.wait_ge(s["rope_act"], 1)
            rope(0)
            split_h(1)

            def attend(t, more, norm_next):
                dve.wait_ge(s["zT"], after(t))
                dve.tensor_copy(sqT.rearrange("p b n -> p (b n)"), tr[:, 512:1024]).then_inc(s["ev_sqT"], 1)
                dve.wait_ge(s["gk"], after(t))
                dve.tensor_scalar(gate_a[:, 0:P], gk_ps[:, 0:P], gkb[:, 0:1], None, ALU.add)
                dve.tensor_scalar(gate_a[:, P:2 * P], gk_ps[:, P:2 * P], gkb[:, 1:2], None, ALU.add
                                  ).then_inc(s["g_pre"], 1)
                dve.wait_ge(s["g_pre"], after(t))
                dve.wait_ge(s["o_ssq"], after(t - 1))
                dve.tensor_scalar(gate_m[:], gate_a[:], 0.0, None, ALU.min).then_inc(s["g_min"], 1)
                dve.wait_ge(s["g_log"], after(t))
                dve.wait_ge(s["g_min"], after(t))
                dve.tensor_tensor(gate_m[:], gate_m[:], gate_l[:], ALU.subtract).then_inc(s["g_sum"], 1)
                dve.wait_ge(s["g_sum"], after(t))
                for pair in range(2):
                    cols = slice(pair * P, (pair + 1) * P)
                    last = dve.tensor_tensor_scan(B[:, cols], gate_m[:, cols], gate_m[:, cols], 0.0,
                                                  ALU.add, ALU.bypass)
                last.then_inc(s["g_scan"], 1)
                dve.wait_ge(s["g_scan"], after(t))
                dve.wait_ge(s["kdT"], after(t - 1))
                for pair in range(2):
                    cols = slice(pair * P, (pair + 1) * P)
                    last = dve.tensor_scalar(kd[:, cols], B[:, cols], B[:, (pair + 1) * P - 1:(pair + 1) * P],
                                             None, ALU.subtract)
                last.then_inc(s["g_kdiff"], 1)
                dve.wait_ge(s_lv[NL - 1], after(t - 1))
                for i, (l0, l1) in enumerate(SPAN_PARTS):
                    for l in range(l0, l1):
                        span = SPANS[l]
                        b4 = B[:].rearrange("p (n a w) -> p n a w", a=2, w=span)
                        d4 = ks[:, l, :].rearrange("p (n a w) -> p n a w", a=2, w=span)
                        ref = b4[:, :, 0, span - 1:span].to_broadcast([P, P // span, span])
                        dve.tensor_tensor(d4[:, :, 0, :], b4[:, :, 0, :], ref, ALU.subtract)
                        last = dve.tensor_tensor(d4[:, :, 1, :], ref, b4[:, :, 1, :], ALU.subtract)
                    last.then_inc(s[f"lv_diff{i}"], 1)
                dve.wait_ge(s["ev_qkT"], after(t))

                def level_operands(i):
                    l0, l1 = SPAN_PARTS[i]
                    dve.wait_ge(s[f"lv_exp{i}"], after(t))
                    dve.tensor_tensor(ks[:, l0:l1], qkT[:, 2:4, :].rearrange("p b n -> p (b n)").unsqueeze(1)
                                      .to_broadcast([P, l1 - l0, 2 * P]), qs[:, l0:l1], ALU.mult
                                      ).then_inc(s[f"lv_k{i}"], 1)
                    dve.wait_ge(s[f"lv_k{i}"], after(t))
                    dve.tensor_tensor(qs[:, l0:l1], qkT[:, 0:2, :].rearrange("p b n -> p (b n)").unsqueeze(1)
                                      .to_broadcast([P, l1 - l0, 2 * P]), qs[:, l0:l1], ALU.mult
                                      ).then_inc(s[f"lv_qk{i}"], 1)

                level_operands(0)
                dve.wait_ge(s["swa_s"], after(t))
                dve.wait_ge(s["mixT_done"], after(t - 1))
                dve.tensor_tensor(prob[:], sc[:].rearrange("p (h k) -> p h k", h=SH),
                                  swa_mask[:].unsqueeze(1).to_broadcast([P, SH, P]), ALU.add
                                  ).then_inc(s["swa_masked"], 1)
                dve.wait_ge(s["swa_masked"], after(t))
                dve.memset(swa_mask[:], 0.0)
                dve.tensor_reduce(negm[:], prob[:], AX_X, ALU.max).then_inc(s["swa_max"], 1)
                dve.wait_ge(s["swa_max"], after(t))
                dve.scalar_tensor_tensor(out=negm[:], in0=negm[:], scalar=-(HD ** -0.5), in1=nsinks[:],
                                         op0=ALU.mult, op1=ALU.min).then_inc(s["swa_neg"], 1)
                dve.wait_ge(s["swa_neg"], after(t))
                dve.tensor_tensor(esink[:], sinks[:], negm[:], ALU.add).then_inc(s["swa_sinkd"], 1)
                level_operands(1)
                dve.wait_ge(s["g_eb"], after(t))
                dve.wait_ge(s["gla_o"], after(t - 1))
                dve.tensor_tensor(qb[:], qkT[:, 0:2, :].rearrange("p b n -> p (b n)"), Eb[:], ALU.mult
                                  ).then_inc(s["g_qb"], 1)
                dve.wait_ge(s["g_kexp"], after(t))
                dve.tensor_tensor(kd[:], qkT[:, 2:4, :].rearrange("p b n -> p (b n)"), kd[:], ALU.mult
                                  ).then_inc(s["g_kd"], 1)
                dve.wait_ge(s["swa_exp"], after(t))
                dve.wait_ge(s["swa_sinke"], after(t))
                dve.tensor_tensor(den[:], den[:], esink[:], ALU.add).then_inc(s["swa_den"], 1)
                dve.wait_ge(s["swa_den"], after(t))
                dve.reciprocal(rden[:], den[:]).then_inc(s["swa_rden"], 1)
                dve.wait_ge(s["gla_o"], after(t - 1))
                for l in range(NL + 1):
                    bank = ob if l % 2 == 0 else sc
                    got = bank[:].rearrange("p (a c) -> p a c", a=2)[:, :, 0:2 * P].rearrange(
                        "p a (b n) -> p a b n", b=2)
                    plain(dve)
                    dve.wait_ge(s_lv[l], after(t))
                    if l < 2:
                        w = SPANS[l]
                        for b0 in range(0, P, 2 * w):
                            last = dve.tensor_copy(pT[b0:b0 + w, :, :, b0 + w:b0 + 2 * w],
                                                   got[b0:b0 + w, :, :, b0 + w:b0 + 2 * w])
                    else:
                        m = masks[:, l - 2, :].unsqueeze(1).unsqueeze(1).to_broadcast([P, 2, 2, P])
                        if l >= 2:
                            dve.wait_ge(s_mg[l - 1], after(t))
                        last = dve.copy_predicated(pT[:], m, got)
                    last.then_inc(s_mg[l], 1)
                dve.wait_ge(s["swa_o"], after(t))
                dve.wait_ge(s["swa_rden"], after(t))
                dve.tensor_tensor(mix[:, GV:DMIX].rearrange("p (h d) -> p h d", h=SH),
                                  ob[:, 512:1024].rearrange("p (h d) -> p h d", h=SH),
                                  rden[:].unsqueeze(2).to_broadcast([P, SH, HD]), ALU.mult
                                  ).then_inc(s["swa_mix"], 1)
                if more:
                    rope(t + 1)
                if norm_next:
                    norm_x(t + 2)
                gate_r(t)
                dve.wait_ge(s["gla_o"], after(t))
                for pair in range(2):
                    last = dve.tensor_scalar(state[:, pair, :], state[:, pair, :],
                                             Eb[:, (pair + 1) * P - 1:(pair + 1) * P], None, ALU.mult)
                last.then_inc(s["st_scaled"], 1)
                dve.wait_ge(s["o_ssq"], after(t))
                dve.tensor_scalar(ossq[:], ossq[:], 1.0 / DV, EPS, ALU.mult, ALU.add).then_inc(s["o_eps"], 1)
                dve.wait_ge(s["gla_up"], after(t))
                dve.wait_ge(s["st_scaled"], after(t))
                dve.tensor_tensor(state[:].rearrange("p a v -> p (a v)"), state[:].rearrange("p a v -> p (a v)"),
                                  sc[:, 0:2 * DV], ALU.add).then_inc(s["st_new"], 1)
                dve.wait_ge(s["o_rstd"], after(t))
                for par in range(2):
                    last = dve.scalar_tensor_tensor(
                        out=mix[:, 0:GV].rearrange("p (a b v) -> p b a v", a=2, b=2)[:, par],
                        in0=gla_out[par].rearrange("p (a v) -> p a v", a=2), scalar=DK ** -0.5,
                        in1=orstd[:].rearrange("p (a b) -> p b a", b=2)[:, par].unsqueeze(2)
                        .to_broadcast([P, 2, DV]), op0=ALU.mult, op1=ALU.mult)
                last.then_inc(s["o_scaled"], 1)
                dve.wait_ge(s["o_scaled"], after(t))
                dve.wait_ge(s["r_gate"], after(t))
                dve.tensor_tensor(mix[:, 0:GV], mix[:, 0:GV], gate[:], ALU.mult).then_inc(s["o_mix"], 1)

            with dve.Fori(0, NT - 2) as t:
                attend(t, True, True)
                split_h(t + 2)
            attend(NT - 2, True, False)
            attend(NT - 1, False, False)
    nc.clear_and_free_semaphores(all_sems)
    nc.all_engine_barrier()


def ffn_phase(nc, t_in, mix_scratch, out):
    with ExitStack() as ctx:
        def sb(name, shape, dt=F32):
            return ctx.enter_context(nc.sbuf_tensor(name, shape, dt))

        def ps(name, cols):
            return ctx.enter_context(nc.psum_tensor(name, [P, cols], F32))

        def sem(name):
            return ctx.enter_context(nc.semaphore(name))

        y = sb("y", [P, TPH, D])
        g2_hi = sb("h2_hi", [P, KD, TOK], F32R)
        g2_lo = sb("h2_lo", [P, KD, TOK], F32R)
        ident = sb("ident_b", [P, P])
        onorm = sb("gla_norm_col", [P, 1])
        norm2 = sb("norm2_col", [P, KD])
        fnorm = sb("final_norm_row", [P, D])
        cw = sb("conv_w_cols", [P, 3, 2 * NC_FF])
        cb = sb("conv_b_cols", [P, 2 * NC_FF])
        carry = sb("conv_carry", [P, 2 * NC_FF, 2])
        nhalf = sb("minus_half_b", [P, 1])
        stats = sb("bn_stats_b", [P, 2, 6])
        mv = sb("mean_var_b", [P, 2])
        ms = sb("mean_square_b", [P, 1])
        rstd = sb("rstd_b", [P, 1])

        gate_ps = ps("gate_ps", TOK)
        up_ps = ps("up_ps", TOK)
        acc_ps = [ps("acc_ps0", D), ps("acc_ps1", D)]

        owned = {
            "pe": "o_mm o_turned f_gate f_up",
            "act": "o_mix_hi o_normed o_split_hi f_wg_hi f_wu_hi f_wd_hi f_gate_tap f_up_tap f_silu f_g_hi",
            "pool": "o_rstd n_rstd",
            "dve": """o_mix_lo o_added o_stats o_ms o_sum o_eps o_split_lo f_wg_lo f_wu_lo f_wd_lo
                f_gate_tap1 f_gate_tap2 f_gate_edge f_gate_conv f_up_tap1 f_up_tap2 f_up_edge f_up_conv
                f_prod f_g_lo d_added n_stats n_ms n_sum n_eps n_out""",
        }
        s = {n: sem("b_" + n) for names in owned.values() for n in names.split()}
        stepped = {who: [s[n] for n in names.split()] for who, names in owned.items()}
        s_dn = [sem(f"b_down{q}") for q in range(TPH)]
        stepped["pe"] += s_dn
        s_ad = [sem(f"b_added{q}") for q in range(TPH)]
        stepped["dve"] += s_ad
        s_wo_hi, s_wo_lo, s_setup, s_pool = sem("b_wo_hi"), sem("b_wo_lo"), sem("b_setup"), sem("b_pool_setup")
        s_const = sem("b_const_load")
        s_wo = [sem("b_wo_load0"), sem("b_wo_load1")]
        s_xm = [sem("b_x_mix_load0"), sem("b_x_mix_load1")]
        s_wg, s_wu, s_wd = sem("b_wg_load"), sem("b_wu_load"), sem("b_wd_load")
        s_out = [sem("b_out_store0"), sem("b_out_store1")]

        with ExitStack() as first:
            def sb1(name, shape, dt=F32):
                return first.enter_context(nc.sbuf_tensor(name, shape, dt))

            wo_hi = sb1("w_out_hi", [P, KD, D], F32R)
            wo_lo = sb1("w_out_lo", [P, KD, D], F32R)
            wo_raw = [sb1("w_out_raw0", [P, D]), sb1("w_out_raw1", [P, D])]
            xt = [sb1("x_res0", [P, D]), sb1("x_res1", [P, D])]
            mixt = [sb1("mix0", [P, KD, P]), sb1("mix1", [P, KD, P])]
            mix_hi = [sb1("mix_hi0", [P, KD, P], F32R), sb1("mix_hi1", [P, KD, P], F32R)]
            mix_lo = [sb1("mix_lo0", [P, KD, P], F32R), sb1("mix_lo1", [P, KD, P], F32R)]
            normed = wo_raw[0]
        wg_raw = sb("w_gate_raw", [P, KD, P])
        wu_raw = sb("w_up_raw", [P, KD, P])
        wd_raw = sb("w_down_raw", [P, D])
        wg_hi, wg_lo = sb("w_gate_hi", [P, KD, P], F32R), sb("w_gate_lo", [P, KD, P], F32R)
        wu_hi, wu_lo = sb("w_up_hi", [P, KD, P], F32R), sb("w_up_lo", [P, KD, P], F32R)
        wd_hi, wd_lo = sb("w_down_hi", [P, D], F32R), sb("w_down_lo", [P, D], F32R)
        g_hi, g_lo = sb("gated_hi", [P, TOK], F32R), sb("gated_lo", [P, TOK], F32R)
        conv_g, conv_u = sb("conv_gate", [P, TOK]), sb("conv_up", [P, TOK])
        gated = sb("gated", [P, TOK])
        fin = [sb("final0", [P, D]), sb("final1", [P, D])]

        block = ctx.enter_context(nc.Block())

        def prime(eng, who):
            for one in stepped[who]:
                eng.sem_inc(one, PRIME)

        def plain(eng, value):
            eng.lower_val(value)
            eng.wait_ge(s_setup, 1)

        def load_tile(sp, n, u):
            sp.dma_start(mixt[u][:], mix_scratch[bass.ds(n, 1)].rearrange("o p k n -> (o p) k n")).then_inc(s_xm[u], 16)
            sp.dma_start(xt[u][:], t_in["x"][0, bass.ds(n * P, P), :]).then_inc(s_xm[u], 16)

        @block.sync
        def _(sp):
            for u in range(2):
                sp.sem_inc(s_out[u], 16 * PRIME)
            for dst, src in ((ident[:], t_in["c_ident"]),
                             (onorm[:], t_in["gla_norm_w"][0].rearrange("(p a) -> p a", a=1)),
                             (norm2[:], t_in["norm2_w"][0].rearrange("(k p) -> p k", p=P)),
                             (fnorm[:], t_in["final_norm_w"].partition_broadcast(P)),
                             (cw[:], t_in["conv_w"][0].rearrange("i (c p) -> p i c", p=P)),
                             (cb[:], t_in["conv_b"][0].rearrange("(c p) -> p c", p=P))):
                sp.dma_start(dst, src, allow_slow_non_contiguous=True).then_inc(s_const, 16)
            with sp.Fori(0, HALVES) as hf:
                for u in range(2):
                    sp.wait_ge(s_out[u], 16 * (hf * (TPH // 2) + PRIME))
                sp.wait_ge(s_dn[TPH - 1], hf * NC_FF + PRIME)
                for k in range(KD):
                    if k >= 2:
                        sp.wait_ge(s_wo_lo, hf * KD + (k - 1))
                    sp.dma_start(wo_raw[k % 2][:], t_in["w_out"][0, k * P:(k + 1) * P, :]).then_inc(s_wo[k % 2], 16)
                    if k < 2:
                        load_tile(sp, hf * TPH + k, k)
                with sp.Fori(0, TPH // 2 - 1) as i:
                    for u in range(2):
                        n = hf * TPH + i * 2 + (2 + u)
                        sp.wait_ge(s["o_added"], after(n - 2))
                        sp.wait_ge(s["o_mix_lo"], after(n - 2))
                        load_tile(sp, n, u)
                plain(sp, hf * TPH + (TPH + PRIME))
                sp.wait_ge(s["o_split_lo"], hf * TPH + (TPH + PRIME))

                with sp.Fori(0, NC_FF) as c:
                    m = hf * NC_FF + c
                    sp.wait_ge(s["f_wg_lo"], after(m - 1))
                    sp.dma_start(wg_raw[:], t_in["w_up"][0].rearrange("(k p) f -> p k f", p=P)[:, :, bass.ds(c * P, P)]
                                 ).then_inc(s_wg, 16)
                    sp.wait_ge(s["f_wu_lo"], after(m - 1))
                    sp.dma_start(wu_raw[:], t_in["w_up"][0].rearrange("(k p) f -> p k f", p=P)
                                 [:, :, bass.ds(c * P + FF, P)]).then_inc(s_wu, 16)
                    sp.wait_ge(s["f_wd_lo"], after(m - 1))
                    sp.dma_start(wd_raw[:], t_in["w_down"][0, bass.ds(c * P, P), :]).then_inc(s_wd, 16)
                with sp.Fori(0, TPH // 2) as i:
                    for u in range(2):
                        n = hf * TPH + i * 2 + u
                        sp.wait_ge(s["n_out"], after(n))
                        sp.dma_start(out[0, bass.ds(n * P, P), :], fin[u][:]).then_inc(s_out[u], 16)
            for u in range(2):
                sp.wait_ge(s_out[u], 16 * after(NT // 2 - 1))

        @block.tensor
        def _(pe):
            prime(pe, "pe")

            def gemm(out_ap, lhs, rhs, first, last):
                pe.matmul(out_ap, lhs[0], rhs[0], start=first, stop=False)
                pe.matmul(out_ap, lhs[0], rhs[1], start=False, stop=False)
                return pe.matmul(out_ap, lhs[1], rhs[0], start=False, stop=last)

            def project_out(n, u):
                pe.wait_ge(s["o_mix_lo"], after(n))
                pe.wait_ge(s["o_added"], after(n - 2))
                for c0 in range(0, D, 512):
                    for k in range(KD):
                        last = gemm(acc_ps[u][:, c0:c0 + 512], (mix_hi[u][:, k, :], mix_lo[u][:, k, :]),
                                    (wo_hi[:, k, c0:c0 + 512], wo_lo[:, k, c0:c0 + 512]), k == 0, k == KD - 1)
                last.then_inc(s["o_mm"], 1)

            def turn(n):
                pe.wait_ge(s["o_normed"], after(n))
                pe.wait_ge(s["o_split_lo"], after(n - 1))
                for k in range(KD):
                    last = pe.transpose(gate_ps[:, k * P:(k + 1) * P], normed[:, k * P:(k + 1) * P], ident[:])
                last.then_inc(s["o_turned"], 1)

            def raise_(bank, hi, lo, done):
                for t0 in range(0, TOK, 512):
                    for k in range(KD):
                        last = gemm(bank[:, t0:t0 + 512], (hi[:, k, :], lo[:, k, :]),
                                    (g2_hi[:, k, t0:t0 + 512], g2_lo[:, k, t0:t0 + 512]), k == 0, k == KD - 1)
                last.then_inc(done, 1)

            def lower(m, tiles):
                pe.wait_ge(s["f_g_lo"], after(m))
                pe.wait_ge(s["f_wd_lo"], after(m))
                for q in tiles:
                    if q >= 2:
                        pe.wait_ge(s_ad[q - 2], after(m))
                    else:
                        pe.wait_ge(s_ad[TPH - 2 + q], after(m - 1))
                    cols = slice(q * P, (q + 1) * P)
                    for c0 in range(0, D, 512):
                        last = gemm(acc_ps[q % 2][:, c0:c0 + 512], (g_hi[:, cols], g_lo[:, cols]),
                                    (wd_hi[:, c0:c0 + 512], wd_lo[:, c0:c0 + 512]), True, True)
                    last.then_inc(s_dn[q], 1)

            def gate_part(m):
                pe.wait_ge(s["f_wg_lo"], after(m))
                pe.wait_ge(s["f_gate_conv"], after(m - 1))
                raise_(gate_ps, wg_hi, wg_lo, s["f_gate"])

            def up_part(m):
                pe.wait_ge(s["f_wu_lo"], after(m))
                pe.wait_ge(s["f_up_conv"], after(m - 1))
                raise_(up_ps, wu_hi, wu_lo, s["f_up"])

            pe.wait_ge(s_setup, 1)
            with pe.Fori(0, HALVES) as hf:
                plain(pe, hf * KD + KD)
                pe.wait_ge(s_wo_lo, hf * KD + KD)
                with pe.Fori(0, TPH // 2) as i:
                    for u in range(2):
                        project_out(hf * TPH + i * 2 + u, u)
                    for u in range(2):
                        turn(hf * TPH + i * 2 + u)
                pe.wait_ge(s["o_split_lo"], hf * TPH + (TPH + PRIME))
                gate_part(hf * NC_FF)
                up_part(hf * NC_FF)
                with pe.Fori(0, NC_FF - 1) as c:
                    m = hf * NC_FF + c
                    gate_part(m + 1)
                    lower(m, range(0, TPH // 2))
                    up_part(m + 1)
                    lower(m, range(TPH // 2, TPH))
                m = hf * NC_FF + (NC_FF - 1)
                lower(m, range(TPH))

        @block.scalar
        def _(act):
            prime(act, "act")
            act.wait_ge(s_setup, 1)

            def split_w(m, raw, hi, loaded, free, done):
                act.wait_ge(loaded, (m + 1) * 16)
                act.wait_ge(free, after(m - 1))
                for k in range(KD):
                    last = act.activation(hi[:, k, :], raw[:, k, :], ACT.Copy, scale=norm2[:, k:k + 1])
                last.then_inc(done, 1)

            def middle_tap(m, bank, conv, col, ready, free, done):
                act.wait_ge(ready, after(m))
                act.wait_ge(free, after(m - 1))
                act.activation(conv[:], bank[:], ACT.Identity, bias=cb[:, bass.ds(col, 1)],
                               scale=cw[:, 2, bass.ds(col, 1)]).then_inc(done, 1)

            with act.Fori(0, HALVES) as hf:
                for k in range(KD):
                    act.wait_ge(s_wo[k % 2], 16 * (hf * (KD // 2) + (k // 2 + 1)))
                    if k < GV // P:
                        act.activation(wo_hi[:, k, :], wo_raw[k % 2][:], ACT.Copy, scale=onorm[:, 0:1]
                                       ).then_inc(s_wo_hi, 1)
                    else:
                        act.activation(wo_hi[:, k, :], wo_raw[k % 2][:], ACT.Copy).then_inc(s_wo_hi, 1)
                with act.Fori(0, TPH // 2) as i:
                    for u in range(2):
                        n = hf * TPH + i * 2 + u
                        act.wait_ge(s_xm[u], 32 * (hf * (TPH // 2) + i + 1))
                        act.wait_ge(s["o_mm"], after(n - 2))
                        act.activation(mix_hi[u][:], mixt[u][:], ACT.Copy).then_inc(s["o_mix_hi"], 1)
                    for u in range(2):
                        n = hf * TPH + i * 2 + u
                        act.wait_ge(s["o_rstd"], after(n))
                        act.wait_ge(s["o_turned"], after(n - 1))
                        act.activation(normed[:], y[:, bass.ds(i * 2 + u, 1), :].rearrange("p o d -> p (o d)"),
                                       ACT.Copy, scale=rstd[:, 0:1]).then_inc(s["o_normed"], 1)
                        act.wait_ge(s["o_turned"], after(n))
                        act.activation(g2_hi[:, :, bass.ds(i * (2 * P) + u * P, P)],
                                       gate_ps[:].rearrange("p (k n) -> p k n", k=KD), ACT.Copy
                                       ).then_inc(s["o_split_hi"], 1)

                m0 = hf * NC_FF
                split_w(m0, wg_raw, wg_hi, s_wg, s["f_gate"], s["f_wg_hi"])
                split_w(m0, wu_raw, wu_hi, s_wu, s["f_up"], s["f_wu_hi"])

                def gated_part(m, c):
                    middle_tap(m, up_ps, conv_u, c + NC_FF, s["f_up"], s["f_prod"], s["f_up_tap"])
                    act.wait_ge(s["f_gate_conv"], after(m))
                    act.activation(conv_g[:], conv_g[:], ACT.Silu).then_inc(s["f_silu"], 1)
                    act.wait_ge(s_wd, (m + 1) * 16)
                    act.wait_ge(s_dn[TPH - 1], after(m - 1))
                    act.activation(wd_hi[:], wd_raw[:], ACT.Copy).then_inc(s["f_wd_hi"], 1)
                    act.wait_ge(s["f_prod"], after(m))
                    act.activation(g_hi[:], gated[:], ACT.Copy).then_inc(s["f_g_hi"], 1)

                with act.Fori(0, NC_FF - 1) as c:
                    m = hf * NC_FF + c
                    middle_tap(m, gate_ps, conv_g, c, s["f_gate"], s["f_prod"], s["f_gate_tap"])
                    split_w(m + 1, wg_raw, wg_hi, s_wg, s["f_gate"], s["f_wg_hi"])
                    gated_part(m, c)
                    split_w(m + 1, wu_raw, wu_hi, s_wu, s["f_up"], s["f_wu_hi"])
                c, m = NC_FF - 1, hf * NC_FF + (NC_FF - 1)
                middle_tap(m, gate_ps, conv_g, c, s["f_gate"], s["f_prod"], s["f_gate_tap"])
                gated_part(m, c)

        @block.gpsimd
        def _(pool):
            prime(pool, "pool")
            pool.memset(nhalf[:], -0.5).then_inc(s_pool, 1)
            pool.wait_ge(s_pool, 1)
            with pool.Fori(0, HALVES) as hf:
                with pool.Fori(0, TPH) as q:
                    pool.wait_ge(s["o_eps"], after(hf * TPH + q))
                    pool.tensor_tensor(rstd[:], ms[:], nhalf[:], ALU.pow).then_inc(s["o_rstd"], 1)
                with pool.Fori(0, TPH) as q:
                    pool.wait_ge(s["n_eps"], after(hf * TPH + q))
                    pool.tensor_tensor(rstd[:], ms[:], nhalf[:], ALU.pow).then_inc(s["n_rstd"], 1)

        @block.vector
        def _(dve):
            prime(dve, "dve")
            dve.memset(carry[:], 0.0)
            dve.wait_ge(s_const, 16 * 6)
            dve.memset(ms[:], 0.0).then_inc(s_setup, 1)
            dve.wait_ge(s_setup, 1)

            def mean_square(n, tile, pre, ready):
                plain(dve, ready[1])
                dve.wait_ge(*ready)
                dve.bn_stats(stats[:, 0, :], tile[:, 0:512])
                dve.bn_stats(stats[:, 1, :], tile[:, 512:1024]).then_inc(s[pre + "stats"], 1)
                plain(dve, after(n))
                dve.wait_ge(s[pre + "stats"], after(n))
                dve.bn_aggr(mv[:], stats[:].rearrange("p a b -> p (a b)")).then_inc(s[pre + "ms"], 1)
                dve.wait_ge(s[pre + "ms"], after(n))
                dve.scalar_tensor_tensor(out=ms[:], in0=mv[:, 0:1], scalar=mv[:, 0:1], in1=mv[:, 1:2],
                                         op0=ALU.mult, op1=ALU.add).then_inc(s[pre + "sum"], 1)
                dve.wait_ge(s[pre + "sum"], after(n))
                dve.tensor_scalar(ms[:], ms[:], EPS, None, ALU.add).then_inc(s[pre + "eps"], 1)

            def split_w(m, raw, hi, lo, done_hi, done):
                dve.wait_ge(done_hi, after(m))
                for k in range(KD):
                    last = dve.scalar_tensor_tensor(out=lo[:, k, :], in0=raw[:, k, :], scalar=norm2[:, k:k + 1],
                                                    in1=hi[:, k, :].bitcast(F32), op0=ALU.mult, op1=ALU.subtract)
                last.then_inc(done, 1)

            def add_down(m, tiles):
                for q in tiles:
                    dve.wait_ge(s_dn[q], after(m))
                    dve.tensor_tensor(y[:, q, :], y[:, q, :], acc_ps[q % 2][:], ALU.add).then_inc(s_ad[q], 1)

            def conv(m, bank, acc, col, pre):
                tap0, tap1 = cw[:, 0, bass.ds(col, 1)], cw[:, 1, bass.ds(col, 1)]
                old = carry[:, bass.ds(col, 1), :].rearrange("p o a -> p (o a)")
                dve.wait_ge(s[pre + "tap"], after(m))
                dve.scalar_tensor_tensor(out=acc[:, 1:TOK], in0=bank[:, 0:TOK - 1], scalar=tap1,
                                         in1=acc[:, 1:TOK], op0=ALU.mult, op1=ALU.add).then_inc(s[pre + "tap1"], 1)
                dve.wait_ge(s[pre + "tap1"], after(m))
                dve.scalar_tensor_tensor(out=acc[:, 2:TOK], in0=bank[:, 0:TOK - 2], scalar=tap0,
                                         in1=acc[:, 2:TOK], op0=ALU.mult, op1=ALU.add)
                dve.scalar_tensor_tensor(out=acc[:, 0:1], in0=old[:, 1:2], scalar=tap1, in1=acc[:, 0:1],
                                         op0=ALU.mult, op1=ALU.add).then_inc(s[pre + "tap2"], 1)
                dve.wait_ge(s[pre + "tap2"], after(m))
                dve.scalar_tensor_tensor(out=acc[:, 0:2], in0=old, scalar=tap0, in1=acc[:, 0:2],
                                         op0=ALU.mult, op1=ALU.add).then_inc(s[pre + "edge"], 1)
                plain(dve, after(m))
                dve.wait_ge(s[pre + "edge"], after(m))
                dve.tensor_copy(old, bank[:, TOK - 2:TOK]).then_inc(s[pre + "conv"], 1)

            def gated_part(m, c):
                conv(m, up_ps, conv_u, c + NC_FF, "f_up_")
                dve.wait_ge(s["f_silu"], after(m))
                dve.wait_ge(s["f_up_conv"], after(m))
                dve.wait_ge(s["f_g_lo"], after(m - 1))
                dve.tensor_tensor(gated[:], conv_g[:], conv_u[:], ALU.mult).then_inc(s["f_prod"], 1)
                dve.wait_ge(s["f_wd_hi"], after(m))
                dve.tensor_tensor(wd_lo[:], wd_raw[:], wd_hi[:].bitcast(F32), ALU.subtract).then_inc(s["f_wd_lo"], 1)
                dve.wait_ge(s["f_g_hi"], after(m))
                dve.tensor_tensor(g_lo[:], gated[:], g_hi[:].bitcast(F32), ALU.subtract).then_inc(s["f_g_lo"], 1)

            with dve.Fori(0, HALVES) as hf:
                for k in range(KD):
                    dve.wait_ge(s_wo_hi, hf * KD + (k + 1))
                    if k < GV // P:
                        dve.scalar_tensor_tensor(out=wo_lo[:, k, :], in0=wo_raw[k % 2][:], scalar=onorm[:, 0:1],
                                                 in1=wo_hi[:, k, :].bitcast(F32), op0=ALU.mult, op1=ALU.subtract
                                                 ).then_inc(s_wo_lo, 1)
                    else:
                        dve.tensor_tensor(wo_lo[:, k, :], wo_raw[k % 2][:], wo_hi[:, k, :].bitcast(F32),
                                          ALU.subtract).then_inc(s_wo_lo, 1)
                with dve.Fori(0, TPH // 2) as i:
                    for u in range(2):
                        n = hf * TPH + i * 2 + u
                        dve.wait_ge(s["o_mix_hi"], after(n))
                        dve.tensor_tensor(mix_lo[u][:], mixt[u][:], mix_hi[u][:].bitcast(F32), ALU.subtract
                                          ).then_inc(s["o_mix_lo"], 1)
                    for u in range(2):
                        n = hf * TPH + i * 2 + u
                        tile = y[:, bass.ds(i * 2 + u, 1), :].rearrange("p o d -> p (o d)")
                        dve.wait_ge(s["o_mm"], after(n))
                        dve.wait_ge(s_xm[u], 32 * (hf * (TPH // 2) + i + 1))
                        dve.tensor_tensor(tile, acc_ps[u][:], xt[u][:], ALU.add).then_inc(s["o_added"], 1)
                        mean_square(n, tile, "o_", (s["o_added"], after(n)))
                        dve.wait_ge(s["o_split_hi"], after(n))
                        dve.tensor_tensor(g2_lo[:, :, bass.ds(i * (2 * P) + u * P, P)],
                                          gate_ps[:].rearrange("p (k n) -> p k n", k=KD),
                                          g2_hi[:, :, bass.ds(i * (2 * P) + u * P, P)].bitcast(F32), ALU.subtract
                                          ).then_inc(s["o_split_lo"], 1)
                m0 = hf * NC_FF
                split_w(m0, wg_raw, wg_hi, wg_lo, s["f_wg_hi"], s["f_wg_lo"])
                split_w(m0, wu_raw, wu_hi, wu_lo, s["f_wu_hi"], s["f_wu_lo"])

                conv(m0, gate_ps, conv_g, 0, "f_gate_")
                split_w(m0 + 1, wg_raw, wg_hi, wg_lo, s["f_wg_hi"], s["f_wg_lo"])
                gated_part(m0, 0)
                split_w(m0 + 1, wu_raw, wu_hi, wu_lo, s["f_wu_hi"], s["f_wu_lo"])
                with dve.Fori(1, NC_FF - 1) as c:
                    m = hf * NC_FF + c
                    add_down(m - 1, range(0, TPH // 2))
                    conv(m, gate_ps, conv_g, c, "f_gate_")
                    split_w(m + 1, wg_raw, wg_hi, wg_lo, s["f_wg_hi"], s["f_wg_lo"])
                    add_down(m - 1, range(TPH // 2, TPH))
                    gated_part(m, c)
                    split_w(m + 1, wu_raw, wu_hi, wu_lo, s["f_wu_hi"], s["f_wu_lo"])
                c, m = NC_FF - 1, hf * NC_FF + (NC_FF - 1)
                add_down(m - 1, range(0, TPH // 2))
                conv(m, gate_ps, conv_g, c, "f_gate_")
                add_down(m - 1, range(TPH // 2, TPH))
                gated_part(m, c)
                add_down(m, range(TPH))

                with dve.Fori(0, TPH // 2) as i:
                    for u in range(2):
                        n = hf * TPH + i * 2 + u
                        tile = y[:, bass.ds(i * 2 + u, 1), :].rearrange("p o d -> p (o d)")
                        mean_square(n, tile, "n_", (s_ad[TPH - 1], after(hf * NC_FF + (NC_FF - 1))))
                        dve.wait_ge(s["n_rstd"], after(n))
                        dve.wait_ge(s_out[u], 16 * after(hf * (TPH // 2) + i - 1))
                        dve.scalar_tensor_tensor(out=fin[u][:], in0=tile, scalar=rstd[:, 0:1], in1=fnorm[:],
                                                 op0=ALU.mult, op1=ALU.mult).then_inc(s["n_out"], 1)


def program(nc, t_in, out):
    mix_scratch = nc.dram_tensor("mix_scratch", (NT, P, KD, P), F32).ap()
    mixer_phase(nc, t_in, mix_scratch)
    ffn_phase(nc, t_in, mix_scratch, out)


_INS = ['x', 'positions', 'norm1_w', 'w_in', 'gla_gk_w2', 'gla_gk_b', 'gla_norm_w', 'swa_sinks', 'w_out',
        'norm2_w', 'w_up', 'conv_w', 'conv_b', 'w_down', 'final_norm_w']


def _constants():
    j, i = np.meshgrid(np.arange(P), np.arange(P), indexing="ij")
    masks = [((j // (2 * w) == i // (2 * w)) & (j % (2 * w) < w) & (i % (2 * w) >= w)) for w in SPANS[2:]]
    masks.append(i == j)
    swa = np.zeros((P, P), np.float32)
    swa[0:CHUNK, 0:CHUNK] = NEG
    inv = np.float32(THETA) ** (-np.arange(RH, dtype=np.float32) / np.float32(RH))
    return {"c_ident": np.eye(P, dtype=np.float32),
            "c_masks": np.ascontiguousarray(np.stack(masks, 1).astype(np.float32).reshape(P, -1)),
            "c_swa_mask": swa,
            "c_inv_freq": np.ascontiguousarray(np.broadcast_to(inv.astype(np.float32), (P, RH)))}


def kernel(**inputs):
    import concourse.bacc as _bacc
    from concourse.bass_utils import run_bass_kernel_spmd as _run

    nc = _bacc.Bacc("TRN2", target_bir_lowering=False, num_devices=1)
    arrays, t_in = {}, {}
    for name, a in [(n, np.ascontiguousarray(inputs[n])) for n in _INS] + list(_constants().items()):
        arrays[f"in_{name}"] = a
        t_in[name] = nc.dram_tensor(f"in_{name}", a.shape, mybir.dt.from_np(a.dtype), kind="ExternalInput").ap()
    out = nc.dram_tensor("out_dram", (1, S, D), F32, kind="ExternalOutput").ap()
    program(nc, t_in, out)
    r = _run(nc, [arrays], core_ids=[0])
    return r.results[0]["out_dram"]
```

```python
from contextlib import ExitStack

import numpy as np

import concourse.bass as bass
from concourse import mybir

P = 128
D = 1024
KD = D // P
S = 2048
NT = S // P
GH, DK, DV, RANK = 4, 64, 128, 16
QK, GV = GH * DK, GH * DV
SH, KVH, HD = 8, 2, 64
GRP = SH // KVH
SQ, SKV = SH * HD, KVH * HD
DMIX = GV + SQ
D_IN = 2 * QK + 2 * GV + RANK + SQ + 2 * SKV
O_QK, O_V, O_R, O_LOW = 0, 2 * QK, 2 * QK + GV, 2 * QK + 2 * GV
O_SQ = O_LOW + RANK
O_SK = O_SQ + SQ
CHUNK = 64
ROPE = HD // 4
RH = ROPE // 2
THETA = 500000.0
EPS = 1e-6
GATE_NORM = 16.0
FF = 2816
NC_FF = FF // P
HALVES = 2
TPH = NT // HALVES
TOK = S // HALVES
SPANS = [64, 32, 16, 8, 4, 2, 1]
NL = len(SPANS)
FIRST_SPANS = 4
SPAN_PARTS = [(0, FIRST_SPANS), (FIRST_SPANS, NL)]
NEG = -1.0e30
TWO_PI = 6.283185307179586
TP_A = 6.28125
TP_B = float(np.float32(int((TWO_PI - TP_A) * 2 ** 21) / 2.0 ** 21))
TP_C = TWO_PI - TP_A - TP_B
ROUNDER = 12582912.0
PI_IN = 3.1415925

F32 = mybir.dt.float32
F32R = mybir.dt.float32r
I32 = mybir.dt.int32
U8 = mybir.dt.uint8
ALU = mybir.AluOpType
ACT = mybir.ActivationFunctionType
AX_X = mybir.AxisListType.X

GROUPS = ["qk", "sq", "small", "v", "r"]
PIECES = {"qk": [(O_QK, 2 * QK)], "sq": [(O_SQ, SQ)], "small": [(O_LOW, RANK), (O_SK, 2 * SKV)],
          "v": [(O_V, GV)], "r": [(O_R, GV)]}
WIDTH = {g: sum(w for _, w in PIECES[g]) for g in GROUPS}
FIRST = {g: sum(WIDTH[f] for f in GROUPS[:i]) for i, g in enumerate(GROUPS)}


PRIME = 2


def after(n):
    return n + (1 + PRIME)


def mixer_phase(nc, t_in, mix_scratch, ffn):
    all_sems = []
    with ExitStack() as ctx:
        def sb(name, shape, dt=F32):
            return ctx.enter_context(nc.sbuf_tensor(name, shape, dt))

        def ps(name, cols):
            return ctx.enter_context(nc.psum_tensor(name, [P, cols], F32))

        def sem(name):
            all_sems.append(nc.alloc_semaphore(name=name))
            return all_sems[-1]

        w_hi = sb("w_in_hi", [P, KD, D_IN], F32R)
        w_lo = sb("w_in_lo", [P, KD, D_IN], F32R)
        x = sb("x_tile", [P, D])
        h_hi = sb("h_hi", [P, KD, P], F32R)
        h_lo = sb("h_lo", [P, KD, P], F32R)
        z_qk = sb("z_qk", [P, 2 * QK])
        z_v = sb("z_v", [P, GV])
        z_r = sb("z_r", [P, GV])
        z_low = sb("z_low", [P, RANK])
        z_sqk = sb("z_sqk", [P, GRP + 1, KVH, HD])
        z_sv = sb("z_sv", [P, SKV])
        ident = sb("ident", [P, P])
        masks = sb("level_masks", [P, NL - 1, P], U8)
        swa_mask = sb("swa_mask", [P, P])
        norm1 = sb("norm1_col", [P, KD])
        w2 = sb("gk_w2", [RANK, QK])
        gkb = sb("gk_b_col", [P, 2])
        sinks = sb("sinks_row", [P, SH])
        nsinks = sb("minus_sinks", [P, SH])
        invf = sb("inv_freq", [P, RH])
        pos_i = sb("pos_i", [P, NT], I32)
        pos_f = sb("pos_f", [P, NT])
        cosT = sb("cosT", [P, NT, RH])
        sinT = sb("sinT", [P, NT, RH])
        nhalf = sb("minus_half", [P, GH])
        stats = sb("bn_stats", [P, 2, 6])
        mv = sb("mean_var", [P, 2])
        ms = sb("mean_square", [P, 1])
        rstd = sb("rstd", [P, 1])
        qkT = sb("qkT", [P, 4, P])
        kwin = sb("k_window", [P, CHUNK + P])
        v_cur = sb("v_cur", [P, SKV])
        v_mid = sb("v_mid", [P, SKV])
        lowT = sb("lowT", [RANK, P])
        gate_a = sb("gate_pre", [P, 2 * P])
        gate_l = sb("gate_log", [P, 2 * P])
        gate_m = sb("gate_min", [P, 2 * P])
        B = sb("gate_cumsum", [P, 2 * P])
        Eb = sb("exp_b", [P, 2 * P])
        kd, kdN, qb = gate_m, gate_a, gate_l
        ks = sb("k_level", [P, NL, 2 * P])
        qs = sb("q_level", [P, NL, 2 * P])
        sqT = qs[:, NL - 2:NL, :].rearrange("p l (b n) -> p (l b) n", b=2)
        pT = sb("intra_scores", [P, 2, 2, P])
        state = sb("state", [P, 2, DV])
        prob = sb("prob", [P, SH, P])
        negm = sb("minus_max", [P, SH])
        den = sb("denominator", [P, SH])
        esink = sb("exp_sink", [P, SH])
        rden = sb("recip_denominator", [P, SH])
        probT = sb("probT", [P, SH, P])
        gate = sb("out_gate", [P, GV])
        ossq = sb("o_ssq", [P, GH])
        orstd = sb("o_rstd", [P, GH])
        mix = prob[:].rearrange("p h k -> p (h k)")
        mixT = probT
        rope_heads = (GRP + 1) * KVH
        rope_room = probT[:].rearrange("p h n -> p (h n)")
        ropeA = rope_room[:, 0:rope_heads * ROPE].rearrange("p (h r) -> p h r", h=rope_heads)
        ropeB = rope_room[:, 512:512 + rope_heads * ROPE].rearrange("p (h r) -> p h r", h=rope_heads)

        squares = ks[:, 0:2, :].rearrange("p l (b n) -> p (l b) n", b=2)
        ang = rope_room[:, 0:NT * RH].rearrange("p (t r) -> p t r", t=NT)

        pj = [ps("proj0", 512), ps("proj1", 512)]
        tr = ps("turn", 1024)
        sc = ps("score", 1024)
        ob = ps("outb", 1024)
        gk_ps = sc[:, 1024 - 2 * P:1024]
        gla_out = [ob[:, 0:2 * DV], sc[:, 512:512 + 2 * DV]]

        owned = {
            "pe": """xT zT sT_k sT_low gk swa_s swa_pT swa_o kdT gla_o gla_up mixT_done""",
            "act": """x_norm hT_hi e_qk e_sq e_small_low e_small_k e_sv e_v e_r r_exp vmid_lo v_copy vmid_hi
                ev_kshift ev_k ev_low ev_qkT ev_pT ev_kd ev_mixT g_abs g_exp g_log g_eb g_kexp lv_exp0 lv_exp1
                swa_exp swa_sinke o_ssq""",
            "pool": """x_rstd o_rstd""",
            "dve": """x_stats x_ms x_sum x_eps hT_lo rope_mul rope_a rope_b ev_sqT g_pre g_min g_sum g_scan g_kdiff
                g_kd g_qb lv_diff0 lv_diff1 lv_k0 lv_k1 lv_qk0 lv_qk1 swa_masked swa_max swa_neg swa_sinkd swa_den swa_rden swa_mix
                st_scaled st_new o_eps o_scaled o_mix r_one r_rec r_gate""",
        }
        s = {n: sem("a_" + n) for names in owned.values() for n in names.split()}
        s_g = {g: sem("a_proj_" + g) for g in GROUPS}
        s_lv = [sem(f"a_lvl{i}") for i in range(NL + 1)]
        s_mg = [sem(f"a_merge{i}") for i in range(NL + 1)]
        stepped = {who: [s[n] for n in names.split()] for who, names in owned.items()}
        stepped["pe"] += [*s_g.values(), *s_lv]
        stepped["dve"] += s_mg
        for n in ("norm1_load", "w_split_hi", "w_split_lo", "dve_setup", "const_ready", "pool_setup", "rope_tab", "rope_act"):
            s[n] = sem("a_" + n)
        NSTAGE = 6
        s_w = [sem(f"a_w_load{i}") for i in range(NSTAGE)]
        s_const = sem("a_const_load")
        s_ffn, s_onorm = sem("a_ffn_const_load"), sem("a_gla_norm_load")
        s_wo = [sem(f"a_w_out_load{k}") for k in range(KD)]
        s_wo_hi, s_wo_lo = sem("a_w_out_hi"), sem("a_w_out_lo")
        s_x = sem("a_x_load")
        s_out = sem("a_mix_store")

        block = ctx.enter_context(nc.Block())

        def prime(eng, who):
            for one in stepped[who]:
                eng.sem_inc(one, PRIME)
        stage_room = [ks[:].rearrange("p l n -> p (l n)"), qs[:].rearrange("p l n -> p (l n)")]
        stage = [stage_room[i // 3][:, (i % 3) * 512:(i % 3 + 1) * 512] for i in range(NSTAGE)]
        pieces = [(g, k) for g in GROUPS for k in range(KD)]

        def loads_of(g):
            return len(PIECES[g])

        def loaded(n):
            return 16 * sum(loads_of(pieces[m][0]) for m in range(n % NSTAGE, n + 1, NSTAGE))

        def last_of_group_evac(g):
            return {"qk": "e_qk", "sq": "e_sq", "small": "e_sv", "v": "e_v", "r": "r_exp"}[g]

        def plain(eng):
            eng.wait_ge(s["const_ready"], 1)

        @block.sync
        def _(sp):
            sp.sem_inc(s_out, 16 * PRIME)
            sp.sem_inc(s_x, 16 * PRIME)
            sp.dma_start(norm1[:], t_in["norm1_w"][0].rearrange("(k p) -> p k", p=P),
                         allow_slow_non_contiguous=True).then_inc(s["norm1_load"], 16)
            sp.dma_start(x[:], t_in["x"][0, 0:P, :]).then_inc(s_x, 16)
            for n, (g, k) in enumerate(pieces):
                if n >= NSTAGE:
                    sp.wait_ge(s["w_split_lo"], n - NSTAGE + 1)
                at = 0
                for c0, w in PIECES[g]:
                    sp.dma_start(stage[n % NSTAGE][:, at:at + w], t_in["w_in"][0, k * P:(k + 1) * P, c0:c0 + w]
                                 ).then_inc(s_w[n % NSTAGE], 16)
                    at += w

            def load_x(n):
                sp.wait_ge(s["xT"], after(n - 1))
                sp.dma_start(x[:], t_in["x"][0, bass.ds(n * P, P), :]).then_inc(s_x, 16)

            def store_mix(t):
                sp.wait_ge(s["ev_mixT"], after(t))
                sp.dma_start(mix_scratch[bass.ds(t, 1)].rearrange("o p k n -> (o p) k n"), mixT[:]).then_inc(s_out, 16)

            load_x(1)
            with sp.Fori(0, NT - 2) as t:
                load_x(t + 2)
                store_mix(t)
            sp.wait_ge(s_g["r"], after(NT - 1))
            sp.dma_start(ffn["onorm"][:], t_in["gla_norm_w"][0].rearrange("(p a) -> p a", a=1)).then_inc(s_onorm, 16)
            for k in range(KD):
                sp.dma_start(ffn["wo_raw"][k], t_in["w_out"][0, k * P:(k + 1) * P, :]).then_inc(s_wo[k], 16)
            store_mix(NT - 2)
            sp.dma_start(ffn["mixt"][:], mix_scratch[0]).then_inc(s_ffn, 16)
            sp.dma_start(ffn["xt"][:], t_in["x"][0, 0:P, :]).then_inc(s_ffn, 16)
            for dst, src in ((ffn["ident"][:], t_in["c_ident"]),
                             (ffn["norm2"][:], t_in["norm2_w"][0].rearrange("(k p) -> p k", p=P)),
                             (ffn["fnorm"][:], t_in["final_norm_w"].partition_broadcast(P)),
                             (ffn["cw"][:], t_in["conv_w"][0].rearrange("i (c p) -> p i c", p=P)),
                             (ffn["cb"][:], t_in["conv_b"][0].rearrange("(c p) -> p c", p=P))):
                sp.dma_start(dst, src, allow_slow_non_contiguous=True).then_inc(s_ffn, 16)
            store_mix(NT - 1)
            sp.wait_ge(s_ffn, 16 * 7)
            sp.wait_ge(s_out, 16 * after(NT - 1))

        @block.tensor
        def _(pe):
            prime(pe, "pe")

            def turn_x(n):
                pe.wait_ge(s["x_norm"], after(n))
                pe.wait_ge(s["swa_mix"], after(n - 2))
                pe.wait_ge(s["o_scaled"], after(n - 2))
                pe.wait_ge(s["hT_lo"], after(n - 1))
                for k in range(KD):
                    last = pe.transpose(ob[:, k * P:(k + 1) * P], x[:, k * P:(k + 1) * P], ident[:])
                last.then_inc(s["xT"], 1)

            def project(n, g):
                i = GROUPS.index(g)
                if i == 0:
                    pe.wait_ge(s["hT_lo"], after(n))
                free = GROUPS[i - 2] if i >= 2 else GROUPS[4 - i]
                pe.wait_ge(s[last_of_group_evac(free)], after(n if i >= 2 else n - 1))
                out = pj[i % 2][:, 0:WIDTH[g]]
                cols = slice(FIRST[g], FIRST[g] + WIDTH[g])
                for k in range(KD):
                    pe.matmul(out, h_hi[:, k, :], w_hi[:, k, cols], start=(k == 0), stop=False)
                    pe.matmul(out, h_hi[:, k, :], w_lo[:, k, cols], start=False, stop=False)
                    last = pe.matmul(out, h_lo[:, k, :], w_hi[:, k, cols], start=False, stop=(k == KD - 1))
                last.then_inc(s_g[g], 1)

            def level(t, l):
                bank = ob if l % 2 == 0 else sc
                if l == 0:
                    pe.wait_ge(s["lv_qk0"], after(t))
                elif l == 1:
                    pe.wait_ge(s["swa_masked"], after(t))
                else:
                    pe.wait_ge(s_mg[l - 2], after(t))
                if l == FIRST_SPANS:
                    pe.wait_ge(s["lv_qk1"], after(t))
                for pair in range(2):
                    for par in range(2):
                        rows = slice(par * DK, (par + 1) * DK)
                        if l < NL:
                            lhs, rhs = ks[rows, l, pair * P:(pair + 1) * P], qs[rows, l, pair * P:(pair + 1) * P]
                        else:
                            lhs, rhs = qkT[rows, 2 + pair, :], qkT[rows, pair, :]
                        at = par * 512 + pair * P
                        last = pe.matmul(bank[:, at:at + P], lhs, rhs, start=True, stop=True)
                last.then_inc(s_lv[l], 1)

            def attend(t, more):
                pe.wait_ge(s["e_qk"], after(t))
                pe.wait_ge(s["rope_b"], after(t))
                pe.wait_ge(s["rope_a"], after(t))
                pe.wait_ge(s["e_small_low"], after(t))
                pe.wait_ge(s["ev_mixT"], after(t - 1))
                for b in range(4):
                    pe.transpose(tr[:, b * P:(b + 1) * P], z_qk[:, b * P:(b + 1) * P], ident[:])
                for b in range(GRP):
                    last = pe.transpose(tr[:, 512 + b * P:512 + (b + 1) * P], z_sqk[:, b, :, :], ident[:])
                last.then_inc(s["zT"], 1)
                pe.wait_ge(s["st_new"], after(t - 1))
                pe.wait_ge(s["o_scaled"], after(t - 1))
                pe.transpose(sc[:, 0:P], z_sqk[:, GRP, :, :], ident[:]).then_inc(s["sT_k"], 1)
                pe.transpose(sc[0:RANK, 512:512 + P], z_low[:], ident[:]).then_inc(s["sT_low"], 1)
                pe.wait_ge(s["ev_low"], after(t))
                for pair in range(2):
                    last = pe.matmul(gk_ps[:, pair * P:(pair + 1) * P], w2[:, pair * P:(pair + 1) * P], lowT[:],
                                     start=True, stop=True)
                last.then_inc(s["gk"], 1)
                if more:
                    project(t + 1, "qk")
                plain(pe)
                pe.wait_ge(s["ev_k"], after(t))
                pe.wait_ge(s["ev_sqT"], after(t))
                pe.wait_ge(s["g_pre"], after(t))
                for b in range(GRP):
                    for g in range(KVH):
                        rows = slice(g * HD, (g + 1) * HD)
                        for c in range(2):
                            last = pe.matmul(
                                sc[c * CHUNK:(c + 1) * CHUNK, g * 512 + b * P:g * 512 + (b + 1) * P],
                                sqT[rows, b, c * CHUNK:(c + 1) * CHUNK], kwin[rows, c * CHUNK:c * CHUNK + P],
                                start=True, stop=True)
                last.then_inc(s["swa_s"], 1)
                if more:
                    project(t + 1, "sq")
                    project(t + 1, "small")
                pe.wait_ge(s["swa_exp"], after(t))
                pe.wait_ge(s["ev_qkT"], after(t))
                for h in range(SH):
                    last = pe.transpose(tr[:, h * P:(h + 1) * P], prob[:, h, :], ident[:])
                last.then_inc(s["swa_pT"], 1)
                for l in range(NL + 1):
                    level(t, l)
                pe.wait_ge(s["g_kd"], after(t))
                pe.wait_ge(s["ev_pT"], after(t))
                for pair in range(2):
                    last = pe.transpose(tr[:, pair * P:(pair + 1) * P], kd[:, pair * P:(pair + 1) * P], ident[:])
                last.then_inc(s["kdT"], 1)
                pe.wait_ge(s["vmid_hi"], after(t))
                pe.wait_ge(s_mg[NL - 1], after(t))
                for h in range(SH):
                    g = h // GRP
                    for c, vals in ((0, v_mid), (1, v_cur)):
                        last = pe.matmul(ob[c * CHUNK:(c + 1) * CHUNK, 512 + h * HD:512 + (h + 1) * HD],
                                         probT[:, h, c * CHUNK:(c + 1) * CHUNK], vals[:, g * HD:(g + 1) * HD],
                                         start=True, stop=True)
                last.then_inc(s["swa_o"], 1)
                if more:
                    project(t + 1, "v")
                pe.wait_ge(s["g_qb"], after(t))
                pe.wait_ge(s_mg[NL], after(t))
                pe.wait_ge(s["st_new"], after(t - 1))
                pe.wait_ge(s["e_v"], after(t))
                for h in range(GH):
                    pair, par = h // 2, h % 2
                    rows = slice(par * DK, (par + 1) * DK)
                    pe.matmul(gla_out[par][:, pair * DV:(pair + 1) * DV], qb[rows, pair * P:(pair + 1) * P],
                              state[rows, pair, :], start=True, stop=False)
                    last = pe.matmul(gla_out[par][:, pair * DV:(pair + 1) * DV], pT[:, par, pair, :],
                                     z_v[:, h * DV:(h + 1) * DV], start=False, stop=True)
                last.then_inc(s["gla_o"], 1)
                pe.wait_ge(s["ev_kd"], after(t))
                for h in range(GH):
                    pair, par = h // 2, h % 2
                    last = pe.matmul(sc[par * DK:(par + 1) * DK, pair * DV:(pair + 1) * DV],
                                     kdN[:, h * DK:(h + 1) * DK], z_v[:, h * DV:(h + 1) * DV], start=True, stop=True)
                last.then_inc(s["gla_up"], 1)
                if more:
                    project(t + 1, "r")
                pe.wait_ge(s["o_mix"], after(t))
                pe.wait_ge(s["swa_mix"], after(t))
                pe.wait_ge(s["ev_kd"], after(t))
                for b in range(KD):
                    last = pe.transpose(tr[:, b * P:(b + 1) * P], mix[:, b * P:(b + 1) * P], ident[:])
                last.then_inc(s["mixT_done"], 1)

            pe.wait_ge(s["const_ready"], 1)
            turn_x(0)
            for i, g in enumerate(GROUPS):
                pe.wait_ge(s["w_split_lo"], (i + 1) * KD)
                project(0, g)
            turn_x(1)
            with pe.Fori(0, NT - 2) as t:
                attend(t, True)
                turn_x(t + 2)
            attend(NT - 2, True)
            attend(NT - 1, False)

        @block.scalar
        def _(act):
            prime(act, "act")

            def norm_x(n):
                act.wait_ge(s["x_rstd"], after(n))
                act.activation(x[:], x[:], ACT.Copy, scale=rstd[:, 0:1]).then_inc(s["x_norm"], 1)

            def split_h(n):
                act.wait_ge(s["xT"], after(n))
                act.wait_ge(s_g["r"], after(n - 1))
                act.activation(h_hi[:].rearrange("p k n -> p (k n)"), ob[:], ACT.Copy).then_inc(s["hT_hi"], 1)

            def evac(n, g):
                act.wait_ge(s_g[g], after(n))
                bank = pj[GROUPS.index(g) % 2]
                if g == "qk":
                    act.wait_ge(s["zT"], after(n - 1))
                    act.activation(z_qk[:], bank[:], ACT.Copy).then_inc(s["e_qk"], 1)
                elif g == "sq":
                    act.wait_ge(s["zT"], after(n - 1))
                    act.activation(z_sqk[:, 0:GRP].rearrange("p b g d -> p g b d"),
                                   bank[:].rearrange("p (g b d) -> p g b d", g=KVH, b=GRP), ACT.Copy
                                   ).then_inc(s["e_sq"], 1)
                elif g == "small":
                    act.wait_ge(s["sT_low"], after(n - 1))
                    act.activation(z_low[:], bank[:, 0:RANK], ACT.Copy).then_inc(s["e_small_low"], 1)
                    act.activation(z_sqk[:, GRP].rearrange("p g d -> p (g d)"), bank[:, RANK:RANK + SKV], ACT.Copy
                                   ).then_inc(s["e_small_k"], 1)
                    act.wait_ge(s["v_copy"], after(n - 1))
                    act.activation(z_sv[:], bank[:, RANK + SKV:RANK + 2 * SKV], ACT.Copy).then_inc(s["e_sv"], 1)
                elif g == "v":
                    act.wait_ge(s["gla_up"], after(n - 1))
                    act.activation(z_v[:], bank[:], ACT.Copy).then_inc(s["e_v"], 1)
                else:
                    act.wait_ge(s["o_mix"], after(n - 1))
                    act.activation(z_r[:], bank[:], ACT.Copy).then_inc(s["e_r"], 1)
                    act.activation(gate[:], bank[:], ACT.Exp, scale=-1.0).then_inc(s["r_exp"], 1)

            for dst, src in ((ident[:], t_in["c_ident"]), (rope_room[:, 0:(NL - 1) * P], t_in["c_masks"]),
                             (swa_mask[:], t_in["c_swa_mask"]), (invf[:], t_in["c_inv_freq"]),
                             (w2[:], t_in["gla_gk_w2"][0]),
                             (gkb[:], t_in["gla_gk_b"][0].rearrange("(k p) -> p k", p=P)),
                             (sinks[:], t_in["swa_sinks"][0].partition_broadcast(P)),
                             (pos_i[:], t_in["positions"][0].rearrange("(t p) -> p t", p=P))):
                act.dma_start(dst, src, allow_slow_non_contiguous=True).then_inc(s_const, 16)
            act.wait_ge(s["norm1_load"], 16)
            for n, (g, k) in enumerate(pieces):
                act.wait_ge(s_w[n % NSTAGE], loaded(n))
                act.activation(w_hi[:, k, FIRST[g]:FIRST[g] + WIDTH[g]], stage[n % NSTAGE][:, 0:WIDTH[g]], ACT.Copy,
                               scale=norm1[:, k:k + 1]).then_inc(s["w_split_hi"], 1)
                if n == NSTAGE - 1:
                    norm_x(0)
                    split_h(0)
                if k == KD - 1 and n >= KD:
                    evac(0, GROUPS[n // KD - 1])
            act.wait_ge(s["rope_tab"], 1)
            act.activation(sinT[:], sinT[:], ACT.Sin)
            act.activation(cosT[:], cosT[:], ACT.Sin).then_inc(s["rope_act"], 1)
            evac(0, GROUPS[-1])
            norm_x(1)
            split_h(1)

            def attend(t, more, norm_next):
                act.wait_ge(s["swa_s"], after(t - 1))
                act.activation(kwin[:, 0:CHUNK], kwin[:, P:P + CHUNK], ACT.Copy).then_inc(s["ev_kshift"], 1)
                act.wait_ge(s["sT_low"], after(t))
                act.wait_ge(s["gk"], after(t - 1))
                act.activation(lowT[:], sc[0:RANK, 512:512 + P], ACT.Copy).then_inc(s["ev_low"], 1)
                act.wait_ge(s["ev_kshift"], after(t))
                act.activation(kwin[:, CHUNK:CHUNK + P], sc[:, 0:P], ACT.Copy).then_inc(s["ev_k"], 1)
                act.activation(qkT[:].rearrange("p b n -> p (b n)"), tr[:, 0:512], ACT.Copy).then_inc(s["ev_qkT"], 1)
                act.wait_ge(s["swa_o"], after(t - 1))
                act.activation(v_mid[0:CHUNK, :], v_cur[CHUNK:P, :], ACT.Copy).then_inc(s["vmid_lo"], 1)
                act.wait_ge(s["vmid_lo"], after(t))
                act.wait_ge(s["e_sv"], after(t))
                act.activation(v_cur[:], z_sv[:], ACT.Copy).then_inc(s["v_copy"], 1)
                act.activation(v_mid[CHUNK:P, :], z_sv[0:CHUNK, :], ACT.Copy).then_inc(s["vmid_hi"], 1)
                act.wait_ge(s["g_pre"], after(t))
                act.activation(gate_l[:], gate_a[:], ACT.Abs).then_inc(s["g_abs"], 1)
                act.wait_ge(s["g_abs"], after(t))
                act.activation(gate_l[:], gate_l[:], ACT.Exp, scale=-1.0).then_inc(s["g_exp"], 1)
                act.wait_ge(s["g_exp"], after(t))
                act.activation(gate_l[:], gate_l[:], ACT.Ln, bias=1.0).then_inc(s["g_log"], 1)
                act.wait_ge(s["g_scan"], after(t))
                act.activation(Eb[:], B[:], ACT.Exp, scale=1.0 / GATE_NORM).then_inc(s["g_eb"], 1)
                act.wait_ge(s["g_kdiff"], after(t))
                act.activation(kd[:], kd[:], ACT.Exp, scale=-1.0 / GATE_NORM).then_inc(s["g_kexp"], 1)
                for i, (l0, l1) in enumerate(SPAN_PARTS):
                    act.wait_ge(s[f"lv_diff{i}"], after(t))
                    if i == 1:
                        if more:
                            evac(t + 1, "qk")
                        act.wait_ge(s["swa_s"], after(t))
                    act.activation(qs[:, l0:l1], ks[:, l0:l1], ACT.Exp, scale=-1.0 / GATE_NORM
                                   ).then_inc(s[f"lv_exp{i}"], 1)
                act.wait_ge(s["swa_neg"], after(t))
                for h in range(SH):
                    last = act.activation(prob[:, h, :], prob[:, h, :], ACT.Exp, bias=negm[:, h:h + 1],
                                          scale=HD ** -0.5, accum_out=den[:, h:h + 1])
                last.then_inc(s["swa_exp"], 1)
                act.wait_ge(s["swa_sinkd"], after(t))
                act.activation(esink[:], esink[:], ACT.Exp).then_inc(s["swa_sinke"], 1)
                if more:
                    evac(t + 1, "sq")
                    evac(t + 1, "small")
                act.wait_ge(s["swa_pT"], after(t))
                act.wait_ge(s_out, after(t - 1) * 16)
                act.activation(probT[:].rearrange("p h n -> p (h n)"), tr[:], ACT.Copy).then_inc(s["ev_pT"], 1)
                if not more:
                    act.wait_ge(s_onorm, 16)
                    for k in range(KD):
                        act.wait_ge(s_wo[k], 16)
                        scale = ffn["onorm"][:, 0:1] if k < GV // P else 1.0
                        act.activation(ffn["wo"][k][:, 0, :], ffn["wo_raw"][k], ACT.Copy, scale=scale
                                       ).then_inc(s_wo_hi, 1)
                act.wait_ge(s["kdT"], after(t))
                act.wait_ge(s["gla_up"], after(t - 1))
                act.activation(kdN[:], tr[:, 0:2 * P], ACT.Copy).then_inc(s["ev_kd"], 1)
                if norm_next:
                    norm_x(t + 2)
                act.wait_ge(s["gla_o"], after(t))
                for h in range(GH):
                    last = act.activation(squares[:, h], gla_out[h % 2][:, (h // 2) * DV:(h // 2 + 1) * DV],
                                          ACT.Square, scale=DK ** -0.5, accum_out=ossq[:, h:h + 1])
                last.then_inc(s["o_ssq"], 1)
                if more:
                    evac(t + 1, "v")
                    evac(t + 1, "r")
                act.wait_ge(s["mixT_done"], after(t))
                act.activation(mixT[:].rearrange("p h n -> p (h n)"), tr[:], ACT.Copy).then_inc(s["ev_mixT"], 1)

            with act.Fori(0, NT - 2) as t:
                attend(t, True, True)
                split_h(t + 2)
            attend(NT - 2, True, False)
            attend(NT - 1, False, False)

        @block.gpsimd
        def _(pool):
            prime(pool, "pool")

            pool.memset(nhalf[:], -0.5).then_inc(s["pool_setup"], 1)
            pool.wait_ge(s["pool_setup"], 1)

            def x_rstd(n):
                pool.wait_ge(s["x_eps"], after(n))
                pool.tensor_tensor(rstd[:], ms[:], nhalf[:, 0:1], ALU.pow).then_inc(s["x_rstd"], 1)

            def attend(t):
                pool.wait_ge(s["o_eps"], after(t))
                pool.tensor_tensor(orstd[:], ossq[:], nhalf[:], ALU.pow).then_inc(s["o_rstd"], 1)

            x_rstd(0)
            x_rstd(1)
            with pool.Fori(0, NT - 2) as t:
                x_rstd(t + 2)
                attend(t)
            attend(NT - 2)
            attend(NT - 1)

        @block.vector
        def _(dve):
            prime(dve, "dve")

            steps = [0]

            def then(ins):
                steps[0] += 1
                ins.then_inc(s["dve_setup"], 1)
                dve.wait_ge(s["dve_setup"], steps[0])

            def norm_x(n):
                dve.wait_ge(s_x, after(n) * 16)
                dve.bn_stats(stats[:, 0, :], x[:, 0:512])
                dve.bn_stats(stats[:, 1, :], x[:, 512:1024]).then_inc(s["x_stats"], 1)
                plain(dve)
                dve.wait_ge(s["x_stats"], after(n))
                dve.bn_aggr(mv[:], stats[:].rearrange("p a b -> p (a b)")).then_inc(s["x_ms"], 1)
                dve.wait_ge(s["x_ms"], after(n))
                dve.scalar_tensor_tensor(out=ms[:], in0=mv[:, 0:1], scalar=mv[:, 0:1], in1=mv[:, 1:2],
                                         op0=ALU.mult, op1=ALU.add).then_inc(s["x_sum"], 1)
                dve.wait_ge(s["x_sum"], after(n))
                dve.tensor_scalar(ms[:], ms[:], EPS, None, ALU.add).then_inc(s["x_eps"], 1)

            def split_h(n):
                dve.wait_ge(s["hT_hi"], after(n))
                dve.tensor_tensor(h_lo[:].rearrange("p k n -> p (k n)"), ob[:],
                                  h_hi[:].rearrange("p k n -> p (k n)").bitcast(F32), ALU.subtract
                                  ).then_inc(s["hT_lo"], 1)

            def rope(n):
                heads = z_sqk[:].rearrange("p b g d -> p (b g) d")[:, :, 0:ROPE]
                halves = heads.rearrange("p h (a r) -> p h a r", a=2)
                nh = (GRP + 1) * KVH
                dve.wait_ge(s["e_sq"], after(n))
                dve.wait_ge(s["e_small_k"], after(n))
                ra = ropeA.rearrange("p h (a r) -> p h a r", a=2)
                rb = ropeB.rearrange("p h (a r) -> p h a r", a=2)
                for a in range(2):
                    c = cosT[:, bass.ds(n, 1), :].to_broadcast([P, nh, RH])
                    sn = sinT[:, bass.ds(n, 1), :].to_broadcast([P, nh, RH])
                    dve.tensor_tensor(ra[:, :, a, :], halves[:, :, a, :], c, ALU.mult)
                    last = dve.tensor_tensor(rb[:, :, a, :], halves[:, :, a, :], sn, ALU.mult)
                last.then_inc(s["rope_mul"], 1)
                dve.wait_ge(s["rope_mul"], after(n))
                dve.tensor_tensor(halves[:, :, 0, :], ra[:, :, 0, :], rb[:, :, 1, :], ALU.subtract
                                  ).then_inc(s["rope_a"], 1)
                dve.tensor_tensor(halves[:, :, 1, :], ra[:, :, 1, :], rb[:, :, 0, :], ALU.add
                                  ).then_inc(s["rope_b"], 1)

            def split_w_out(k):
                dve.wait_ge(s_wo_hi, k + 1)
                hi, lo = ffn["wo"][k][:, 0, :].bitcast(F32), ffn["wo"][k][:, 1, :]
                if k < GV // P:
                    dve.scalar_tensor_tensor(out=lo, in0=ffn["wo_raw"][k], scalar=ffn["onorm"][:, 0:1], in1=hi,
                                             op0=ALU.mult, op1=ALU.subtract).then_inc(s_wo_lo, 1)
                else:
                    dve.tensor_tensor(lo, ffn["wo_raw"][k], hi, ALU.subtract).then_inc(s_wo_lo, 1)

            def gate_r(n):
                dve.wait_ge(s["r_exp"], after(n))
                dve.tensor_scalar(gate[:], gate[:], 1.0, None, ALU.add).then_inc(s["r_one"], 1)
                dve.wait_ge(s["r_one"], after(n))
                dve.reciprocal(gate[:], gate[:]).then_inc(s["r_rec"], 1)
                dve.wait_ge(s["r_rec"], after(n))
                dve.tensor_tensor(gate[:], gate[:], z_r[:], ALU.mult).then_inc(s["r_gate"], 1)

            dve.memset(state[:], 0.0)
            dve.memset(pT[:], 0.0)
            dve.memset(kwin[:], 0.0)
            dve.memset(v_cur[:], 0.0)
            dve.wait_ge(s_const, 16 * 8)
            then(dve.tensor_scalar(nsinks[:], sinks[:], -1.0, None, ALU.mult))
            then(dve.tensor_copy(masks[:].rearrange("p l n -> p (l n)"), rope_room[:, 0:(NL - 1) * P]))
            dve.memset(v_mid[:], 0.0).then_inc(s["const_ready"], 1)
            norm_x(0)
            then(dve.tensor_copy(pos_f[:], pos_i[:]))
            then(dve.tensor_tensor(ang, pos_f[:].unsqueeze(2).to_broadcast([P, NT, RH]),
                                   invf[:].unsqueeze(1).to_broadcast([P, NT, RH]), ALU.mult))
            then(dve.tensor_scalar(cosT[:], ang, 1.0 / TWO_PI, ROUNDER, ALU.mult, ALU.add))
            then(dve.tensor_scalar(cosT[:], cosT[:], -ROUNDER, None, ALU.add))
            for part in (TP_A, TP_B, TP_C):
                then(dve.scalar_tensor_tensor(out=ang, in0=cosT[:], scalar=-part, in1=ang,
                                              op0=ALU.mult, op1=ALU.add))
            then(dve.tensor_scalar(sinT[:], ang, PI_IN, -PI_IN, ALU.min, ALU.max))
            then(dve.tensor_scalar(ang, ang, TWO_PI / 4, None, ALU.add))
            then(dve.tensor_scalar(cosT[:], ang, TWO_PI / 2, -TWO_PI, ALU.is_gt, ALU.mult))
            then(dve.tensor_tensor(cosT[:], cosT[:], ang, ALU.add))
            dve.tensor_scalar(cosT[:], cosT[:], PI_IN, -PI_IN, ALU.min, ALU.max).then_inc(s["rope_tab"], 1)
            for n, (g, k) in enumerate(pieces):
                dve.wait_ge(s["w_split_hi"], n + 1)
                cols = slice(FIRST[g], FIRST[g] + WIDTH[g])
                dve.scalar_tensor_tensor(out=w_lo[:, k, cols], in0=stage[n % NSTAGE][:, 0:WIDTH[g]],
                                         scalar=norm1[:, k:k + 1], in1=w_hi[:, k, cols].bitcast(F32),
                                         op0=ALU.mult, op1=ALU.subtract).then_inc(s["w_split_lo"], 1)
                if n == NSTAGE - 1:
                    split_h(0)
            norm_x(1)
            dve.wait_ge(s["rope_act"], 1)
            rope(0)
            split_h(1)

            def attend(t, more, norm_next):
                dve.wait_ge(s["zT"], after(t))
                dve.tensor_copy(sqT.rearrange("p b n -> p (b n)"), tr[:, 512:1024]).then_inc(s["ev_sqT"], 1)
                dve.wait_ge(s["gk"], after(t))
                dve.tensor_scalar(gate_a[:, 0:P], gk_ps[:, 0:P], gkb[:, 0:1], None, ALU.add)
                dve.tensor_scalar(gate_a[:, P:2 * P], gk_ps[:, P:2 * P], gkb[:, 1:2], None, ALU.add
                                  ).then_inc(s["g_pre"], 1)
                dve.wait_ge(s["g_pre"], after(t))
                dve.wait_ge(s["o_ssq"], after(t - 1))
                dve.tensor_scalar(gate_m[:], gate_a[:], 0.0, None, ALU.min).then_inc(s["g_min"], 1)
                dve.wait_ge(s["g_log"], after(t))
                dve.wait_ge(s["g_min"], after(t))
                dve.tensor_tensor(gate_m[:], gate_m[:], gate_l[:], ALU.subtract).then_inc(s["g_sum"], 1)
                dve.wait_ge(s["g_sum"], after(t))
                for pair in range(2):
                    cols = slice(pair * P, (pair + 1) * P)
                    last = dve.tensor_tensor_scan(B[:, cols], gate_m[:, cols], gate_m[:, cols], 0.0,
                                                  ALU.add, ALU.bypass)
                last.then_inc(s["g_scan"], 1)
                dve.wait_ge(s["g_scan"], after(t))
                dve.wait_ge(s["kdT"], after(t - 1))
                for pair in range(2):
                    cols = slice(pair * P, (pair + 1) * P)
                    last = dve.tensor_scalar(kd[:, cols], B[:, cols], B[:, (pair + 1) * P - 1:(pair + 1) * P],
                                             None, ALU.subtract)
                last.then_inc(s["g_kdiff"], 1)
                dve.wait_ge(s_lv[NL - 1], after(t - 1))
                for i, (l0, l1) in enumerate(SPAN_PARTS):
                    for l in range(l0, l1):
                        span = SPANS[l]
                        b4 = B[:].rearrange("p (n a w) -> p n a w", a=2, w=span)
                        d4 = ks[:, l, :].rearrange("p (n a w) -> p n a w", a=2, w=span)
                        ref = b4[:, :, 0, span - 1:span].to_broadcast([P, P // span, span])
                        dve.tensor_tensor(d4[:, :, 0, :], b4[:, :, 0, :], ref, ALU.subtract)
                        last = dve.tensor_tensor(d4[:, :, 1, :], ref, b4[:, :, 1, :], ALU.subtract)
                    last.then_inc(s[f"lv_diff{i}"], 1)
                dve.wait_ge(s["ev_qkT"], after(t))

                def level_operands(i):
                    l0, l1 = SPAN_PARTS[i]
                    dve.wait_ge(s[f"lv_exp{i}"], after(t))
                    dve.tensor_tensor(ks[:, l0:l1], qkT[:, 2:4, :].rearrange("p b n -> p (b n)").unsqueeze(1)
                                      .to_broadcast([P, l1 - l0, 2 * P]), qs[:, l0:l1], ALU.mult
                                      ).then_inc(s[f"lv_k{i}"], 1)
                    dve.wait_ge(s[f"lv_k{i}"], after(t))
                    dve.tensor_tensor(qs[:, l0:l1], qkT[:, 0:2, :].rearrange("p b n -> p (b n)").unsqueeze(1)
                                      .to_broadcast([P, l1 - l0, 2 * P]), qs[:, l0:l1], ALU.mult
                                      ).then_inc(s[f"lv_qk{i}"], 1)

                level_operands(0)
                dve.wait_ge(s["swa_s"], after(t))
                dve.wait_ge(s["mixT_done"], after(t - 1))
                dve.tensor_tensor(prob[:], sc[:].rearrange("p (h k) -> p h k", h=SH),
                                  swa_mask[:].unsqueeze(1).to_broadcast([P, SH, P]), ALU.add
                                  ).then_inc(s["swa_masked"], 1)
                dve.wait_ge(s["swa_masked"], after(t))
                dve.memset(swa_mask[:], 0.0)
                dve.tensor_reduce(negm[:], prob[:], AX_X, ALU.max).then_inc(s["swa_max"], 1)
                dve.wait_ge(s["swa_max"], after(t))
                dve.scalar_tensor_tensor(out=negm[:], in0=negm[:], scalar=-(HD ** -0.5), in1=nsinks[:],
                                         op0=ALU.mult, op1=ALU.min).then_inc(s["swa_neg"], 1)
                dve.wait_ge(s["swa_neg"], after(t))
                dve.tensor_tensor(esink[:], sinks[:], negm[:], ALU.add).then_inc(s["swa_sinkd"], 1)
                level_operands(1)
                dve.wait_ge(s["g_eb"], after(t))
                dve.wait_ge(s["gla_o"], after(t - 1))
                dve.tensor_tensor(qb[:], qkT[:, 0:2, :].rearrange("p b n -> p (b n)"), Eb[:], ALU.mult
                                  ).then_inc(s["g_qb"], 1)
                dve.wait_ge(s["g_kexp"], after(t))
                dve.tensor_tensor(kd[:], qkT[:, 2:4, :].rearrange("p b n -> p (b n)"), kd[:], ALU.mult
                                  ).then_inc(s["g_kd"], 1)
                dve.wait_ge(s["swa_exp"], after(t))
                dve.wait_ge(s["swa_sinke"], after(t))
                dve.tensor_tensor(den[:], den[:], esink[:], ALU.add).then_inc(s["swa_den"], 1)
                dve.wait_ge(s["swa_den"], after(t))
                dve.reciprocal(rden[:], den[:]).then_inc(s["swa_rden"], 1)
                if not more:
                    gate_r(t)
                dve.wait_ge(s["gla_o"], after(t - 1))
                for l in range(NL + 1):
                    bank = ob if l % 2 == 0 else sc
                    got = bank[:].rearrange("p (a c) -> p a c", a=2)[:, :, 0:2 * P].rearrange(
                        "p a (b n) -> p a b n", b=2)
                    plain(dve)
                    dve.wait_ge(s_lv[l], after(t))
                    if l < 2:
                        w = SPANS[l]
                        for b0 in range(0, P, 2 * w):
                            last = dve.tensor_copy(pT[b0:b0 + w, :, :, b0 + w:b0 + 2 * w],
                                                   got[b0:b0 + w, :, :, b0 + w:b0 + 2 * w])
                    else:
                        m = masks[:, l - 2, :].unsqueeze(1).unsqueeze(1).to_broadcast([P, 2, 2, P])
                        if l >= 2:
                            dve.wait_ge(s_mg[l - 1], after(t))
                        last = dve.copy_predicated(pT[:], m, got)
                    last.then_inc(s_mg[l], 1)
                    if not more:
                        split_w_out(l)
                dve.wait_ge(s["swa_o"], after(t))
                dve.wait_ge(s["swa_rden"], after(t))
                dve.tensor_tensor(mix[:, GV:DMIX].rearrange("p (h d) -> p h d", h=SH),
                                  ob[:, 512:1024].rearrange("p (h d) -> p h d", h=SH),
                                  rden[:].unsqueeze(2).to_broadcast([P, SH, HD]), ALU.mult
                                  ).then_inc(s["swa_mix"], 1)
                if more:
                    rope(t + 1)
                if norm_next:
                    norm_x(t + 2)
                if more:
                    gate_r(t)
                dve.wait_ge(s["gla_o"], after(t))
                for pair in range(2):
                    last = dve.tensor_scalar(state[:, pair, :], state[:, pair, :],
                                             Eb[:, (pair + 1) * P - 1:(pair + 1) * P], None, ALU.mult)
                last.then_inc(s["st_scaled"], 1)
                dve.wait_ge(s["o_ssq"], after(t))
                dve.tensor_scalar(ossq[:], ossq[:], 1.0 / DV, EPS, ALU.mult, ALU.add).then_inc(s["o_eps"], 1)
                dve.wait_ge(s["gla_up"], after(t))
                dve.wait_ge(s["st_scaled"], after(t))
                dve.tensor_tensor(state[:].rearrange("p a v -> p (a v)"), state[:].rearrange("p a v -> p (a v)"),
                                  sc[:, 0:2 * DV], ALU.add).then_inc(s["st_new"], 1)
                dve.wait_ge(s["o_rstd"], after(t))
                for par in range(2):
                    last = dve.scalar_tensor_tensor(
                        out=mix[:, 0:GV].rearrange("p (a b v) -> p b a v", a=2, b=2)[:, par],
                        in0=gla_out[par].rearrange("p (a v) -> p a v", a=2), scalar=DK ** -0.5,
                        in1=orstd[:].rearrange("p (a b) -> p b a", b=2)[:, par].unsqueeze(2)
                        .to_broadcast([P, 2, DV]), op0=ALU.mult, op1=ALU.mult)
                last.then_inc(s["o_scaled"], 1)
                dve.wait_ge(s["o_scaled"], after(t))
                dve.wait_ge(s["r_gate"], after(t))
                dve.tensor_tensor(mix[:, 0:GV], mix[:, 0:GV], gate[:], ALU.mult).then_inc(s["o_mix"], 1)

            with dve.Fori(0, NT - 2) as t:
                attend(t, True, True)
                split_h(t + 2)
            attend(NT - 2, True, False)
            attend(NT - 1, False, False)
    nc.clear_and_free_semaphores(all_sems)
    nc.all_engine_barrier()


def ffn_memory(nc, ctx):
    def sb(name, shape, dt=F32, where=ctx):
        return where.enter_context(nc.sbuf_tensor(name, shape, dt))

    m = {}
    wo_first = sb("w_out_first", [P, KD // 2, 2, D], F32R)
    m["ident"] = sb("ident_b", [P, P])
    m["onorm"] = sb("gla_norm_col", [P, 1])
    m["norm2"] = sb("norm2_col", [P, KD])
    m["fnorm"] = sb("final_norm_row", [P, D])
    m["cw"] = sb("conv_w_cols", [P, 3, 2 * NC_FF])
    m["cb"] = sb("conv_b_cols", [P, 2 * NC_FF])
    m["carry"] = sb("conv_carry", [P, 2 * NC_FF, 2])
    m["nhalf"] = sb("minus_half_b", [P, 1])
    m["ms"] = sb("mean_square_b", [P, 1])
    m["rstd"] = sb("rstd_b", [P, 1])
    m["f_ms"] = sb("mean_square_last", [P, 1])
    m["f_rstd"] = sb("rstd_last", [P, 1])
    m["normed"] = sb("normed", [P, D])
    m["fin"] = [sb("final0", [P, D]), sb("final1", [P, D])]
    spare = sb("w_out_raw", [P, D])
    with ExitStack() as projection:
        wo_last = sb("w_out_last", [P, KD // 2, 2, D], F32R, projection)
        m["mixt"] = sb("mix_tile", [P, KD, P], F32, projection)
        m["xt"] = sb("x_res", [P, D], F32, projection)
        m["mix_hi"] = [sb(f"mix_hi{u}", [P, KD, P], F32R, projection) for u in range(2)]
        m["mix_lo"] = [sb(f"mix_lo{u}", [P, KD, P], F32R, projection) for u in range(2)]
    for name in ("conv_g", "conv_u", "gated", "wd_raw"):
        m[name] = sb(name, [P, TOK])[:]
    for name in ("wd_hi", "wd_lo", "g_hi", "g_lo"):
        m[name] = sb(name, [P, TOK], F32R)[:]
    for name in ("wg_raw", "wu_raw"):
        m[name] = sb(name, [P, KD, P])
    for name in ("wg_hi", "wg_lo", "wu_hi", "wu_lo"):
        m[name] = sb(name, [P, KD, P], F32R)
    y = m["y"] = sb("y", [P, TPH, D])
    m["g2_hi"] = sb("h2_hi", [P, KD, TOK], F32R)
    m["g2_lo"] = sb("h2_lo", [P, KD, TOK], F32R)
    m["wo"] = [wo_first[:, k] for k in range(KD // 2)] + [wo_last[:, k] for k in range(KD // 2)]
    m["wo_raw"] = [y[:, k, :] for k in range(4)] + [m["normed"][:], m["fin"][0][:], m["fin"][1][:], spare[:]]
    return m


def ffn_phase(nc, t_in, mix_scratch, out, mem):
    with ExitStack() as ctx:
        def ps(name, cols):
            return ctx.enter_context(nc.psum_tensor(name, [P, cols], F32))

        def sem(name):
            return ctx.enter_context(nc.semaphore(name))

        wo, wo_raw, ident, norm2, fnorm = mem["wo"], mem["wo_raw"], mem["ident"], mem["norm2"], mem["fnorm"]
        cw, cb, carry, nhalf = mem["cw"], mem["cb"], mem["carry"], mem["nhalf"]
        ms, rstd, f_ms, f_rstd = mem["ms"], mem["rstd"], mem["f_ms"], mem["f_rstd"]
        normed, fin, y, g2_hi, g2_lo = mem["normed"], mem["fin"], mem["y"], mem["g2_hi"], mem["g2_lo"]
        mixt, xt, mix_hi, mix_lo = mem["mixt"], mem["xt"], mem["mix_hi"], mem["mix_lo"]
        conv_g, conv_u, gated = mem["conv_g"], mem["conv_u"], mem["gated"]
        wd_raw, wd_hi, wd_lo, g_hi, g_lo = mem["wd_raw"], mem["wd_hi"], mem["wd_lo"], mem["g_hi"], mem["g_lo"]
        wg_raw, wg_hi, wg_lo = mem["wg_raw"], mem["wg_hi"], mem["wg_lo"]
        wu_raw, wu_hi, wu_lo = mem["wu_raw"], mem["wu_hi"], mem["wu_lo"]

        gate_ps = ps("gate_ps", TOK)
        up_ps = ps("up_ps", TOK)
        acc_ps = [ps("acc_ps0", D), ps("acc_ps1", D)]

        owned = {
            "pe": "o_mm o_turned f_gate f_up",
            "act": """o_mix_hi o_sq o_normed o_split_hi f_wg_hi f_wu_hi f_wd_hi f_gate_tap f_up_tap f_silu f_g_hi
                n_sq""",
            "pool": "o_rstd n_rstd",
            "dve": """o_mix_lo o_added o_eps o_split_lo f_wg_lo f_wu_lo f_wd_lo
                f_gate_tap1 f_gate_tap2 f_gate_edge f_gate_conv f_up_tap1 f_up_tap2 f_up_edge f_up_conv
                f_prod f_g_lo n_eps n_out""",
        }
        s = {n: sem("b_" + n) for names in owned.values() for n in names.split()}
        stepped = {who: [s[n] for n in names.split()] for who, names in owned.items()}
        s_dn = [sem(f"b_down{q}") for q in range(TPH)]
        stepped["pe"] += s_dn
        s_ad = [sem(f"b_added{q}") for q in range(TPH)]
        stepped["dve"] += s_ad
        s_setup, s_pool = sem("b_setup"), sem("b_pool_setup")
        again = range(KD // 2, KD)
        s_wo, s_wo_hi, s_wo_lo = [sem(f"b_w_out_load{k}") for k in again], sem("b_w_out_hi"), sem("b_w_out_lo")
        s_mix, s_x = sem("b_mix_load"), sem("b_x_load")
        s_wg, s_wu, s_wd = sem("b_wg_load"), sem("b_wu_load"), sem("b_wd_load")
        s_out = [sem("b_out_store0"), sem("b_out_store1")]

        block = ctx.enter_context(nc.Block())

        LAST = NC_FF - 1

        def slice_of(hf, c):
            return hf * NC_FF + c

        def tile_of(q):
            return y[:, bass.ds(q, 1), :].rearrange("p o d -> p (o d)")

        def prime(eng, who):
            for one in stepped[who]:
                eng.sem_inc(one, PRIME)

        def plain(eng, value):
            if not isinstance(value, int):
                eng.lower_val(value)
            eng.wait_ge(s_setup, 1)

        def loaded(n):
            return 16 * (n + PRIME)

        @block.sync
        def _(sp):
            for u in range(2):
                sp.sem_inc(s_out[u], 16 * PRIME)
            sp.sem_inc(s_mix, 16 * PRIME)
            sp.sem_inc(s_x, 16 * PRIME)

            def load_mix(n):
                sp.wait_ge(s["o_mix_lo"], after(n - 1))
                sp.dma_start(mixt[:], mix_scratch[bass.ds(n, 1)].rearrange("o p k n -> (o p) k n")).then_inc(s_mix, 16)

            def load_x(n):
                sp.wait_ge(s["o_added"], after(n - 1))
                sp.dma_start(xt[:], t_in["x"][0, bass.ds(n * P, P), :]).then_inc(s_x, 16)

            def store(n, u):
                sp.wait_ge(s["n_out"], after(n))
                sp.dma_start(out[0, bass.ds(n * P, P), :], fin[u][:]).then_inc(s_out[u], 16)

            def load_slice(m, c):
                sp.wait_ge(s["f_wg_lo"], after(m - 1))
                sp.dma_start(wg_raw[:], t_in["w_up"][0].rearrange("(k p) f -> p k f", p=P)[:, :, bass.ds(c * P, P)]
                             ).then_inc(s_wg, 16)
                sp.wait_ge(s["f_wu_lo"], after(m - 1))
                sp.dma_start(wu_raw[:], t_in["w_up"][0].rearrange("(k p) f -> p k f", p=P)
                             [:, :, bass.ds(c * P + FF, P)]).then_inc(s_wu, 16)
                sp.wait_ge(s["f_wd_lo"], after(m - 1))
                sp.dma_start(wd_raw, t_in["w_down"][0, bass.ds(c * P, P), :]).then_inc(s_wd, 16)

            for hf in range(HALVES):
                n0 = hf * TPH
                if hf > 0:
                    sp.wait_ge(s["f_wg_lo"], after(slice_of(hf - 1, LAST)))
                    load_mix(n0)
                    sp.wait_ge(s["f_wu_lo"], after(slice_of(hf - 1, LAST)))
                    load_x(n0)
                load_mix(n0 + 1)
                old = n0 - TPH
                with sp.Fori(0, TPH // 2 - 1) as i:
                    for u in range(2):
                        load_mix(n0 + i * 2 + (2 + u))
                        if hf > 0:
                            store(old + i * 2 + u, u)
                        load_x(n0 + i * 2 + (1 + u))
                if hf > 0:
                    store(n0 - 2, 0)
                load_x(n0 + TPH - 1)
                if hf > 0:
                    store(n0 - 1, 1)
                sp.wait_ge(s["o_mix_lo"], after(n0 + TPH - 1))
                sp.wait_ge(s["o_added"], after(n0 + TPH - 1))
                sp.wait_ge(s["o_mm"], after(n0 + TPH - 1))
                load_slice(slice_of(hf, 0), 0)
                with sp.Fori(1, NC_FF) as c:
                    load_slice(slice_of(hf, c), c)
                if hf + 1 < HALVES:
                    for i, k in enumerate(again):
                        sp.dma_start(wo_raw[k], t_in["w_out"][0, k * P:(k + 1) * P, :]).then_inc(s_wo[i], 16)
            with sp.Fori(0, TPH // 2) as i:
                for u in range(2):
                    store(NT - TPH + i * 2 + u, u)
            for u in range(2):
                sp.wait_ge(s_out[u], 16 * after(NT // 2 - 1))

        @block.tensor
        def _(pe):
            prime(pe, "pe")

            def gemm(out_ap, lhs, rhs, first, last):
                pe.matmul(out_ap, lhs[0], rhs[0], start=first, stop=False)
                pe.matmul(out_ap, lhs[0], rhs[1], start=False, stop=False)
                return pe.matmul(out_ap, lhs[1], rhs[0], start=False, stop=last)

            def project_out(n, u, reloaded=False):
                pe.wait_ge(s["o_mix_lo"], after(n))
                pe.wait_ge(s["o_added"], after(n - 2))
                for c0 in range(0, D, 512):
                    for k in range(KD):
                        if reloaded and c0 == 0 and k in again:
                            pe.wait_ge(s_wo_lo, k - again[0] + 1)
                        last = gemm(acc_ps[u][:, c0:c0 + 512], (mix_hi[u][:, k, :], mix_lo[u][:, k, :]),
                                    (wo[k][:, 0, c0:c0 + 512], wo[k][:, 1, c0:c0 + 512]), k == 0, k == KD - 1)
                last.then_inc(s["o_mm"], 1)

            def turn(n):
                pe.wait_ge(s["o_normed"], after(n))
                pe.wait_ge(s["o_split_lo"], after(n - 1))
                for k in range(KD):
                    last = pe.transpose(gate_ps[:, k * P:(k + 1) * P], normed[:, k * P:(k + 1) * P], ident[:])
                last.then_inc(s["o_turned"], 1)

            def raise_(bank, hi, lo, done):
                for t0 in range(0, TOK, 512):
                    for k in range(KD):
                        last = gemm(bank[:, t0:t0 + 512], (hi[:, k, :], lo[:, k, :]),
                                    (g2_hi[:, k, t0:t0 + 512], g2_lo[:, k, t0:t0 + 512]), k == 0, k == KD - 1)
                last.then_inc(done, 1)

            def lower(m, tiles):
                pe.wait_ge(s["f_g_lo"], after(m))
                pe.wait_ge(s["f_wd_lo"], after(m))
                for q in tiles:
                    if q >= 2:
                        pe.wait_ge(s_ad[q - 2], after(m))
                    else:
                        pe.wait_ge(s_ad[TPH - 2 + q], after(m - 1))
                    cols = slice(q * P, (q + 1) * P)
                    for c0 in range(0, D, 512):
                        last = gemm(acc_ps[q % 2][:, c0:c0 + 512], (g_hi[:, cols], g_lo[:, cols]),
                                    (wd_hi[:, c0:c0 + 512], wd_lo[:, c0:c0 + 512]), True, True)
                    last.then_inc(s_dn[q], 1)

            def gate_part(m):
                pe.wait_ge(s["f_wg_lo"], after(m))
                pe.wait_ge(s["f_gate_conv"], after(m - 1))
                raise_(gate_ps, wg_hi, wg_lo, s["f_gate"])

            def up_part(m):
                pe.wait_ge(s["f_wu_lo"], after(m))
                pe.wait_ge(s["f_up_conv"], after(m - 1))
                raise_(up_ps, wu_hi, wu_lo, s["f_up"])

            pe.wait_ge(s_setup, 1)
            for hf in range(HALVES):
                n0, m0 = hf * TPH, slice_of(hf, 0)
                if hf > 0:
                    pe.wait_ge(s_ad[TPH - 1], after(m0 - 1))
                project_out(n0, 0, reloaded=hf > 0)
                with pe.Fori(0, TPH // 2 - 1) as i:
                    project_out(n0 + i * 2 + 1, 1)
                    turn(n0 + i * 2)
                    project_out(n0 + i * 2 + 2, 0)
                    turn(n0 + i * 2 + 1)
                project_out(n0 + TPH - 1, 1)
                turn(n0 + TPH - 2)
                turn(n0 + TPH - 1)
                pe.wait_ge(s["o_split_lo"], after(n0 + TPH - 1))
                gate_part(m0)
                up_part(m0)
                with pe.Fori(0, NC_FF - 2) as c:
                    m = m0 + c
                    gate_part(m + 1)
                    lower(m, range(0, TPH // 2))
                    up_part(m + 1)
                    lower(m, range(TPH // 2, TPH))
                m = slice_of(hf, LAST)
                gate_part(m)
                up_part(m)
                lower(m - 1, range(TPH))
                lower(m, range(TPH))

        @block.scalar
        def _(act):
            prime(act, "act")
            act.wait_ge(s_setup, 1)

            def split_w(m, raw, hi, loaded, free, done):
                act.wait_ge(loaded, (m + 1) * 16)
                act.wait_ge(free, after(m - 1))
                for k in range(KD):
                    last = act.activation(hi[:, k, :], raw[:, k, :], ACT.Copy, scale=norm2[:, k:k + 1])
                last.then_inc(done, 1)

            def last_tap(m, bank, conv, col, ready, free, done):
                plain(act, after(m))
                act.wait_ge(ready, after(m))
                act.wait_ge(free, after(m - 1))
                act.activation(conv, bank[:], ACT.Copy, scale=cw[:, 2, bass.ds(col, 1)]).then_inc(done, 1)

            def gated_part(m, c):
                last_tap(m, up_ps, conv_u, c + NC_FF, s["f_up"], s["f_prod"], s["f_up_tap"])
                plain(act, after(m))
                act.wait_ge(s["f_gate_conv"], after(m))
                act.activation(conv_g, conv_g, ACT.Silu, bias=cb[:, bass.ds(c, 1)]).then_inc(s["f_silu"], 1)
                act.wait_ge(s_wd, (m + 1) * 16)
                act.wait_ge(s_dn[TPH - 1], after(m - 1))
                act.activation(wd_hi, wd_raw, ACT.Copy).then_inc(s["f_wd_hi"], 1)
                act.wait_ge(s["f_prod"], after(m))
                act.activation(g_hi, gated, ACT.Copy).then_inc(s["f_g_hi"], 1)

            def mix_high(n, u):
                act.wait_ge(s_mix, loaded(n))
                act.wait_ge(s["o_mm"], after(n - 2))
                act.activation(mix_hi[u][:], mixt[:], ACT.Copy).then_inc(s["o_mix_hi"], 1)

            def square(n, q):
                plain(act, after(n))
                act.wait_ge(s["o_added"], after(n))
                act.wait_ge(s["o_turned"], after(n - 1))
                act.activation(normed[:], tile_of(q), ACT.Square, accum_out=ms[:, 0:1]).then_inc(s["o_sq"], 1)

            def normalise(n, q):
                plain(act, after(n))
                act.wait_ge(s["o_rstd"], after(n))
                act.activation(normed[:], tile_of(q), ACT.Copy, scale=rstd[:, 0:1]).then_inc(s["o_normed"], 1)

            def turned_high(n, q):
                plain(act, after(n))
                act.wait_ge(s["o_turned"], after(n))
                act.activation(g2_hi[:, :, bass.ds(q * P, P)], gate_ps[:].rearrange("p (k n) -> p k n", k=KD),
                               ACT.Copy).then_inc(s["o_split_hi"], 1)

            def last_square(n, q, u, stored):
                plain(act, after(n - 1))
                act.wait_ge(s["n_rstd"], after(n - 1))
                act.wait_ge(s_out[u], 16 * (stored + PRIME))
                act.activation(fin[u][:], tile_of(q), ACT.Square, accum_out=f_ms[:, 0:1]).then_inc(s["n_sq"], 1)

            for hf in range(HALVES):
                n0, m0, old = hf * TPH, slice_of(hf, 0), (hf - 1) * TPH
                if hf > 0:
                    act.wait_ge(s["f_gate"], after(m0 - 1))
                mix_high(n0, 0)
                if hf > 0:
                    for k in again[:2]:
                        act.wait_ge(s_wo[k - again[0]], 16)
                        act.wait_ge(s["f_g_lo"], after(m0 - 1))
                        act.activation(wo[k][:, 0, :], wo_raw[k], ACT.Copy).then_inc(s_wo_hi, 1)
                mix_high(n0 + 1, 1)
                if hf > 0:
                    for k in again[2:]:
                        act.wait_ge(s_wo[k - again[0]], 16)
                        act.wait_ge(s_dn[TPH - 1], after(m0 - 1))
                        act.activation(wo[k][:, 0, :], wo_raw[k], ACT.Copy).then_inc(s_wo_hi, 1)
                    act.wait_ge(s_wo_lo, len(again))
                    act.wait_ge(s_ad[TPH - 1], after(m0 - 1))
                    last_square(old, 0, 0, old // 2)
                with act.Fori(0, TPH // 2 - 1) as i:
                    for u in range(2):
                        q = i * 2 + u
                        square(n0 + q, q)
                        if hf > 0:
                            last_square(old + q + 1, q + 1, 1 - u, i + (old // 2 + u))
                        normalise(n0 + q, q)
                        mix_high(n0 + q + 2, u)
                        turned_high(n0 + q, q)
                for q in range(TPH - 2, TPH):
                    square(n0 + q, q)
                    if hf > 0 and q + 1 < TPH:
                        last_square(old + q + 1, q + 1, (q + 1) % 2, (old + q + 1) // 2)
                    normalise(n0 + q, q)
                    turned_high(n0 + q, q)

                act.wait_ge(s["o_mm"], after(n0 + TPH - 1))
                split_w(m0, wg_raw, wg_hi, s_wg, s["f_gate"], s["f_wg_hi"])
                split_w(m0, wu_raw, wu_hi, s_wu, s["f_up"], s["f_wu_hi"])
                with act.Fori(0, NC_FF - 1) as c:
                    m = m0 + c
                    last_tap(m, gate_ps, conv_g, c, s["f_gate"], s["f_prod"], s["f_gate_tap"])
                    split_w(m + 1, wg_raw, wg_hi, s_wg, s["f_gate"], s["f_wg_hi"])
                    gated_part(m, c)
                    split_w(m + 1, wu_raw, wu_hi, s_wu, s["f_up"], s["f_wu_hi"])
                m = slice_of(hf, LAST)
                last_tap(m, gate_ps, conv_g, LAST, s["f_gate"], s["f_prod"], s["f_gate_tap"])
                gated_part(m, LAST)
            for q in range(TPH):
                n = NT - TPH + q
                act.wait_ge(s_ad[q], after(slice_of(HALVES - 1, LAST)))
                last_square(n, q, q % 2, n // 2)

        @block.gpsimd
        def _(pool):
            prime(pool, "pool")
            pool.memset(nhalf[:], -0.5).then_inc(s_pool, 1)
            pool.wait_ge(s_pool, 1)

            def root(n, mean, inv, pre):
                pool.wait_ge(s[pre + "eps"], after(n))
                pool.tensor_tensor(inv[:], mean[:], nhalf[:], ALU.pow).then_inc(s[pre + "rstd"], 1)

            with pool.Fori(0, TPH) as q:
                root(q, ms, rstd, "o_")
            for hf in range(1, HALVES):
                n0, old = hf * TPH, (hf - 1) * TPH
                for k in again:
                    pool.wait_ge(s_wo_hi, k - again[0] + 1)
                    pool.tensor_tensor(wo[k][:, 1, :], wo_raw[k], wo[k][:, 0, :].bitcast(F32), ALU.subtract
                                       ).then_inc(s_wo_lo, 1)
                root(old, f_ms, f_rstd, "n_")
                with pool.Fori(0, TPH - 1) as q:
                    root(n0 + q, ms, rstd, "o_")
                    root(old + 1 + q, f_ms, f_rstd, "n_")
                root(n0 + TPH - 1, ms, rstd, "o_")
            with pool.Fori(0, TPH) as q:
                root(NT - TPH + q, f_ms, f_rstd, "n_")

        @block.vector
        def _(dve):
            prime(dve, "dve")
            dve.memset(carry[:], 0.0).then_inc(s_setup, 1)
            dve.wait_ge(s_setup, 1)

            def split_w(m, raw, hi, lo, done_hi, done):
                dve.wait_ge(done_hi, after(m))
                for k in range(KD):
                    last = dve.scalar_tensor_tensor(out=lo[:, k, :], in0=raw[:, k, :], scalar=norm2[:, k:k + 1],
                                                    in1=hi[:, k, :].bitcast(F32), op0=ALU.mult, op1=ALU.subtract)
                last.then_inc(done, 1)

            def add_down(m, tiles):
                for q in tiles:
                    dve.wait_ge(s_dn[q], after(m))
                    dve.tensor_tensor(y[:, q, :], y[:, q, :], acc_ps[q % 2][:], ALU.add).then_inc(s_ad[q], 1)

            def conv(m, bank, acc, col, pre):
                tap0, tap1 = cw[:, 0, bass.ds(col, 1)], cw[:, 1, bass.ds(col, 1)]
                old = carry[:, bass.ds(col, 1), :].rearrange("p o a -> p (o a)")
                dve.wait_ge(s[pre + "tap"], after(m))
                dve.scalar_tensor_tensor(out=acc[:, 1:TOK], in0=bank[:, 0:TOK - 1], scalar=tap1,
                                         in1=acc[:, 1:TOK], op0=ALU.mult, op1=ALU.add).then_inc(s[pre + "tap1"], 1)
                dve.wait_ge(s[pre + "tap1"], after(m))
                dve.scalar_tensor_tensor(out=acc[:, 2:TOK], in0=bank[:, 0:TOK - 2], scalar=tap0,
                                         in1=acc[:, 2:TOK], op0=ALU.mult, op1=ALU.add)
                dve.scalar_tensor_tensor(out=acc[:, 0:1], in0=old[:, 1:2], scalar=tap1, in1=acc[:, 0:1],
                                         op0=ALU.mult, op1=ALU.add).then_inc(s[pre + "tap2"], 1)
                dve.wait_ge(s[pre + "tap2"], after(m))
                dve.scalar_tensor_tensor(out=acc[:, 0:2], in0=old, scalar=tap0, in1=acc[:, 0:2],
                                         op0=ALU.mult, op1=ALU.add).then_inc(s[pre + "edge"], 1)
                plain(dve, after(m))
                dve.wait_ge(s[pre + "edge"], after(m))
                dve.tensor_copy(old, bank[:, TOK - 2:TOK]).then_inc(s[pre + "conv"], 1)

            def conv_gate(m, c):
                conv(m, gate_ps, conv_g, c, "f_gate_")

            def conv_up(m, c):
                conv(m, up_ps, conv_u, c + NC_FF, "f_up_")

            def gated_part(m, c):
                dve.wait_ge(s["f_silu"], after(m))
                dve.wait_ge(s["f_up_conv"], after(m))
                dve.wait_ge(s["f_g_lo"], after(m - 1))
                dve.scalar_tensor_tensor(out=gated, in0=conv_u, scalar=cb[:, bass.ds(c + NC_FF, 1)], in1=conv_g,
                                         op0=ALU.add, op1=ALU.mult).then_inc(s["f_prod"], 1)
                dve.wait_ge(s["f_wd_hi"], after(m))
                dve.tensor_tensor(wd_lo, wd_raw, wd_hi.bitcast(F32), ALU.subtract).then_inc(s["f_wd_lo"], 1)
                dve.wait_ge(s["f_g_hi"], after(m))
                dve.tensor_tensor(g_lo, gated, g_hi.bitcast(F32), ALU.subtract).then_inc(s["f_g_lo"], 1)

            def mix_low(n, u):
                dve.wait_ge(s["o_mix_hi"], after(n))
                dve.tensor_tensor(mix_lo[u][:], mixt[:], mix_hi[u][:].bitcast(F32), ALU.subtract
                                  ).then_inc(s["o_mix_lo"], 1)

            def add_residual(n, q, u, old=None):
                if old is not None:
                    dve.wait_ge(s["n_out"], after(old))
                dve.wait_ge(s["o_mm"], after(n))
                dve.wait_ge(s_x, loaded(n))
                dve.tensor_tensor(tile_of(q), acc_ps[u][:], xt[:], ALU.add).then_inc(s["o_added"], 1)

            def mean(n, sums, pre):
                dve.wait_ge(s[pre + "sq"], after(n))
                dve.tensor_scalar(sums[:], sums[:], 1.0 / D, EPS, ALU.mult, ALU.add).then_inc(s[pre + "eps"], 1)

            def turned_low(n, q):
                dve.wait_ge(s["o_split_hi"], after(n))
                dve.tensor_tensor(g2_lo[:, :, bass.ds(q * P, P)], gate_ps[:].rearrange("p (k n) -> p k n", k=KD),
                                  g2_hi[:, :, bass.ds(q * P, P)].bitcast(F32), ALU.subtract
                                  ).then_inc(s["o_split_lo"], 1)

            def last_norm(n, q, u):
                dve.wait_ge(s["n_rstd"], after(n))
                dve.scalar_tensor_tensor(out=fin[u][:], in0=tile_of(q), scalar=f_rstd[:, 0:1], in1=fnorm[:],
                                         op0=ALU.mult, op1=ALU.mult).then_inc(s["n_out"], 1)

            for hf in range(HALVES):
                n0, m0, old = hf * TPH, slice_of(hf, 0), (hf - 1) * TPH
                if hf > 0:
                    dve.wait_ge(s["f_up"], after(m0 - 1))
                mix_low(n0, 0)
                if hf > 0:
                    add_down(m0 - 1, range(TPH))
                mix_low(n0 + 1, 1)
                if hf > 0:
                    mean(old, f_ms, "n_")
                with dve.Fori(0, TPH // 2 - 1) as i:
                    for u in range(2):
                        q = i * 2 + u
                        if hf > 0:
                            last_norm(old + q, q, u)
                        add_residual(n0 + q, q, u, old + q if hf > 0 else None)
                        mean(n0 + q, ms, "o_")
                        if hf > 0:
                            mean(old + q + 1, f_ms, "n_")
                        mix_low(n0 + q + 2, u)
                        turned_low(n0 + q, q)
                for q in range(TPH - 2, TPH):
                    if hf > 0:
                        last_norm(old + q, q, q % 2)
                    add_residual(n0 + q, q, q % 2, old + q if hf > 0 else None)
                    mean(n0 + q, ms, "o_")
                    if hf > 0 and q + 1 < TPH:
                        mean(old + q + 1, f_ms, "n_")
                    turned_low(n0 + q, q)

                split_w(m0, wg_raw, wg_hi, wg_lo, s["f_wg_hi"], s["f_wg_lo"])
                split_w(m0, wu_raw, wu_hi, wu_lo, s["f_wu_hi"], s["f_wu_lo"])
                conv_gate(m0, 0)
                split_w(m0 + 1, wg_raw, wg_hi, wg_lo, s["f_wg_hi"], s["f_wg_lo"])
                conv_up(m0, 0)
                gated_part(m0, 0)
                split_w(m0 + 1, wu_raw, wu_hi, wu_lo, s["f_wu_hi"], s["f_wu_lo"])
                with dve.Fori(1, LAST) as c:
                    m = m0 + c
                    add_down(m - 1, range(0, TPH // 2))
                    conv_gate(m, c)
                    split_w(m + 1, wg_raw, wg_hi, wg_lo, s["f_wg_hi"], s["f_wg_lo"])
                    add_down(m - 1, range(TPH // 2, TPH))
                    conv_up(m, c)
                    gated_part(m, c)
                    split_w(m + 1, wu_raw, wu_hi, wu_lo, s["f_wu_hi"], s["f_wu_lo"])
                m = slice_of(hf, LAST)
                conv_gate(m, LAST)
                conv_up(m, LAST)
                add_down(m - 1, range(TPH))
                gated_part(m, LAST)
            m = slice_of(HALVES - 1, LAST)
            for q in range(TPH + 2):
                if q < TPH:
                    add_down(m, [q])
                if q >= 2:
                    last_norm(NT - TPH + q - 2, q - 2, q % 2)
                if 1 <= q <= TPH:
                    mean(NT - TPH + q - 1, f_ms, "n_")


def program(nc, t_in, out):
    mix_scratch = nc.dram_tensor("mix_scratch", (NT, P, KD, P), F32).ap()
    with ExitStack() as ctx:
        mem = ffn_memory(nc, ctx)
    mixer_phase(nc, t_in, mix_scratch, mem)
    ffn_phase(nc, t_in, mix_scratch, out, mem)


_INS = ['x', 'positions', 'norm1_w', 'w_in', 'gla_gk_w2', 'gla_gk_b', 'gla_norm_w', 'swa_sinks', 'w_out',
        'norm2_w', 'w_up', 'conv_w', 'conv_b', 'w_down', 'final_norm_w']


def _constants():
    j, i = np.meshgrid(np.arange(P), np.arange(P), indexing="ij")
    masks = [((j // (2 * w) == i // (2 * w)) & (j % (2 * w) < w) & (i % (2 * w) >= w)) for w in SPANS[2:]]
    masks.append(i == j)
    swa = np.zeros((P, P), np.float32)
    swa[0:CHUNK, 0:CHUNK] = NEG
    inv = np.float32(THETA) ** (-np.arange(RH, dtype=np.float32) / np.float32(RH))
    return {"c_ident": np.eye(P, dtype=np.float32),
            "c_masks": np.ascontiguousarray(np.stack(masks, 1).astype(np.float32).reshape(P, -1)),
            "c_swa_mask": swa,
            "c_inv_freq": np.ascontiguousarray(np.broadcast_to(inv.astype(np.float32), (P, RH)))}


def kernel(**inputs):
    import concourse.bacc as _bacc
    from concourse.bass_utils import run_bass_kernel_spmd as _run

    nc = _bacc.Bacc("TRN2", target_bir_lowering=False, num_devices=1)
    arrays, t_in = {}, {}
    for name, a in [(n, np.ascontiguousarray(inputs[n])) for n in _INS] + list(_constants().items()):
        arrays[f"in_{name}"] = a
        t_in[name] = nc.dram_tensor(f"in_{name}", a.shape, mybir.dt.from_np(a.dtype), kind="ExternalInput").ap()
    out = nc.dram_tensor("out_dram", (1, S, D), F32, kind="ExternalOutput").ap()
    program(nc, t_in, out)
    r = _run(nc, [arrays], core_ids=[0])
    return r.results[0]["out_dram"]
```

```python
from contextlib import ExitStack

import numpy as np

import concourse.bass as bass
from concourse import mybir

P = 128
D = 1024
KD = D // P
S = 2048
NT = S // P
GH, DK, DV, RANK = 4, 64, 128, 16
QK, GV = GH * DK, GH * DV
SH, KVH, HD = 8, 2, 64
GRP = SH // KVH
SQ, SKV = SH * HD, KVH * HD
DMIX = GV + SQ
D_IN = 2 * QK + 2 * GV + RANK + SQ + 2 * SKV
O_QK, O_V, O_R, O_LOW = 0, 2 * QK, 2 * QK + GV, 2 * QK + 2 * GV
O_SQ = O_LOW + RANK
O_SK = O_SQ + SQ
CHUNK = 64
ROPE = HD // 4
RH = ROPE // 2
THETA = 500000.0
EPS = 1e-6
GATE_NORM = 16.0
FF = 2816
NC_FF = FF // P
HALVES = 2
TPH = NT // HALVES
TOK = S // HALVES
SPANS = [64, 32, 16, 8, 4, 2, 1]
NL = len(SPANS)
FIRST_SPANS = 4
SPAN_PARTS = [(0, FIRST_SPANS), (FIRST_SPANS, NL)]
NEG = -1.0e30
TWO_PI = 6.283185307179586
TP_A = 6.28125
TP_B = float(np.float32(int((TWO_PI - TP_A) * 2 ** 21) / 2.0 ** 21))
TP_C = TWO_PI - TP_A - TP_B
ROUNDER = 12582912.0
PI_IN = 3.1415925

F32 = mybir.dt.float32
F32R = mybir.dt.float32r
I32 = mybir.dt.int32
U8 = mybir.dt.uint8
ALU = mybir.AluOpType
ACT = mybir.ActivationFunctionType
AX_X = mybir.AxisListType.X

GROUPS = ["qk", "sq", "small", "v", "r"]
PIECES = {"qk": [(O_QK, 2 * QK)], "sq": [(O_SQ, SQ)], "small": [(O_LOW, RANK), (O_SK, 2 * SKV)],
          "v": [(O_V, GV)], "r": [(O_R, GV)]}
WIDTH = {g: sum(w for _, w in PIECES[g]) for g in GROUPS}
FIRST = {g: sum(WIDTH[f] for f in GROUPS[:i]) for i, g in enumerate(GROUPS)}


PRIME = 2


def after(n):
    return n + (1 + PRIME)


def mixer_phase(nc, t_in, mix_scratch, ffn):
    all_sems = []
    with ExitStack() as ctx:
        def sb(name, shape, dt=F32):
            return ctx.enter_context(nc.sbuf_tensor(name, shape, dt))

        def ps(name, cols):
            return ctx.enter_context(nc.psum_tensor(name, [P, cols], F32))

        def sem(name):
            all_sems.append(nc.alloc_semaphore(name=name))
            return all_sems[-1]

        w_hi = sb("w_in_hi", [P, KD, D_IN], F32R)
        w_lo = sb("w_in_lo", [P, KD, D_IN], F32R)
        x = sb("x_tile", [P, D])
        h_hi = sb("h_hi", [P, KD, P], F32R)
        h_lo = sb("h_lo", [P, KD, P], F32R)
        z_qk = sb("z_qk", [P, 2 * QK])
        z_v = sb("z_v", [P, GV])
        z_r = sb("z_r", [P, GV])
        z_low = sb("z_low", [P, RANK])
        z_sqk = sb("z_sqk", [P, GRP + 1, KVH, HD])
        z_sv = sb("z_sv", [P, SKV])
        ident = sb("ident", [P, P])
        masks = sb("level_masks", [P, NL - 1, P], U8)
        swa_mask = sb("swa_mask", [P, P])
        norm1 = sb("norm1_col", [P, KD])
        w2 = sb("gk_w2", [RANK, QK])
        gkb = sb("gk_b_col", [P, 2])
        sinks = sb("sinks_row", [P, SH])
        nsinks = sb("minus_sinks", [P, SH])
        invf = sb("inv_freq", [P, RH])
        pos_i = sb("pos_i", [P, NT], I32)
        pos_f = sb("pos_f", [P, NT])
        cosT = sb("cosT", [P, NT, RH])
        sinT = sb("sinT", [P, NT, RH])
        nhalf = sb("minus_half", [P, GH])
        stats = sb("bn_stats", [P, 2, 6])
        mv = sb("mean_var", [P, 2])
        ms = sb("mean_square", [P, 1])
        rstd = sb("rstd", [P, 1])
        qkT = sb("qkT", [P, 4, P])
        kwin = sb("k_window", [P, CHUNK + P])
        v_cur = sb("v_cur", [P, SKV])
        v_mid = sb("v_mid", [P, SKV])
        lowT = sb("lowT", [RANK, P])
        gate_a = sb("gate_pre", [P, 2 * P])
        gate_l = sb("gate_log", [P, 2 * P])
        gate_m = sb("gate_min", [P, 2 * P])
        B = sb("gate_cumsum", [P, 2 * P])
        Eb = sb("exp_b", [P, 2 * P])
        kd, kdN, qb = gate_m, gate_a, gate_l
        ks = sb("k_level", [P, NL, 2 * P])
        qs = sb("q_level", [P, NL, 2 * P])
        sqT = qs[:, NL - 2:NL, :].rearrange("p l (b n) -> p (l b) n", b=2)
        pT = sb("intra_scores", [P, 2, 2, P])
        state = sb("state", [P, 2, DV])
        prob = sb("prob", [P, SH, P])
        negm = sb("minus_max", [P, SH])
        den = sb("denominator", [P, SH])
        esink = sb("exp_sink", [P, SH])
        rden = sb("recip_denominator", [P, SH])
        probT = sb("probT", [P, SH, P])
        gate = sb("out_gate", [P, GV])
        ossq = sb("o_ssq", [P, GH])
        orstd = sb("o_rstd", [P, GH])
        mix = prob[:].rearrange("p h k -> p (h k)")
        mixT = probT
        rope_heads = (GRP + 1) * KVH
        rope_room = probT[:].rearrange("p h n -> p (h n)")
        ropeA = rope_room[:, 0:rope_heads * ROPE].rearrange("p (h r) -> p h r", h=rope_heads)
        ropeB = rope_room[:, 512:512 + rope_heads * ROPE].rearrange("p (h r) -> p h r", h=rope_heads)

        squares = ks[:, 0:2, :].rearrange("p l (b n) -> p (l b) n", b=2)
        ang = rope_room[:, 0:NT * RH].rearrange("p (t r) -> p t r", t=NT)

        pj = [ps("proj0", 512), ps("proj1", 512)]
        tr = ps("turn", 1024)
        sc = ps("score", 1024)
        ob = ps("outb", 1024)
        gk_ps = sc[:, 1024 - 2 * P:1024]
        gla_out = [ob[:, 0:2 * DV], sc[:, 512:512 + 2 * DV]]

        owned = {
            "pe": """xT zT sT_low gk swa_s swa_pT swa_o kdT gla_o gla_up mixT_done""",
            "act": """x_norm hT_hi0 hT_hi1 e_qk e_sq e_small_low e_small_k e_sv e_v r_exp vmid_lo v_copy vmid_hi
                ev_kshift ev_k ev_low ev_qkT ev_pT ev_kd ev_mixT g_abs g_exp g_log g_eb g_kexp lv_exp0 lv_exp1
                swa_exp swa_sinke o_ssq""",
            "pool": """x_rstd o_rstd""",
            "dve": """x_stats x_ms x_sum x_eps hT_lo0 hT_lo1 rope_mul rope_a rope_b ev_sqT g_pre g_min g_sum g_scan g_kdiff
                g_kd g_qb lv_diff0 lv_diff1 lv_k0 lv_k1 lv_qk0 lv_qk1 swa_masked swa_max swa_neg swa_sinkd swa_den swa_rden swa_mix
                st_scaled st_new o_eps o_scaled o_mix r_one r_rec0 r_rec1 r_gate""",
        }
        s = {n: sem("a_" + n) for names in owned.values() for n in names.split()}
        s_g = {g: sem("a_proj_" + g) for g in GROUPS}
        s_lv = [sem(f"a_lvl{i}") for i in range(NL + 1)]
        s_mg = [sem(f"a_merge{i}") for i in range(NL + 1)]
        stepped = {who: [s[n] for n in names.split()] for who, names in owned.items()}
        stepped["pe"] += [*s_g.values(), *s_lv]
        stepped["dve"] += s_mg
        for n in ("norm1_load", "w_split_hi", "w_split_lo", "dve_setup", "pool_setup", "rope_tab", "rope_act"):
            s[n] = sem("a_" + n)
        NSTAGE = 6
        H_PARTS = [(0, KD // 2), (KD // 2, KD)]
        s_w = [sem(f"a_w_load{i}") for i in range(NSTAGE)]
        s_const = sem("a_const_load")
        s_ffn, s_onorm = sem("a_ffn_const_load"), sem("a_gla_norm_load")
        s_wo = [sem(f"a_w_out_load{k}") for k in range(KD)]
        s_wo_hi, s_wo_lo = sem("a_w_out_hi"), sem("a_w_out_lo")
        s_x = sem("a_x_load")
        s_out = sem("a_mix_store")

        block = ctx.enter_context(nc.Block())

        def prime(eng, who):
            for one in stepped[who]:
                eng.sem_inc(one, PRIME)
        stage_room = [ks[:].rearrange("p l n -> p (l n)"), qs[:].rearrange("p l n -> p (l n)")]
        stage = [stage_room[i // 3][:, (i % 3) * 512:(i % 3 + 1) * 512] for i in range(NSTAGE)]
        pieces = [(g, k) for g in GROUPS for k in range(KD)]

        def loads_of(g):
            return len(PIECES[g])

        def loaded(n):
            return 16 * sum(loads_of(pieces[m][0]) for m in range(n % NSTAGE, n + 1, NSTAGE))

        def last_of_group_evac(g):
            return {"qk": "e_qk", "sq": "e_sq", "small": "e_sv", "v": "e_v", "r": "r_exp"}[g]

        def plain(eng):
            eng.wait_ge(s["pool_setup"], 1)

        @block.sync
        def _(sp):
            sp.sem_inc(s_out, 16 * PRIME)
            sp.sem_inc(s_x, 16 * PRIME)
            sp.dma_start(norm1[:], t_in["norm1_w"][0].rearrange("(k p) -> p k", p=P),
                         allow_slow_non_contiguous=True).then_inc(s["norm1_load"], 16)
            sp.dma_start(x[:], t_in["x"][0, 0:P, :]).then_inc(s_x, 16)
            for n, (g, k) in enumerate(pieces):
                if n >= NSTAGE:
                    sp.wait_ge(s["w_split_lo"], n - NSTAGE + 1)
                at = 0
                for c0, w in PIECES[g]:
                    sp.dma_start(stage[n % NSTAGE][:, at:at + w], t_in["w_in"][0, k * P:(k + 1) * P, c0:c0 + w]
                                 ).then_inc(s_w[n % NSTAGE], 16)
                    at += w

            def load_x(n):
                sp.wait_ge(s["xT"], after(n - 1))
                sp.dma_start(x[:], t_in["x"][0, bass.ds(n * P, P), :]).then_inc(s_x, 16)

            def store_mix(t):
                sp.wait_ge(s["ev_mixT"], after(t))
                sp.dma_start(mix_scratch[bass.ds(t, 1)].rearrange("o p k n -> (o p) k n"), mixT[:]).then_inc(s_out, 16)

            load_x(1)
            with sp.Fori(0, NT - 2) as t:
                load_x(t + 2)
                store_mix(t)
            sp.wait_ge(s_g["r"], after(NT - 1))
            sp.dma_start(ffn["onorm"][:], t_in["gla_norm_w"][0].rearrange("(p a) -> p a", a=1)).then_inc(s_onorm, 16)
            for k in range(KD):
                sp.dma_start(ffn["wo_raw"][k], t_in["w_out"][0, k * P:(k + 1) * P, :]).then_inc(s_wo[k], 16)
            store_mix(NT - 2)
            sp.dma_start(ffn["mixt"][:], mix_scratch[0]).then_inc(s_ffn, 16)
            sp.dma_start(ffn["xt"][:], t_in["x"][0, 0:P, :]).then_inc(s_ffn, 16)
            for dst, src in ((ffn["ident"][:], t_in["c_ident"]),
                             (ffn["norm2"][:], t_in["norm2_w"][0].rearrange("(k p) -> p k", p=P)),
                             (ffn["fnorm"][:], t_in["final_norm_w"].partition_broadcast(P)),
                             (ffn["cw"][:], t_in["conv_w"][0].rearrange("i (c p) -> p i c", p=P)),
                             (ffn["cb"][:], t_in["conv_b"][0].rearrange("(c p) -> p c", p=P))):
                sp.dma_start(dst, src, allow_slow_non_contiguous=True).then_inc(s_ffn, 16)
            store_mix(NT - 1)
            sp.wait_ge(s_ffn, 16 * 7)
            sp.wait_ge(s_out, 16 * after(NT - 1))

        @block.tensor
        def _(pe):
            prime(pe, "pe")

            def turn_x(n):
                pe.wait_ge(s["x_norm"], after(n))
                pe.wait_ge(s["swa_mix"], after(n - 2))
                pe.wait_ge(s["o_scaled"], after(n - 2))
                pe.wait_ge(s["hT_lo1"], after(n - 1))
                for k in range(KD):
                    last = pe.transpose(ob[:, k * P:(k + 1) * P], x[:, k * P:(k + 1) * P], ident[:])
                last.then_inc(s["xT"], 1)

            def project(n, g, blocks=range(KD)):
                if 0 in blocks:
                    project_waits(n, g)
                out = pj[GROUPS.index(g) % 2][:, 0:WIDTH[g]]
                cols = slice(FIRST[g], FIRST[g] + WIDTH[g])
                for k in blocks:
                    if g == GROUPS[0] and k == H_PARTS[1][0]:
                        pe.wait_ge(s["hT_lo1"], after(n))
                    pe.matmul(out, h_hi[:, k, :], w_hi[:, k, cols], start=(k == 0), stop=False)
                    pe.matmul(out, h_hi[:, k, :], w_lo[:, k, cols], start=False, stop=False)
                    last = pe.matmul(out, h_lo[:, k, :], w_hi[:, k, cols], start=False, stop=(k == KD - 1))
                if KD - 1 in blocks:
                    last.then_inc(s_g[g], 1)

            def project_waits(n, g):
                i = GROUPS.index(g)
                if i == 0:
                    pe.wait_ge(s["hT_lo0"], after(n))
                free = GROUPS[i - 2] if i >= 2 else GROUPS[4 - i]
                pe.wait_ge(s[last_of_group_evac(free)], after(n if i >= 2 else n - 1))

            def second_halves(cols, l):
                return cols.rearrange("p (n a w) -> p n a w", a=2, w=SPANS[l])[:, :, 1, :]

            def level(t, l):
                bank = ob if l % 2 == 0 else sc
                if l == 0:
                    pe.wait_ge(s["lv_qk0"], after(t))
                elif l == 1:
                    pe.wait_ge(s["swa_masked"], after(t))
                else:
                    pe.wait_ge(s_mg[l - 2], after(t))
                if l == FIRST_SPANS:
                    pe.wait_ge(s["lv_qk1"], after(t))
                for pair in range(2):
                    for par in range(2):
                        rows = slice(par * DK, (par + 1) * DK)
                        if l < NL:
                            lhs, rhs = ks[rows, l, pair * P:(pair + 1) * P], qs[rows, l, pair * P:(pair + 1) * P]
                        else:
                            lhs, rhs = qkT[rows, 2 + pair, :], qkT[rows, pair, :]
                        at = par * 512 + pair * P
                        got = bank[:, at:at + P]
                        if l < NL:
                            rhs, got = second_halves(rhs, l), second_halves(got, l)
                        last = pe.matmul(got, lhs, rhs, start=True, stop=True)
                last.then_inc(s_lv[l], 1)

            def attend(t, more):
                pe.wait_ge(s["rope_b"], after(t))
                pe.wait_ge(s["rope_a"], after(t))
                pe.wait_ge(s["e_small_low"], after(t))
                pe.wait_ge(s["st_new"], after(t - 1))
                pe.wait_ge(s["o_scaled"], after(t - 1))
                pe.transpose(sc[:, 0:P], z_sqk[:, GRP, :, :], ident[:])
                pe.transpose(sc[0:RANK, 512:512 + P], z_low[:], ident[:]).then_inc(s["sT_low"], 1)
                pe.wait_ge(s["e_qk"], after(t))
                pe.wait_ge(s["ev_mixT"], after(t - 1))
                for b in range(4):
                    pe.transpose(tr[:, b * P:(b + 1) * P], z_qk[:, b * P:(b + 1) * P], ident[:])
                for b in range(GRP):
                    last = pe.transpose(tr[:, 512 + b * P:512 + (b + 1) * P], z_sqk[:, b, :, :], ident[:])
                last.then_inc(s["zT"], 1)
                pe.wait_ge(s["ev_low"], after(t))
                for pair in range(2):
                    last = pe.matmul(gk_ps[:, pair * P:(pair + 1) * P], w2[:, pair * P:(pair + 1) * P], lowT[:],
                                     start=True, stop=True)
                last.then_inc(s["gk"], 1)
                if more:
                    project(t + 1, "qk")
                plain(pe)
                pe.wait_ge(s["ev_k"], after(t))
                pe.wait_ge(s["ev_sqT"], after(t))
                pe.wait_ge(s["g_pre"], after(t))
                for b in range(GRP):
                    for g in range(KVH):
                        rows = slice(g * HD, (g + 1) * HD)
                        for c in range(2):
                            last = pe.matmul(
                                sc[c * CHUNK:(c + 1) * CHUNK, g * 512 + b * P:g * 512 + (b + 1) * P],
                                sqT[rows, b, c * CHUNK:(c + 1) * CHUNK], kwin[rows, c * CHUNK:c * CHUNK + P],
                                start=True, stop=True)
                last.then_inc(s["swa_s"], 1)
                if more:
                    project(t + 1, "sq")
                    project(t + 1, "small")
                pe.wait_ge(s["swa_exp"], after(t))
                pe.wait_ge(s["ev_qkT"], after(t))
                for h in range(SH):
                    last = pe.transpose(tr[:, h * P:(h + 1) * P], prob[:, h, :], ident[:])
                last.then_inc(s["swa_pT"], 1)
                for l in range(NL + 1):
                    level(t, l)
                    if more:
                        project(t + 1, "v", [l])
                pe.wait_ge(s["g_kd"], after(t))
                pe.wait_ge(s["ev_pT"], after(t))
                for pair in range(2):
                    last = pe.transpose(tr[:, pair * P:(pair + 1) * P], kd[:, pair * P:(pair + 1) * P], ident[:])
                last.then_inc(s["kdT"], 1)
                pe.wait_ge(s["vmid_hi"], after(t))
                pe.wait_ge(s_mg[NL - 1], after(t))
                for h in range(SH):
                    g = h // GRP
                    for c, vals in ((0, v_mid), (1, v_cur)):
                        last = pe.matmul(ob[c * CHUNK:(c + 1) * CHUNK, 512 + h * HD:512 + (h + 1) * HD],
                                         probT[:, h, c * CHUNK:(c + 1) * CHUNK], vals[:, g * HD:(g + 1) * HD],
                                         start=True, stop=True)
                last.then_inc(s["swa_o"], 1)
                pe.wait_ge(s["g_qb"], after(t))
                pe.wait_ge(s_mg[NL], after(t))
                pe.wait_ge(s["st_new"], after(t - 1))
                pe.wait_ge(s["e_v"], after(t))
                for h in range(GH):
                    pair, par = h // 2, h % 2
                    rows = slice(par * DK, (par + 1) * DK)
                    pe.matmul(gla_out[par][:, pair * DV:(pair + 1) * DV], qb[rows, pair * P:(pair + 1) * P],
                              state[rows, pair, :], start=True, stop=False)
                    last = pe.matmul(gla_out[par][:, pair * DV:(pair + 1) * DV], pT[:, par, pair, :],
                                     z_v[:, h * DV:(h + 1) * DV], start=False, stop=True)
                last.then_inc(s["gla_o"], 1)
                pe.wait_ge(s["ev_kd"], after(t))
                for h in range(GH):
                    pair, par = h // 2, h % 2
                    last = pe.matmul(sc[par * DK:(par + 1) * DK, pair * DV:(pair + 1) * DV],
                                     kdN[:, h * DK:(h + 1) * DK], z_v[:, h * DV:(h + 1) * DV], start=True, stop=True)
                last.then_inc(s["gla_up"], 1)
                if more:
                    project(t + 1, "r")
                pe.wait_ge(s["o_mix"], after(t))
                pe.wait_ge(s["swa_mix"], after(t))
                pe.wait_ge(s["ev_kd"], after(t))
                for b in range(KD):
                    last = pe.transpose(tr[:, b * P:(b + 1) * P], mix[:, b * P:(b + 1) * P], ident[:])
                last.then_inc(s["mixT_done"], 1)

            pe.wait_ge(s_const, 16 * 8)
            turn_x(0)
            for i, g in enumerate(GROUPS):
                pe.wait_ge(s["w_split_lo"], (i + 1) * KD)
                project(0, g)
            turn_x(1)
            with pe.Fori(0, NT - 2) as t:
                attend(t, True)
                turn_x(t + 2)
            attend(NT - 2, True)
            attend(NT - 1, False)

        @block.scalar
        def _(act):
            prime(act, "act")

            def norm_x(n):
                act.wait_ge(s["x_rstd"], after(n))
                act.activation(x[:], x[:], ACT.Copy, scale=rstd[:, 0:1]).then_inc(s["x_norm"], 1)

            def split_h(n):
                act.wait_ge(s["xT"], after(n))
                act.wait_ge(s_g["r"], after(n - 1))
                for i, (k0, k1) in enumerate(H_PARTS):
                    act.activation(h_hi[:, k0:k1].rearrange("p k n -> p (k n)"), ob[:, k0 * P:k1 * P], ACT.Copy
                                   ).then_inc(s[f"hT_hi{i}"], 1)

            def evac(n, g):
                act.wait_ge(s_g[g], after(n))
                bank = pj[GROUPS.index(g) % 2]
                if g == "qk":
                    act.wait_ge(s["zT"], after(n - 1))
                    act.activation(z_qk[:], bank[:], ACT.Copy).then_inc(s["e_qk"], 1)
                elif g == "sq":
                    act.wait_ge(s["zT"], after(n - 1))
                    act.activation(z_sqk[:, 0:GRP].rearrange("p b g d -> p g b d"),
                                   bank[:].rearrange("p (g b d) -> p g b d", g=KVH, b=GRP), ACT.Copy
                                   ).then_inc(s["e_sq"], 1)
                elif g == "small":
                    act.wait_ge(s["sT_low"], after(n - 1))
                    act.wait_ge(s["zT"], after(n - 1))
                    act.activation(z_low[:], bank[:, 0:RANK], ACT.Copy).then_inc(s["e_small_low"], 1)
                    act.activation(z_sqk[:, GRP].rearrange("p g d -> p (g d)"), bank[:, RANK:RANK + SKV], ACT.Copy
                                   ).then_inc(s["e_small_k"], 1)
                    act.wait_ge(s["v_copy"], after(n - 1))
                    act.activation(z_sv[:], bank[:, RANK + SKV:RANK + 2 * SKV], ACT.Copy).then_inc(s["e_sv"], 1)
                elif g == "v":
                    act.wait_ge(s["gla_up"], after(n - 1))
                    act.activation(z_v[:], bank[:], ACT.Copy).then_inc(s["e_v"], 1)
                else:
                    act.wait_ge(s["o_mix"], after(n - 1))
                    act.activation(z_r[:], bank[:], ACT.Copy)
                    act.activation(gate[:], bank[:], ACT.Exp, scale=-1.0).then_inc(s["r_exp"], 1)

            for dst, src in ((ident[:], t_in["c_ident"]), (rope_room[:, 0:(NL - 1) * P], t_in["c_masks"]),
                             (swa_mask[:], t_in["c_swa_mask"]), (invf[:], t_in["c_inv_freq"]),
                             (w2[:], t_in["gla_gk_w2"][0]),
                             (gkb[:], t_in["gla_gk_b"][0].rearrange("(k p) -> p k", p=P)),
                             (sinks[:], t_in["swa_sinks"][0].partition_broadcast(P)),
                             (pos_i[:], t_in["positions"][0].rearrange("(t p) -> p t", p=P))):
                act.dma_start(dst, src, allow_slow_non_contiguous=True).then_inc(s_const, 16)
            act.wait_ge(s["norm1_load"], 16)
            for n, (g, k) in enumerate(pieces):
                act.wait_ge(s_w[n % NSTAGE], loaded(n))
                act.activation(w_hi[:, k, FIRST[g]:FIRST[g] + WIDTH[g]], stage[n % NSTAGE][:, 0:WIDTH[g]], ACT.Copy,
                               scale=norm1[:, k:k + 1]).then_inc(s["w_split_hi"], 1)
                if n == KD // 2 - 1:
                    norm_x(0)
                if n == KD - 1:
                    split_h(0)
                if k == KD - 1 and n >= 2 * KD:
                    evac(0, GROUPS[n // KD - 2])
            act.wait_ge(s["rope_tab"], 1)
            act.activation(sinT[:], sinT[:], ACT.Sin)
            act.activation(cosT[:], cosT[:], ACT.Sin).then_inc(s["rope_act"], 1)
            for g in GROUPS[-2:]:
                evac(0, g)
            norm_x(1)
            split_h(1)

            def attend(t, more, norm_next):
                act.wait_ge(s["swa_s"], after(t - 1))
                act.activation(kwin[:, 0:CHUNK], kwin[:, P:P + CHUNK], ACT.Copy).then_inc(s["ev_kshift"], 1)
                act.wait_ge(s["sT_low"], after(t))
                act.wait_ge(s["gk"], after(t - 1))
                act.activation(lowT[:], sc[0:RANK, 512:512 + P], ACT.Copy).then_inc(s["ev_low"], 1)
                act.wait_ge(s["ev_kshift"], after(t))
                act.activation(kwin[:, CHUNK:CHUNK + P], sc[:, 0:P], ACT.Copy).then_inc(s["ev_k"], 1)
                act.wait_ge(s["zT"], after(t))
                act.activation(qkT[:].rearrange("p b n -> p (b n)"), tr[:, 0:512], ACT.Copy).then_inc(s["ev_qkT"], 1)
                act.wait_ge(s["swa_o"], after(t - 1))
                act.activation(v_mid[0:CHUNK, :], v_cur[CHUNK:P, :], ACT.Copy).then_inc(s["vmid_lo"], 1)
                act.wait_ge(s["vmid_lo"], after(t))
                act.wait_ge(s["e_sv"], after(t))
                act.activation(v_cur[:], z_sv[:], ACT.Copy).then_inc(s["v_copy"], 1)
                act.activation(v_mid[CHUNK:P, :], z_sv[0:CHUNK, :], ACT.Copy).then_inc(s["vmid_hi"], 1)
                act.wait_ge(s["g_pre"], after(t))
                act.activation(gate_l[:], gate_a[:], ACT.Abs).then_inc(s["g_abs"], 1)
                act.wait_ge(s["g_abs"], after(t))
                act.activation(gate_l[:], gate_l[:], ACT.Exp, scale=-1.0).then_inc(s["g_exp"], 1)
                act.wait_ge(s["g_exp"], after(t))
                act.activation(gate_l[:], gate_l[:], ACT.Ln, bias=1.0).then_inc(s["g_log"], 1)
                act.wait_ge(s["g_scan"], after(t))
                act.activation(Eb[:], B[:], ACT.Exp, scale=1.0 / GATE_NORM).then_inc(s["g_eb"], 1)
                act.wait_ge(s["g_kdiff"], after(t))
                act.activation(kd[:], kd[:], ACT.Exp, scale=-1.0 / GATE_NORM).then_inc(s["g_kexp"], 1)
                for i, (l0, l1) in enumerate(SPAN_PARTS):
                    act.wait_ge(s[f"lv_diff{i}"], after(t))
                    if i == 1:
                        if more:
                            evac(t + 1, "qk")
                        act.wait_ge(s["swa_s"], after(t))
                    act.activation(qs[:, l0:l1], ks[:, l0:l1], ACT.Exp, scale=-1.0 / GATE_NORM
                                   ).then_inc(s[f"lv_exp{i}"], 1)
                act.wait_ge(s["swa_neg"], after(t))
                for h in range(SH):
                    last = act.activation(prob[:, h, :], prob[:, h, :], ACT.Exp, bias=negm[:, h:h + 1],
                                          scale=HD ** -0.5, accum_out=den[:, h:h + 1])
                last.then_inc(s["swa_exp"], 1)
                act.wait_ge(s["swa_sinkd"], after(t))
                act.activation(esink[:], esink[:], ACT.Exp).then_inc(s["swa_sinke"], 1)
                if more:
                    evac(t + 1, "sq")
                    evac(t + 1, "small")
                act.wait_ge(s["swa_pT"], after(t))
                act.wait_ge(s_out, after(t - 1) * 16)
                act.activation(probT[:].rearrange("p h n -> p (h n)"), tr[:], ACT.Copy).then_inc(s["ev_pT"], 1)
                if not more:
                    act.wait_ge(s_onorm, 16)
                    for k in range(KD):
                        act.wait_ge(s_wo[k], 16)
                        scale = ffn["onorm"][:, 0:1] if k < GV // P else 1.0
                        act.activation(ffn["wo"][k][:, 0, :], ffn["wo_raw"][k], ACT.Copy, scale=scale
                                       ).then_inc(s_wo_hi, 1)
                act.wait_ge(s["kdT"], after(t))
                act.wait_ge(s["gla_up"], after(t - 1))
                act.activation(kdN[:], tr[:, 0:2 * P], ACT.Copy).then_inc(s["ev_kd"], 1)
                if norm_next:
                    norm_x(t + 2)
                act.wait_ge(s["gla_o"], after(t))
                for h in range(GH):
                    last = act.activation(squares[:, h], gla_out[h % 2][:, (h // 2) * DV:(h // 2 + 1) * DV],
                                          ACT.Square, scale=DK ** -0.5, accum_out=ossq[:, h:h + 1])
                last.then_inc(s["o_ssq"], 1)
                if more:
                    evac(t + 1, "v")
                    evac(t + 1, "r")
                act.wait_ge(s["mixT_done"], after(t))
                act.activation(mixT[:].rearrange("p h n -> p (h n)"), tr[:], ACT.Copy).then_inc(s["ev_mixT"], 1)

            with act.Fori(0, NT - 2) as t:
                attend(t, True, True)
                split_h(t + 2)
            attend(NT - 2, True, False)
            attend(NT - 1, False, False)

        @block.gpsimd
        def _(pool):
            prime(pool, "pool")

            pool.memset(nhalf[:], -0.5).then_inc(s["pool_setup"], 1)
            pool.wait_ge(s["pool_setup"], 1)

            def x_rstd(n):
                pool.wait_ge(s["x_eps"], after(n))
                pool.tensor_tensor(rstd[:], ms[:], nhalf[:, 0:1], ALU.pow).then_inc(s["x_rstd"], 1)

            def attend(t):
                pool.wait_ge(s["o_eps"], after(t))
                pool.tensor_tensor(orstd[:], ossq[:], nhalf[:], ALU.pow).then_inc(s["o_rstd"], 1)

            x_rstd(0)
            x_rstd(1)
            with pool.Fori(0, NT - 2) as t:
                x_rstd(t + 2)
                attend(t)
            attend(NT - 2)
            attend(NT - 1)

        @block.vector
        def _(dve):
            prime(dve, "dve")

            steps = [0]

            def then(ins):
                steps[0] += 1
                ins.then_inc(s["dve_setup"], 1)
                dve.wait_ge(s["dve_setup"], steps[0])

            def norm_x(n, part):
                if part == 0:
                    dve.wait_ge(s_x, after(n) * 16)
                    dve.bn_stats(stats[:, 0, :], x[:, 0:512])
                    return
                if part == 1:
                    dve.bn_stats(stats[:, 1, :], x[:, 512:1024]).then_inc(s["x_stats"], 1)
                    return
                plain(dve)
                dve.wait_ge(s["x_stats"], after(n))
                dve.bn_aggr(mv[:], stats[:].rearrange("p a b -> p (a b)")).then_inc(s["x_ms"], 1)
                dve.wait_ge(s["x_ms"], after(n))
                dve.scalar_tensor_tensor(out=ms[:], in0=mv[:, 0:1], scalar=mv[:, 0:1], in1=mv[:, 1:2],
                                         op0=ALU.mult, op1=ALU.add).then_inc(s["x_sum"], 1)
                dve.wait_ge(s["x_sum"], after(n))
                dve.tensor_scalar(ms[:], ms[:], EPS, None, ALU.add).then_inc(s["x_eps"], 1)

            def split_h(n):
                for i, (k0, k1) in enumerate(H_PARTS):
                    dve.wait_ge(s[f"hT_hi{i}"], after(n))
                    dve.tensor_tensor(h_lo[:, k0:k1].rearrange("p k n -> p (k n)"), ob[:, k0 * P:k1 * P],
                                      h_hi[:, k0:k1].rearrange("p k n -> p (k n)").bitcast(F32), ALU.subtract
                                      ).then_inc(s[f"hT_lo{i}"], 1)

            def rope(n):
                heads = z_sqk[:].rearrange("p b g d -> p (b g) d")[:, :, 0:ROPE]
                halves = heads.rearrange("p h (a r) -> p h a r", a=2)
                nh = (GRP + 1) * KVH
                dve.wait_ge(s["e_sq"], after(n))
                dve.wait_ge(s["e_small_k"], after(n))
                ra = ropeA.rearrange("p h (a r) -> p h a r", a=2)
                rb = ropeB.rearrange("p h (a r) -> p h a r", a=2)
                for a in range(2):
                    c = cosT[:, bass.ds(n, 1), :].to_broadcast([P, nh, RH])
                    sn = sinT[:, bass.ds(n, 1), :].to_broadcast([P, nh, RH])
                    dve.tensor_tensor(ra[:, :, a, :], halves[:, :, a, :], c, ALU.mult)
                    last = dve.tensor_tensor(rb[:, :, a, :], halves[:, :, a, :], sn, ALU.mult)
                last.then_inc(s["rope_mul"], 1)
                dve.wait_ge(s["rope_mul"], after(n))
                dve.tensor_tensor(halves[:, :, 0, :], ra[:, :, 0, :], rb[:, :, 1, :], ALU.subtract
                                  ).then_inc(s["rope_a"], 1)
                dve.tensor_tensor(halves[:, :, 1, :], ra[:, :, 1, :], rb[:, :, 0, :], ALU.add
                                  ).then_inc(s["rope_b"], 1)

            def split_w_out(k):
                dve.wait_ge(s_wo_hi, k + 1)
                hi, lo = ffn["wo"][k][:, 0, :].bitcast(F32), ffn["wo"][k][:, 1, :]
                if k < GV // P:
                    dve.scalar_tensor_tensor(out=lo, in0=ffn["wo_raw"][k], scalar=ffn["onorm"][:, 0:1], in1=hi,
                                             op0=ALU.mult, op1=ALU.subtract).then_inc(s_wo_lo, 1)
                else:
                    dve.tensor_tensor(lo, ffn["wo_raw"][k], hi, ALU.subtract).then_inc(s_wo_lo, 1)

            def sigmoid_r(n, part):
                if part == 0:
                    dve.wait_ge(s["r_exp"], after(n))
                    dve.tensor_scalar(gate[:], gate[:], 1.0, None, ALU.add).then_inc(s["r_one"], 1)
                dve.wait_ge(s["r_one"], after(n))
                half = slice(part * (GV // 2), (part + 1) * (GV // 2))
                dve.reciprocal(gate[:, half], gate[:, half]).then_inc(s[f"r_rec{part}"], 1)

            def gate_r(n):
                for part in range(2):
                    dve.wait_ge(s[f"r_rec{part}"], after(n))
                dve.tensor_tensor(gate[:], gate[:], z_r[:], ALU.mult).then_inc(s["r_gate"], 1)

            dve.memset(state[:], 0.0)
            dve.memset(pT[:], 0.0)
            dve.memset(kwin[:], 0.0)
            dve.memset(v_cur[:], 0.0)
            dve.memset(v_mid[:], 0.0)
            dve.wait_ge(s["norm1_load"], 16)
            for n, (g, k) in enumerate(pieces):
                dve.wait_ge(s["w_split_hi"], n + 1)
                cols = slice(FIRST[g], FIRST[g] + WIDTH[g])
                dve.scalar_tensor_tensor(out=w_lo[:, k, cols], in0=stage[n % NSTAGE][:, 0:WIDTH[g]],
                                         scalar=norm1[:, k:k + 1], in1=w_hi[:, k, cols].bitcast(F32),
                                         op0=ALU.mult, op1=ALU.subtract).then_inc(s["w_split_lo"], 1)
                if n == 1:
                    for part in range(3):
                        norm_x(0, part)
                if n == KD - 1:
                    split_h(0)
            dve.wait_ge(s_const, 16 * 8)
            then(dve.tensor_scalar(nsinks[:], sinks[:], -1.0, None, ALU.mult))
            then(dve.tensor_copy(masks[:].rearrange("p l n -> p (l n)"), rope_room[:, 0:(NL - 1) * P]))
            then(dve.tensor_copy(pos_f[:], pos_i[:]))
            then(dve.tensor_tensor(ang, pos_f[:].unsqueeze(2).to_broadcast([P, NT, RH]),
                                   invf[:].unsqueeze(1).to_broadcast([P, NT, RH]), ALU.mult))
            then(dve.tensor_scalar(cosT[:], ang, 1.0 / TWO_PI, ROUNDER, ALU.mult, ALU.add))
            then(dve.tensor_scalar(cosT[:], cosT[:], -ROUNDER, None, ALU.add))
            for part in (TP_A, TP_B, TP_C):
                then(dve.scalar_tensor_tensor(out=ang, in0=cosT[:], scalar=-part, in1=ang,
                                              op0=ALU.mult, op1=ALU.add))
            then(dve.tensor_scalar(sinT[:], ang, PI_IN, -PI_IN, ALU.min, ALU.max))
            then(dve.tensor_scalar(ang, ang, TWO_PI / 4, None, ALU.add))
            then(dve.tensor_scalar(cosT[:], ang, TWO_PI / 2, -TWO_PI, ALU.is_gt, ALU.mult))
            then(dve.tensor_tensor(cosT[:], cosT[:], ang, ALU.add))
            dve.tensor_scalar(cosT[:], cosT[:], PI_IN, -PI_IN, ALU.min, ALU.max).then_inc(s["rope_tab"], 1)
            for part in range(3):
                norm_x(1, part)
            dve.wait_ge(s["rope_act"], 1)
            rope(0)
            split_h(1)

            def attend(t, more, norm_next):
                dve.wait_ge(s["zT"], after(t))
                dve.tensor_copy(sqT.rearrange("p b n -> p (b n)"), tr[:, 512:1024]).then_inc(s["ev_sqT"], 1)
                dve.wait_ge(s["gk"], after(t))
                dve.tensor_scalar(gate_a[:, 0:P], gk_ps[:, 0:P], gkb[:, 0:1], None, ALU.add)
                dve.tensor_scalar(gate_a[:, P:2 * P], gk_ps[:, P:2 * P], gkb[:, 1:2], None, ALU.add
                                  ).then_inc(s["g_pre"], 1)
                dve.wait_ge(s["g_pre"], after(t))
                dve.wait_ge(s["o_ssq"], after(t - 1))
                dve.tensor_scalar(gate_m[:], gate_a[:], 0.0, None, ALU.min).then_inc(s["g_min"], 1)
                sigmoid_r(t, 0)
                dve.wait_ge(s["g_log"], after(t))
                dve.wait_ge(s["g_min"], after(t))
                dve.tensor_tensor(gate_m[:], gate_m[:], gate_l[:], ALU.subtract).then_inc(s["g_sum"], 1)
                dve.wait_ge(s["g_sum"], after(t))
                for pair in range(2):
                    cols = slice(pair * P, (pair + 1) * P)
                    last = dve.tensor_tensor_scan(B[:, cols], gate_m[:, cols], gate_m[:, cols], 0.0,
                                                  ALU.add, ALU.bypass)
                last.then_inc(s["g_scan"], 1)
                dve.wait_ge(s["g_scan"], after(t))
                dve.wait_ge(s["kdT"], after(t - 1))
                for pair in range(2):
                    cols = slice(pair * P, (pair + 1) * P)
                    last = dve.tensor_scalar(kd[:, cols], B[:, cols], B[:, (pair + 1) * P - 1:(pair + 1) * P],
                                             None, ALU.subtract)
                last.then_inc(s["g_kdiff"], 1)
                dve.wait_ge(s_lv[NL - 1], after(t - 1))
                for i, (l0, l1) in enumerate(SPAN_PARTS):
                    for l in range(l0, l1):
                        span = SPANS[l]
                        b4 = B[:].rearrange("p (n a w) -> p n a w", a=2, w=span)
                        d4 = ks[:, l, :].rearrange("p (n a w) -> p n a w", a=2, w=span)
                        ref = b4[:, :, 0, span - 1:span].to_broadcast([P, P // span, span])
                        dve.tensor_tensor(d4[:, :, 0, :], b4[:, :, 0, :], ref, ALU.subtract)
                        last = dve.tensor_tensor(d4[:, :, 1, :], ref, b4[:, :, 1, :], ALU.subtract)
                    last.then_inc(s[f"lv_diff{i}"], 1)
                dve.wait_ge(s["ev_qkT"], after(t))

                def level_operands(i):
                    l0, l1 = SPAN_PARTS[i]
                    dve.wait_ge(s[f"lv_exp{i}"], after(t))
                    dve.tensor_tensor(ks[:, l0:l1], qkT[:, 2:4, :].rearrange("p b n -> p (b n)").unsqueeze(1)
                                      .to_broadcast([P, l1 - l0, 2 * P]), qs[:, l0:l1], ALU.mult
                                      ).then_inc(s[f"lv_k{i}"], 1)
                    dve.wait_ge(s[f"lv_k{i}"], after(t))
                    dve.tensor_tensor(qs[:, l0:l1], qkT[:, 0:2, :].rearrange("p b n -> p (b n)").unsqueeze(1)
                                      .to_broadcast([P, l1 - l0, 2 * P]), qs[:, l0:l1], ALU.mult
                                      ).then_inc(s[f"lv_qk{i}"], 1)

                dve.wait_ge(s["swa_s"], after(t))
                dve.wait_ge(s["mixT_done"], after(t - 1))
                dve.tensor_tensor(prob[:], sc[:].rearrange("p (h k) -> p h k", h=SH),
                                  swa_mask[:].unsqueeze(1).to_broadcast([P, SH, P]), ALU.add
                                  ).then_inc(s["swa_masked"], 1)
                dve.wait_ge(s["swa_masked"], after(t))
                dve.memset(swa_mask[:], 0.0)
                dve.tensor_reduce(negm[:], prob[:], AX_X, ALU.max).then_inc(s["swa_max"], 1)
                dve.wait_ge(s["swa_max"], after(t))
                dve.scalar_tensor_tensor(out=negm[:], in0=negm[:], scalar=-(HD ** -0.5), in1=nsinks[:],
                                         op0=ALU.mult, op1=ALU.min).then_inc(s["swa_neg"], 1)
                dve.wait_ge(s["swa_neg"], after(t))
                dve.tensor_tensor(esink[:], sinks[:], negm[:], ALU.add).then_inc(s["swa_sinkd"], 1)
                level_operands(0)
                level_operands(1)
                dve.wait_ge(s["g_eb"], after(t))
                dve.wait_ge(s["gla_o"], after(t - 1))
                dve.tensor_tensor(qb[:], qkT[:, 0:2, :].rearrange("p b n -> p (b n)"), Eb[:], ALU.mult
                                  ).then_inc(s["g_qb"], 1)
                dve.wait_ge(s["g_kexp"], after(t))
                dve.tensor_tensor(kd[:], qkT[:, 2:4, :].rearrange("p b n -> p (b n)"), kd[:], ALU.mult
                                  ).then_inc(s["g_kd"], 1)
                dve.wait_ge(s["swa_exp"], after(t))
                dve.wait_ge(s["swa_sinke"], after(t))
                dve.tensor_tensor(den[:], den[:], esink[:], ALU.add).then_inc(s["swa_den"], 1)
                dve.wait_ge(s["swa_den"], after(t))
                dve.reciprocal(rden[:], den[:]).then_inc(s["swa_rden"], 1)
                sigmoid_r(t, 1)
                dve.wait_ge(s["gla_o"], after(t - 1))
                for l in range(NL + 1):
                    bank = ob if l % 2 == 0 else sc
                    got = bank[:].rearrange("p (a c) -> p a c", a=2)[:, :, 0:2 * P].rearrange(
                        "p a (b n) -> p a b n", b=2)
                    plain(dve)
                    dve.wait_ge(s_lv[l], after(t))
                    if l < 2:
                        w = SPANS[l]
                        for b0 in range(0, P, 2 * w):
                            last = dve.tensor_copy(pT[b0:b0 + w, :, :, b0 + w:b0 + 2 * w],
                                                   got[b0:b0 + w, :, :, b0 + w:b0 + 2 * w])
                    else:
                        m = masks[:, l - 2, :].unsqueeze(1).unsqueeze(1).to_broadcast([P, 2, 2, P])
                        if l >= 2:
                            dve.wait_ge(s_mg[l - 1], after(t))
                        last = dve.copy_predicated(pT[:], m, got)
                    last.then_inc(s_mg[l], 1)
                    if not more:
                        split_w_out(l)
                    if norm_next and l in (2, 4, 6):
                        norm_x(t + 2, l // 2 - 1)
                gate_r(t)
                dve.wait_ge(s["swa_o"], after(t))
                dve.wait_ge(s["swa_rden"], after(t))
                dve.tensor_tensor(mix[:, GV:DMIX].rearrange("p (h d) -> p h d", h=SH),
                                  ob[:, 512:1024].rearrange("p (h d) -> p h d", h=SH),
                                  rden[:].unsqueeze(2).to_broadcast([P, SH, HD]), ALU.mult
                                  ).then_inc(s["swa_mix"], 1)
                if more:
                    rope(t + 1)
                dve.wait_ge(s["gla_o"], after(t))
                for pair in range(2):
                    last = dve.tensor_scalar(state[:, pair, :], state[:, pair, :],
                                             Eb[:, (pair + 1) * P - 1:(pair + 1) * P], None, ALU.mult)
                last.then_inc(s["st_scaled"], 1)
                dve.wait_ge(s["o_ssq"], after(t))
                dve.tensor_scalar(ossq[:], ossq[:], 1.0 / DV, EPS, ALU.mult, ALU.add).then_inc(s["o_eps"], 1)
                dve.wait_ge(s["gla_up"], after(t))
                dve.wait_ge(s["st_scaled"], after(t))
                dve.tensor_tensor(state[:].rearrange("p a v -> p (a v)"), state[:].rearrange("p a v -> p (a v)"),
                                  sc[:, 0:2 * DV], ALU.add).then_inc(s["st_new"], 1)
                dve.wait_ge(s["o_rstd"], after(t))
                for par in range(2):
                    last = dve.scalar_tensor_tensor(
                        out=mix[:, 0:GV].rearrange("p (a b v) -> p b a v", a=2, b=2)[:, par],
                        in0=gla_out[par].rearrange("p (a v) -> p a v", a=2), scalar=DK ** -0.5,
                        in1=orstd[:].rearrange("p (a b) -> p b a", b=2)[:, par].unsqueeze(2)
                        .to_broadcast([P, 2, DV]), op0=ALU.mult, op1=ALU.mult)
                last.then_inc(s["o_scaled"], 1)
                dve.wait_ge(s["o_scaled"], after(t))
                dve.wait_ge(s["r_gate"], after(t))
                dve.tensor_tensor(mix[:, 0:GV], mix[:, 0:GV], gate[:], ALU.mult).then_inc(s["o_mix"], 1)

            with dve.Fori(0, NT - 2) as t:
                attend(t, True, True)
                split_h(t + 2)
            attend(NT - 2, True, False)
            attend(NT - 1, False, False)
    nc.clear_and_free_semaphores(all_sems)
    nc.all_engine_barrier()


def ffn_memory(nc, ctx):
    def sb(name, shape, dt=F32, where=ctx):
        return where.enter_context(nc.sbuf_tensor(name, shape, dt))

    m = {}
    wo_first = sb("w_out_first", [P, KD // 2, 2, D], F32R)
    m["ident"] = sb("ident_b", [P, P])
    m["onorm"] = sb("gla_norm_col", [P, 1])
    m["norm2"] = sb("norm2_col", [P, KD])
    m["fnorm"] = sb("final_norm_row", [P, D])
    m["cw"] = sb("conv_w_cols", [P, 3, 2 * NC_FF])
    m["cb"] = sb("conv_b_cols", [P, 2 * NC_FF])
    m["carry"] = sb("conv_carry", [P, 2 * NC_FF, 2])
    m["nhalf"] = sb("minus_half_b", [P, 1])
    m["ms"] = sb("mean_square_b", [P, 1])
    m["rstd"] = sb("rstd_b", [P, 1])
    m["f_ms"] = sb("mean_square_last", [P, 2])
    m["f_rstd"] = sb("rstd_last", [P, 2])
    m["normed"] = sb("normed", [P, D])
    m["fin"] = [sb("final0", [P, D]), sb("final1", [P, D])]
    spare = m["spare"] = sb("w_out_raw", [P, D])
    with ExitStack() as projection:
        wo_last = sb("w_out_last", [P, KD // 2, 2, D], F32R, projection)
        m["mixt"] = sb("mix_tile", [P, KD, P], F32, projection)
        m["xt"] = sb("x_res", [P, D], F32, projection)
        m["mix_hi"] = [sb(f"mix_hi{u}", [P, KD, P], F32R, projection) for u in range(2)]
        m["mix_lo"] = [sb(f"mix_lo{u}", [P, KD, P], F32R, projection) for u in range(2)]
    for name in ("conv_g", "conv_u", "gated", "wd_raw"):
        m[name] = sb(name, [P, TOK])[:]
    for name in ("wd_hi", "wd_lo", "g_hi", "g_lo"):
        m[name] = sb(name, [P, TOK], F32R)[:]
    for name in ("wg_raw", "wu_raw"):
        m[name] = sb(name, [P, KD, P])
    for name in ("wg_hi", "wg_lo", "wu_hi", "wu_lo"):
        m[name] = sb(name, [P, KD, P], F32R)
    y = m["y"] = sb("y", [P, TPH, D])
    m["g2_hi"] = sb("h2_hi", [P, KD, TOK], F32R)
    m["g2_lo"] = sb("h2_lo", [P, KD, TOK], F32R)
    m["wo"] = [wo_first[:, k] for k in range(KD // 2)] + [wo_last[:, k] for k in range(KD // 2)]
    m["wo_raw"] = [y[:, k, :] for k in range(4)] + [m["normed"][:], m["fin"][0][:], m["fin"][1][:], spare[:]]
    return m


def ffn_phase(nc, t_in, mix_scratch, out, mem):
    with ExitStack() as ctx:
        def ps(name, cols):
            return ctx.enter_context(nc.psum_tensor(name, [P, cols], F32))

        def sem(name):
            return ctx.enter_context(nc.semaphore(name))

        wo, wo_raw, ident, norm2, fnorm = mem["wo"], mem["wo_raw"], mem["ident"], mem["norm2"], mem["fnorm"]
        cw, cb, carry, nhalf = mem["cw"], mem["cb"], mem["carry"], mem["nhalf"]
        ms, rstd, f_ms, f_rstd = mem["ms"], mem["rstd"], mem["f_ms"], mem["f_rstd"]
        f_squares = mem["spare"]
        normed, fin, y, g2_hi, g2_lo = mem["normed"], mem["fin"], mem["y"], mem["g2_hi"], mem["g2_lo"]
        mixt, xt, mix_hi, mix_lo = mem["mixt"], mem["xt"], mem["mix_hi"], mem["mix_lo"]
        conv_g, conv_u, gated = mem["conv_g"], mem["conv_u"], mem["gated"]
        wd_raw, wd_hi, wd_lo, g_hi, g_lo = mem["wd_raw"], mem["wd_hi"], mem["wd_lo"], mem["g_hi"], mem["g_lo"]
        wg_raw, wg_hi, wg_lo = mem["wg_raw"], mem["wg_hi"], mem["wg_lo"]
        wu_raw, wu_hi, wu_lo = mem["wu_raw"], mem["wu_hi"], mem["wu_lo"]

        gate_ps = ps("gate_ps", TOK)
        up_ps = ps("up_ps", TOK)
        acc_ps = [ps("acc_ps0", D), ps("acc_ps1", D)]

        owned = {
            "pe": "o_mm o_turned f_gate f_up",
            "act": """o_mix_hi o_sq o_normed o_split_hi f_wg_hi f_wu_hi f_wd_hi f_gate_tap f_up_tap f_silu f_g_hi
                n_sq""",
            "pool": "o_rstd n_rstd",
            "dve": """o_mix_lo o_added o_eps o_split_lo f_wg_lo f_wu_lo f_wd_lo
                f_gate_tap1 f_gate_tap2 f_gate_edge f_gate_conv f_up_tap1 f_up_tap2 f_up_edge f_up_conv
                f_prod f_g_lo n_eps n_out""",
        }
        s = {n: sem("b_" + n) for names in owned.values() for n in names.split()}
        stepped = {who: [s[n] for n in names.split()] for who, names in owned.items()}
        s_dn = [sem(f"b_down{q}") for q in range(TPH)]
        stepped["pe"] += s_dn
        s_ad = [sem(f"b_added{q}") for q in range(TPH)]
        stepped["dve"] += s_ad
        s_setup, s_pool = sem("b_setup"), sem("b_pool_setup")
        again = range(KD // 2, KD)
        s_wo, s_wo_hi, s_wo_lo = [sem(f"b_w_out_load{k}") for k in again], sem("b_w_out_hi"), sem("b_w_out_lo")
        s_mix, s_x = sem("b_mix_load"), sem("b_x_load")
        s_wg, s_wu, s_wd = sem("b_wg_load"), sem("b_wu_load"), sem("b_wd_load")
        s_out = [sem("b_out_store0"), sem("b_out_store1")]

        block = ctx.enter_context(nc.Block())

        LAST = NC_FF - 1

        def slice_of(hf, c):
            return hf * NC_FF + c

        def tile_of(q):
            return y[:, bass.ds(q, 1), :].rearrange("p o d -> p (o d)")

        def prime(eng, who):
            for one in stepped[who]:
                eng.sem_inc(one, PRIME)

        def plain(eng, value):
            if not isinstance(value, int):
                eng.lower_val(value)
            eng.wait_ge(s_setup, 1)

        def loaded(n):
            return 16 * (n + PRIME)

        @block.sync
        def _(sp):
            for u in range(2):
                sp.sem_inc(s_out[u], 16 * PRIME)
            sp.sem_inc(s_mix, 16 * PRIME)
            sp.sem_inc(s_x, 16 * PRIME)

            def load_mix(n):
                sp.wait_ge(s["o_mix_lo"], after(n - 1))
                sp.dma_start(mixt[:], mix_scratch[bass.ds(n, 1)].rearrange("o p k n -> (o p) k n")).then_inc(s_mix, 16)

            def load_x(n):
                sp.wait_ge(s["o_added"], after(n - 1))
                sp.dma_start(xt[:], t_in["x"][0, bass.ds(n * P, P), :]).then_inc(s_x, 16)

            def store(n, u):
                sp.wait_ge(s["n_out"], after(n))
                sp.dma_start(out[0, bass.ds(n * P, P), :], fin[u][:]).then_inc(s_out[u], 16)

            def load_gate(m, c):
                sp.wait_ge(s["f_wg_lo"], after(m - 1))
                sp.dma_start(wg_raw[:], t_in["w_up"][0].rearrange("(k p) f -> p k f", p=P)[:, :, bass.ds(c * P, P)]
                             ).then_inc(s_wg, 16)

            def load_up(m, c):
                sp.wait_ge(s["f_wu_lo"], after(m - 1))
                sp.dma_start(wu_raw[:], t_in["w_up"][0].rearrange("(k p) f -> p k f", p=P)
                             [:, :, bass.ds(c * P + FF, P)]).then_inc(s_wu, 16)

            def load_down(m, c):
                sp.wait_ge(s["f_wd_lo"], after(m - 1))
                sp.dma_start(wd_raw, t_in["w_down"][0, bass.ds(c * P, P), :]).then_inc(s_wd, 16)

            for hf in range(HALVES):
                n0 = hf * TPH
                if hf > 0:
                    sp.wait_ge(s["f_wg_lo"], after(slice_of(hf - 1, LAST)))
                    load_mix(n0)
                    sp.wait_ge(s["f_wu_lo"], after(slice_of(hf - 1, LAST)))
                    load_x(n0)
                load_mix(n0 + 1)
                old = n0 - TPH
                with sp.Fori(0, TPH // 2 - 1) as i:
                    for u in range(2):
                        load_mix(n0 + i * 2 + (2 + u))
                        if hf > 0:
                            store(old + i * 2 + u, u)
                        load_x(n0 + i * 2 + (1 + u))
                if hf > 0:
                    store(n0 - 2, 0)
                load_x(n0 + TPH - 1)
                sp.wait_ge(s["o_mix_lo"], after(n0 + TPH - 1))
                load_gate(slice_of(hf, 0), 0)
                if hf > 0:
                    store(n0 - 1, 1)
                sp.wait_ge(s["o_added"], after(n0 + TPH - 1))
                load_up(slice_of(hf, 0), 0)
                sp.wait_ge(s["o_mm"], after(n0 + TPH - 1))
                load_down(slice_of(hf, 0), 0)
                with sp.Fori(1, NC_FF) as c:
                    m = slice_of(hf, c)
                    load_gate(m, c)
                    load_up(m, c)
                    load_down(m, c)
                if hf + 1 < HALVES:
                    for i, k in enumerate(again):
                        sp.dma_start(wo_raw[k], t_in["w_out"][0, k * P:(k + 1) * P, :]).then_inc(s_wo[i], 16)
            with sp.Fori(0, TPH // 2) as i:
                for u in range(2):
                    store(NT - TPH + i * 2 + u, u)
            for u in range(2):
                sp.wait_ge(s_out[u], 16 * after(NT // 2 - 1))

        @block.tensor
        def _(pe):
            prime(pe, "pe")

            def gemm(out_ap, lhs, rhs, first, last):
                pe.matmul(out_ap, lhs[0], rhs[0], start=first, stop=False)
                pe.matmul(out_ap, lhs[0], rhs[1], start=False, stop=False)
                return pe.matmul(out_ap, lhs[1], rhs[0], start=False, stop=last)

            def project_out(n, u, reloaded=False):
                pe.wait_ge(s["o_mix_lo"], after(n))
                pe.wait_ge(s["o_added"], after(n - 2))
                for c0 in range(0, D, 512):
                    for k in range(KD):
                        if reloaded and c0 == 0 and k in again:
                            pe.wait_ge(s_wo_lo, k - again[0] + 1)
                        last = gemm(acc_ps[u][:, c0:c0 + 512], (mix_hi[u][:, k, :], mix_lo[u][:, k, :]),
                                    (wo[k][:, 0, c0:c0 + 512], wo[k][:, 1, c0:c0 + 512]), k == 0, k == KD - 1)
                last.then_inc(s["o_mm"], 1)

            def turn(n):
                pe.wait_ge(s["o_normed"], after(n))
                pe.wait_ge(s["o_split_lo"], after(n - 1))
                for k in range(KD):
                    last = pe.transpose(up_ps[:, k * P:(k + 1) * P], normed[:, k * P:(k + 1) * P], ident[:])
                last.then_inc(s["o_turned"], 1)

            def raise_(bank, hi, lo, t0, blocks=range(KD)):
                for k in blocks:
                    last = gemm(bank[:, t0:t0 + 512], (hi[:, k, :], lo[:, k, :]),
                                (g2_hi[:, k, t0:t0 + 512], g2_lo[:, k, t0:t0 + 512]), k == 0, k == KD - 1)
                return last

            def lower(m, tiles):
                pe.wait_ge(s["f_g_lo"], after(m))
                pe.wait_ge(s["f_wd_lo"], after(m))
                for q in tiles:
                    if q >= 2:
                        pe.wait_ge(s_ad[q - 2], after(m))
                    else:
                        pe.wait_ge(s_ad[TPH - 2 + q], after(m - 1))
                    cols = slice(q * P, (q + 1) * P)
                    for c0 in range(0, D, 512):
                        last = gemm(acc_ps[q % 2][:, c0:c0 + 512], (g_hi[:, cols], g_lo[:, cols]),
                                    (wd_hi[:, c0:c0 + 512], wd_lo[:, c0:c0 + 512]), True, True)
                    last.then_inc(s_dn[q], 1)

            def gate_part(m, last_tile=None):
                pe.wait_ge(s["f_wg_lo"], after(m))
                pe.wait_ge(s["f_gate_conv"], after(m - 1))
                raise_(gate_ps, wg_hi, wg_lo, 0)
                if last_tile is not None:
                    pe.wait_ge(s["o_split_lo"], after(last_tile))
                raise_(gate_ps, wg_hi, wg_lo, 512).then_inc(s["f_gate"], 1)

            def up_part(m, lowered=None):
                pe.wait_ge(s["f_wu_lo"], after(m))
                pe.wait_ge(s["f_up_conv"], after(m - 1))
                raise_(up_ps, wu_hi, wu_lo, 0)
                if lowered is not None:
                    lower(lowered, (2, 3))
                raise_(up_ps, wu_hi, wu_lo, 512, range(KD // 2))
                if lowered is not None:
                    lower(lowered, (4, 5))
                raise_(up_ps, wu_hi, wu_lo, 512, range(KD // 2, KD)).then_inc(s["f_up"], 1)

            pe.wait_ge(s_setup, 1)
            for hf in range(HALVES):
                n0, m0 = hf * TPH, slice_of(hf, 0)
                if hf > 0:
                    pe.wait_ge(s_ad[TPH - 1], after(m0 - 1))
                project_out(n0, 0, reloaded=hf > 0)
                with pe.Fori(0, TPH // 2 - 1) as i:
                    project_out(n0 + i * 2 + 1, 1)
                    turn(n0 + i * 2)
                    project_out(n0 + i * 2 + 2, 0)
                    turn(n0 + i * 2 + 1)
                project_out(n0 + TPH - 1, 1)
                turn(n0 + TPH - 2)
                turn(n0 + TPH - 1)
                gate_part(m0, last_tile=n0 + TPH - 1)
                up_part(m0)
                with pe.Fori(0, LAST) as c:
                    m = m0 + c
                    gate_part(m + 1)
                    lower(m, (0, 1))
                    up_part(m + 1, lowered=m)
                    lower(m, (6, 7))
                lower(slice_of(hf, LAST), range(TPH))

        @block.scalar
        def _(act):
            prime(act, "act")
            act.wait_ge(s_setup, 1)

            def split_w(m, raw, hi, loaded, free, done):
                act.wait_ge(loaded, (m + 1) * 16)
                act.wait_ge(free, after(m - 1))
                for k in range(KD):
                    last = act.activation(hi[:, k, :], raw[:, k, :], ACT.Copy, scale=norm2[:, k:k + 1])
                last.then_inc(done, 1)

            def last_tap(m, bank, conv, col, ready, free, done):
                plain(act, after(m))
                act.wait_ge(ready, after(m))
                act.wait_ge(free, after(m - 1))
                act.activation(conv, bank[:], ACT.Copy, scale=cw[:, 2, bass.ds(col, 1)]).then_inc(done, 1)

            def gated_part(m, c):
                last_tap(m, up_ps, conv_u, c + NC_FF, s["f_up"], s["f_prod"], s["f_up_tap"])
                plain(act, after(m))
                act.wait_ge(s["f_gate_conv"], after(m))
                act.activation(conv_g, conv_g, ACT.Silu, bias=cb[:, bass.ds(c, 1)]).then_inc(s["f_silu"], 1)
                act.wait_ge(s_wd, (m + 1) * 16)
                act.wait_ge(s_dn[TPH - 1], after(m - 1))
                act.activation(wd_hi, wd_raw, ACT.Copy).then_inc(s["f_wd_hi"], 1)
                act.wait_ge(s["f_prod"], after(m))
                act.activation(g_hi, gated, ACT.Copy).then_inc(s["f_g_hi"], 1)

            def mix_high(n, u):
                act.wait_ge(s_mix, loaded(n))
                act.wait_ge(s["o_mm"], after(n - 2))
                act.activation(mix_hi[u][:], mixt[:], ACT.Copy).then_inc(s["o_mix_hi"], 1)

            def square(n, q):
                plain(act, after(n))
                act.wait_ge(s["o_added"], after(n))
                act.wait_ge(s["o_turned"], after(n - 1))
                act.activation(normed[:], tile_of(q), ACT.Square, accum_out=ms[:, 0:1]).then_inc(s["o_sq"], 1)

            def normalise(n, q):
                plain(act, after(n))
                act.wait_ge(s["o_rstd"], after(n))
                act.activation(normed[:], tile_of(q), ACT.Copy, scale=rstd[:, 0:1]).then_inc(s["o_normed"], 1)

            def turned_high(n, q):
                plain(act, after(n))
                act.wait_ge(s["o_turned"], after(n))
                act.activation(g2_hi[:, :, bass.ds(q * P, P)], up_ps[:].rearrange("p (k n) -> p k n", k=KD),
                               ACT.Copy).then_inc(s["o_split_hi"], 1)

            def last_square(n, q, u):
                plain(act, after(n - 2))
                act.wait_ge(s["n_rstd"], after(n - 2))
                act.wait_ge(s["n_sq"], after(n - 1))
                act.activation(f_squares[:], tile_of(q), ACT.Square, accum_out=f_ms[:, u:u + 1]).then_inc(s["n_sq"], 1)

            for hf in range(HALVES):
                n0, m0, old = hf * TPH, slice_of(hf, 0), (hf - 1) * TPH
                if hf > 0:
                    act.wait_ge(s["f_gate"], after(m0 - 1))
                mix_high(n0, 0)
                if hf > 0:
                    for k in again[:2]:
                        act.wait_ge(s_wo[k - again[0]], 16)
                        act.wait_ge(s["f_g_lo"], after(m0 - 1))
                        act.activation(wo[k][:, 0, :], wo_raw[k], ACT.Copy).then_inc(s_wo_hi, 1)
                mix_high(n0 + 1, 1)
                if hf > 0:
                    for k in again[2:]:
                        act.wait_ge(s_wo[k - again[0]], 16)
                        act.wait_ge(s_dn[TPH - 1], after(m0 - 1))
                        act.activation(wo[k][:, 0, :], wo_raw[k], ACT.Copy).then_inc(s_wo_hi, 1)
                    act.wait_ge(s_wo_lo, len(again))
                    act.wait_ge(s_ad[TPH - 1], after(m0 - 1))
                    last_square(old, 0, 0)
                with act.Fori(0, TPH // 2 - 1) as i:
                    for u in range(2):
                        q = i * 2 + u
                        square(n0 + q, q)
                        if hf > 0:
                            last_square(old + q + 1, q + 1, 1 - u)
                        normalise(n0 + q, q)
                        mix_high(n0 + q + 2, u)
                        turned_high(n0 + q, q)
                q, n = TPH - 1, n0 + TPH - 1
                square(n - 1, q - 1)
                if hf > 0:
                    last_square(old + q, q, q % 2)
                normalise(n - 1, q - 1)
                square(n, q)
                turned_high(n - 1, q - 1)
                act.wait_ge(s["o_mm"], after(n))
                split_w(m0, wg_raw, wg_hi, s_wg, s["f_gate"], s["f_wg_hi"])
                normalise(n, q)
                turned_high(n, q)
                split_w(m0, wu_raw, wu_hi, s_wu, s["f_up"], s["f_wu_hi"])
                with act.Fori(0, NC_FF - 1) as c:
                    m = m0 + c
                    last_tap(m, gate_ps, conv_g, c, s["f_gate"], s["f_prod"], s["f_gate_tap"])
                    split_w(m + 1, wg_raw, wg_hi, s_wg, s["f_gate"], s["f_wg_hi"])
                    gated_part(m, c)
                    split_w(m + 1, wu_raw, wu_hi, s_wu, s["f_up"], s["f_wu_hi"])
                m = slice_of(hf, LAST)
                last_tap(m, gate_ps, conv_g, LAST, s["f_gate"], s["f_prod"], s["f_gate_tap"])
                gated_part(m, LAST)
            for q in range(TPH):
                n = NT - TPH + q
                act.wait_ge(s_ad[q], after(slice_of(HALVES - 1, LAST)))
                last_square(n, q, q % 2)

        @block.gpsimd
        def _(pool):
            prime(pool, "pool")
            pool.memset(nhalf[:], -0.5).then_inc(s_pool, 1)
            pool.wait_ge(s_pool, 1)

            def root(n):
                pool.wait_ge(s["o_eps"], after(n))
                pool.tensor_tensor(rstd[:], ms[:], nhalf[:], ALU.pow).then_inc(s["o_rstd"], 1)

            def last_root(n, u):
                pool.wait_ge(s["n_eps"], after(n))
                pool.wait_ge(s["n_out"], after(n - 2))
                pool.tensor_tensor(f_rstd[:, u:u + 1], f_ms[:, u:u + 1], nhalf[:], ALU.pow).then_inc(s["n_rstd"], 1)

            with pool.Fori(0, TPH) as q:
                root(q)
            for hf in range(1, HALVES):
                n0, old = hf * TPH, (hf - 1) * TPH
                for k in again:
                    pool.wait_ge(s_wo_hi, k - again[0] + 1)
                    pool.tensor_tensor(wo[k][:, 1, :], wo_raw[k], wo[k][:, 0, :].bitcast(F32), ALU.subtract
                                       ).then_inc(s_wo_lo, 1)
                last_root(old, 0)
                with pool.Fori(0, TPH // 2 - 1) as i:
                    for u in range(2):
                        root(n0 + i * 2 + u)
                        last_root(old + i * 2 + (1 + u), 1 - u)
                root(n0 + TPH - 2)
                last_root(old + TPH - 1, 1)
                root(n0 + TPH - 1)
            with pool.Fori(0, TPH // 2) as i:
                for u in range(2):
                    last_root(NT - TPH + i * 2 + u, u)

        @block.vector
        def _(dve):
            prime(dve, "dve")
            dve.memset(carry[:], 0.0).then_inc(s_setup, 1)
            dve.wait_ge(s_setup, 1)

            def split_w(m, raw, hi, lo, done_hi, done):
                dve.wait_ge(done_hi, after(m))
                for k in range(KD):
                    last = dve.scalar_tensor_tensor(out=lo[:, k, :], in0=raw[:, k, :], scalar=norm2[:, k:k + 1],
                                                    in1=hi[:, k, :].bitcast(F32), op0=ALU.mult, op1=ALU.subtract)
                last.then_inc(done, 1)

            def add_down(m, tiles):
                for q in tiles:
                    dve.wait_ge(s_dn[q], after(m))
                    dve.tensor_tensor(y[:, q, :], y[:, q, :], acc_ps[q % 2][:], ALU.add).then_inc(s_ad[q], 1)

            def conv(m, bank, acc, col, pre):
                tap0, tap1 = cw[:, 0, bass.ds(col, 1)], cw[:, 1, bass.ds(col, 1)]
                old = carry[:, bass.ds(col, 1), :].rearrange("p o a -> p (o a)")
                dve.wait_ge(s[pre + "tap"], after(m))
                dve.scalar_tensor_tensor(out=acc[:, 1:TOK], in0=bank[:, 0:TOK - 1], scalar=tap1,
                                         in1=acc[:, 1:TOK], op0=ALU.mult, op1=ALU.add).then_inc(s[pre + "tap1"], 1)
                dve.wait_ge(s[pre + "tap1"], after(m))
                dve.scalar_tensor_tensor(out=acc[:, 2:TOK], in0=bank[:, 0:TOK - 2], scalar=tap0,
                                         in1=acc[:, 2:TOK], op0=ALU.mult, op1=ALU.add)
                dve.scalar_tensor_tensor(out=acc[:, 0:1], in0=old[:, 1:2], scalar=tap1, in1=acc[:, 0:1],
                                         op0=ALU.mult, op1=ALU.add).then_inc(s[pre + "tap2"], 1)
                dve.wait_ge(s[pre + "tap2"], after(m))
                dve.scalar_tensor_tensor(out=acc[:, 0:2], in0=old, scalar=tap0, in1=acc[:, 0:2],
                                         op0=ALU.mult, op1=ALU.add).then_inc(s[pre + "edge"], 1)
                plain(dve, after(m))
                dve.wait_ge(s[pre + "edge"], after(m))
                dve.tensor_copy(old, bank[:, TOK - 2:TOK]).then_inc(s[pre + "conv"], 1)

            def conv_gate(m, c):
                conv(m, gate_ps, conv_g, c, "f_gate_")

            def conv_up(m, c):
                conv(m, up_ps, conv_u, c + NC_FF, "f_up_")

            def gated_part(m, c):
                dve.wait_ge(s["f_silu"], after(m))
                dve.wait_ge(s["f_up_conv"], after(m))
                dve.wait_ge(s["f_g_lo"], after(m - 1))
                dve.scalar_tensor_tensor(out=gated, in0=conv_u, scalar=cb[:, bass.ds(c + NC_FF, 1)], in1=conv_g,
                                         op0=ALU.add, op1=ALU.mult).then_inc(s["f_prod"], 1)
                dve.wait_ge(s["f_wd_hi"], after(m))
                dve.tensor_tensor(wd_lo, wd_raw, wd_hi.bitcast(F32), ALU.subtract).then_inc(s["f_wd_lo"], 1)
                dve.wait_ge(s["f_g_hi"], after(m))
                dve.tensor_tensor(g_lo, gated, g_hi.bitcast(F32), ALU.subtract).then_inc(s["f_g_lo"], 1)

            def mix_low(n, u):
                dve.wait_ge(s["o_mix_hi"], after(n))
                dve.tensor_tensor(mix_lo[u][:], mixt[:], mix_hi[u][:].bitcast(F32), ALU.subtract
                                  ).then_inc(s["o_mix_lo"], 1)

            def add_residual(n, q, u, old=None):
                if old is not None:
                    dve.wait_ge(s["n_out"], after(old))
                dve.wait_ge(s["o_mm"], after(n))
                dve.wait_ge(s_x, loaded(n))
                dve.tensor_tensor(tile_of(q), acc_ps[u][:], xt[:], ALU.add).then_inc(s["o_added"], 1)

            def mean(n):
                dve.wait_ge(s["o_sq"], after(n))
                dve.tensor_scalar(ms[:], ms[:], 1.0 / D, EPS, ALU.mult, ALU.add).then_inc(s["o_eps"], 1)

            def last_mean(n, u):
                dve.wait_ge(s["n_sq"], after(n))
                dve.tensor_scalar(f_ms[:, u:u + 1], f_ms[:, u:u + 1], 1.0 / D, EPS, ALU.mult, ALU.add
                                  ).then_inc(s["n_eps"], 1)

            def turned_low(n, q):
                dve.wait_ge(s["o_split_hi"], after(n))
                dve.tensor_tensor(g2_lo[:, :, bass.ds(q * P, P)], up_ps[:].rearrange("p (k n) -> p k n", k=KD),
                                  g2_hi[:, :, bass.ds(q * P, P)].bitcast(F32), ALU.subtract
                                  ).then_inc(s["o_split_lo"], 1)

            def last_norm(n, q, u, stored):
                dve.wait_ge(s["n_rstd"], after(n))
                dve.wait_ge(s_out[u], 16 * (stored + PRIME))
                dve.scalar_tensor_tensor(out=fin[u][:], in0=tile_of(q), scalar=f_rstd[:, u:u + 1], in1=fnorm[:],
                                         op0=ALU.mult, op1=ALU.mult).then_inc(s["n_out"], 1)

            for hf in range(HALVES):
                n0, m0, old = hf * TPH, slice_of(hf, 0), (hf - 1) * TPH
                if hf > 0:
                    dve.wait_ge(s["f_up"], after(m0 - 1))
                mix_low(n0, 0)
                if hf > 0:
                    add_down(m0 - 1, range(TPH))
                mix_low(n0 + 1, 1)
                if hf > 0:
                    last_mean(old, 0)
                    dve.wait_ge(s_wo_lo, len(again))
                with dve.Fori(0, TPH // 2 - 1) as i:
                    for u in range(2):
                        q = i * 2 + u
                        if hf > 0:
                            last_norm(old + q, q, u, i + old // 2)
                        add_residual(n0 + q, q, u, old + q if hf > 0 else None)
                        mean(n0 + q)
                        if hf > 0:
                            last_mean(old + q + 1, 1 - u)
                        mix_low(n0 + q + 2, u)
                        turned_low(n0 + q, q)
                q, n = TPH - 1, n0 + TPH - 1
                if hf > 0:
                    last_norm(old + q - 1, q - 1, (q - 1) % 2, (old + q - 1) // 2)
                add_residual(n - 1, q - 1, (q - 1) % 2, old + q - 1 if hf > 0 else None)
                mean(n - 1)
                if hf > 0:
                    last_mean(old + q, q % 2)
                    last_norm(old + q, q, q % 2, (old + q) // 2)
                add_residual(n, q, q % 2, old + q if hf > 0 else None)
                turned_low(n - 1, q - 1)
                mean(n)
                split_w(m0, wg_raw, wg_hi, wg_lo, s["f_wg_hi"], s["f_wg_lo"])
                turned_low(n, q)
                split_w(m0, wu_raw, wu_hi, wu_lo, s["f_wu_hi"], s["f_wu_lo"])

                def slice_step(m, c, first=False, last=False):
                    if not first:
                        add_down(m - 1, (0, 1))
                    conv_gate(m, c)
                    if not first:
                        add_down(m - 1, (2, 3))
                    if not last:
                        split_w(m + 1, wg_raw, wg_hi, wg_lo, s["f_wg_hi"], s["f_wg_lo"])
                    if not first:
                        add_down(m - 1, (4, 5))
                    conv_up(m, c)
                    if not first:
                        add_down(m - 1, (6, 7))
                    gated_part(m, c)
                    if not last:
                        split_w(m + 1, wu_raw, wu_hi, wu_lo, s["f_wu_hi"], s["f_wu_lo"])

                slice_step(m0, 0, first=True)
                with dve.Fori(1, LAST) as c:
                    slice_step(m0 + c, c)
                slice_step(slice_of(hf, LAST), LAST, last=True)
            m = slice_of(HALVES - 1, LAST)
            for q in range(TPH + 2):
                if q < TPH:
                    add_down(m, [q])
                if 1 <= q <= TPH:
                    last_mean(NT - TPH + q - 1, (q - 1) % 2)
                if q >= 2:
                    last_norm(NT - TPH + q - 2, q - 2, q % 2, (NT - TPH + q - 2) // 2)


def program(nc, t_in, out):
    mix_scratch = nc.dram_tensor("mix_scratch", (NT, P, KD, P), F32).ap()
    with ExitStack() as ctx:
        mem = ffn_memory(nc, ctx)
    mixer_phase(nc, t_in, mix_scratch, mem)
    ffn_phase(nc, t_in, mix_scratch, out, mem)


_INS = ['x', 'positions', 'norm1_w', 'w_in', 'gla_gk_w2', 'gla_gk_b', 'gla_norm_w', 'swa_sinks', 'w_out',
        'norm2_w', 'w_up', 'conv_w', 'conv_b', 'w_down', 'final_norm_w']


def _constants():
    j, i = np.meshgrid(np.arange(P), np.arange(P), indexing="ij")
    masks = [((j // (2 * w) == i // (2 * w)) & (j % (2 * w) < w) & (i % (2 * w) >= w)) for w in SPANS[2:]]
    masks.append(i == j)
    swa = np.zeros((P, P), np.float32)
    swa[0:CHUNK, 0:CHUNK] = NEG
    inv = np.float32(THETA) ** (-np.arange(RH, dtype=np.float32) / np.float32(RH))
    return {"c_ident": np.eye(P, dtype=np.float32),
            "c_masks": np.ascontiguousarray(np.stack(masks, 1).astype(np.float32).reshape(P, -1)),
            "c_swa_mask": swa,
            "c_inv_freq": np.ascontiguousarray(np.broadcast_to(inv.astype(np.float32), (P, RH)))}


def kernel(**inputs):
    import concourse.bacc as _bacc
    from concourse.bass_utils import run_bass_kernel_spmd as _run

    nc = _bacc.Bacc("TRN2", target_bir_lowering=False, num_devices=1)
    arrays, t_in = {}, {}
    for name, a in [(n, np.ascontiguousarray(inputs[n])) for n in _INS] + list(_constants().items()):
        arrays[f"in_{name}"] = a
        t_in[name] = nc.dram_tensor(f"in_{name}", a.shape, mybir.dt.from_np(a.dtype), kind="ExternalInput").ap()
    out = nc.dram_tensor("out_dram", (1, S, D), F32, kind="ExternalOutput").ap()
    program(nc, t_in, out)
    r = _run(nc, [arrays], core_ids=[0])
    return r.results[0]["out_dram"]
```
